# Optimizing a Trainium2 kernel written in Bass

```python
import jax, jax.numpy as jnp
from jax import lax
import numpy as np

D_MODEL = 1024
BATCH = 1
SEQ = 128
DEPTH = 1
DEC_BATCH = 1
DEC_SEQ = 512
PAST_LEN = 128

GRID_W = 64
EPS = 1e-6
FOURIER_GROUPS = 8
FOURIER_GROUP_DIM = 128
FOURIER_DIM = FOURIER_GROUPS * FOURIER_GROUP_DIM
D_INNER = 2 * D_MODEL
HEAD_DIM = 64
N_HEADS = D_INNER // HEAD_DIM
N_GROUPS = 4
HEADS_PER_GROUP = N_HEADS // N_GROUPS
D_STATE = 128
GN = N_GROUPS * D_STATE
CONV_DIM = D_INNER + 2 * GN
CONV_W = 5
CHUNK = 128
COL_Z = FOURIER_DIM
COL_XBC = COL_Z + D_INNER
COL_DT = COL_XBC + CONV_DIM
COL_GATE = COL_DT + 2 * N_HEADS
D_IN_PROJ = COL_GATE + 2 * D_MODEL
PEER_HEADS = 8
N_KEYS = 128
N_EXPERTS = N_KEYS * N_KEYS
D_KEY = 256
HALF_KEY = D_KEY // 2
TOPK = 16
TOKEN_BLOCK = 128

kernel_name = 'hybrid_fnet_ssd_peer_diffusion_step'

def _rmsnorm(x, w):
    xf = x.astype(jnp.float32)
    y = xf * lax.rsqrt(jnp.mean(xf * xf, axis=-1, keepdims=True) + EPS)
    return (y * w.astype(jnp.float32)).astype(x.dtype)

def _grid_posemb(rows, dtype):
    r = jnp.repeat(jnp.arange(rows, dtype=jnp.float32), GRID_W)
    col = jnp.tile(jnp.arange(GRID_W, dtype=jnp.float32), rows)
    quarter = D_MODEL // 4
    omega = 1.0 / (10000.0 ** (jnp.arange(quarter, dtype=jnp.float32) / quarter))
    ar = r[:, None] * omega
    ac = col[:, None] * omega
    return jnp.concatenate([jnp.sin(ar), jnp.cos(ar), jnp.sin(ac), jnp.cos(ac)], axis=-1).astype(dtype)

def _fourier_mix(u):
    b, L, _ = u.shape
    ug = u.astype(jnp.float32).reshape(b, L, FOURIER_GROUPS, FOURIER_GROUP_DIM)
    f = jnp.fft.fft2(ug, axes=(1, 3), norm='ortho').real
    return f.reshape(b, L, FOURIER_DIM).astype(u.dtype)

def _centred_dwconv(u, w, bias):
    pad = CONV_W // 2
    L = u.shape[1]
    up = jnp.pad(u, ((0, 0), (pad, pad), (0, 0)))
    out = bias
    for k in range(CONV_W):
        out = out + up[:, k:k + L] * w[k]
    return out

def _ssd_scan(x, dt_raw, Bm, Cm, a_log, dt_bias, d_skip, h0):
    f32 = jnp.float32
    b, L = x.shape[:2]
    nc = L // CHUNK
    dt = jax.nn.softplus(dt_raw.astype(f32) + dt_bias.astype(f32))
    dA = dt * (-jnp.exp(a_log.astype(f32)))
    xf = x.astype(f32)
    xc = (xf * dt[..., None]).reshape(b, nc, CHUNK, N_GROUPS, HEADS_PER_GROUP, HEAD_DIM)
    dAc = dA.reshape(b, nc, CHUNK, N_GROUPS, HEADS_PER_GROUP)
    Bc = Bm.astype(f32).reshape(b, nc, CHUNK, N_GROUPS, D_STATE)
    Cc = Cm.astype(f32).reshape(b, nc, CHUNK, N_GROUPS, D_STATE)
    cs = jnp.cumsum(dAc, axis=2)
    lower = jnp.tril(jnp.ones((CHUNK, CHUNK), dtype=bool))[:, :, None, None]
    seg = cs[:, :, :, None] - cs[:, :, None, :]
    decay_in = jnp.exp(jnp.where(lower, seg, -jnp.inf))
    cb = jnp.einsum('bclgn,bcsgn->bclsg', Cc, Bc)
    y_diag = jnp.einsum('bclsg,bclsgr,bcsgrp->bclgrp', cb, decay_in, xc)
    decay_to_end = jnp.exp(cs[:, :, -1:] - cs)
    chunk_states = jnp.einsum('bctgn,bctgr,bctgrp->bcgrpn', Bc, decay_to_end, xc)
    chunk_decay = jnp.exp(cs[:, :, -1])

    def carry_state(h, inp):
        st, dec = inp
        return h * dec[..., None, None] + st, h

    h_init = h0.astype(f32).reshape(b, N_GROUPS, HEADS_PER_GROUP, HEAD_DIM, D_STATE)
    h_last, h_enter = lax.scan(carry_state, h_init,
                               (jnp.moveaxis(chunk_states, 1, 0), jnp.moveaxis(chunk_decay, 1, 0)))
    h_enter = jnp.moveaxis(h_enter, 0, 1)
    y_off = jnp.einsum('bctgn,bcgrpn,bctgr->bctgrp', Cc, h_enter, jnp.exp(cs))
    y = (y_diag + y_off).reshape(b, L, N_HEADS, HEAD_DIM) + d_skip.astype(f32)[:, None] * xf
    return y, h_last.reshape(b, N_HEADS, HEAD_DIM, D_STATE)

def _ssd_branch(u_z, u_xbc, u_dt, w_conv, b_conv, a_log, dt_bias, d_skip, w_norm, h0):
    b, L = u_xbc.shape[:2]
    xbc = jax.nn.silu(_centred_dwconv(u_xbc, w_conv, b_conv))
    x = xbc[..., :D_INNER].reshape(b, L, N_HEADS, HEAD_DIM)
    Bm = xbc[..., D_INNER:D_INNER + GN].reshape(b, L, N_GROUPS, D_STATE)
    Cm = xbc[..., D_INNER + GN:].reshape(b, L, N_GROUPS, D_STATE)
    rev = lambda t: jnp.flip(t, axis=1)
    y_f, h_f = _ssd_scan(x, u_dt[..., :N_HEADS], Bm, Cm, a_log[0], dt_bias[0], d_skip[0], h0[:, 0])
    y_b, h_b = _ssd_scan(rev(x), rev(u_dt[..., N_HEADS:]), rev(Bm), rev(Cm),
                         a_log[1], dt_bias[1], d_skip[1], h0[:, 1])
    y = (y_f + rev(y_b)).reshape(b, L, D_INNER)
    y = _rmsnorm(y * jax.nn.silu(u_z.astype(jnp.float32)), w_norm).astype(u_z.dtype)
    return y, jnp.stack([h_f, h_b], axis=1)

def _token_mixer(h, h0, w_in, w_conv, b_conv, a_log, dt_bias, d_skip, ssd_norm, w_fourier, w_ssd_out, w_out):
    b, L, _ = h.shape
    proj = h @ w_in
    a_out = _fourier_mix(proj[..., :FOURIER_DIM]) @ w_fourier
    s_y, h_fin = _ssd_branch(proj[..., COL_Z:COL_XBC], proj[..., COL_XBC:COL_DT], proj[..., COL_DT:COL_GATE],
                             w_conv, b_conv, a_log, dt_bias, d_skip, ssd_norm, h0)
    b_out = s_y @ w_ssd_out
    gates = jax.nn.sigmoid(proj[..., COL_GATE:].astype(jnp.float32)).reshape(b, L, 2, D_MODEL)
    merged = (gates[:, :, 0] * a_out.astype(jnp.float32) + gates[:, :, 1] * b_out.astype(jnp.float32)).astype(h.dtype)
    return merged @ w_out, h_fin

def _peer(h, w_query, sub_keys, expert_u, expert_v):
    shape = h.shape
    blocks = h.reshape(-1, TOKEN_BLOCK, D_MODEL)

    def block_fn(xb):
        t = xb.shape[0]
        q = (xb @ w_query).reshape(t, PEER_HEADS, 2, HALF_KEY)
        s = jnp.einsum('thik,hink->thin', q, sub_keys).astype(jnp.float32)
        v_half, i_half = lax.top_k(s, TOPK)
        cand = (v_half[:, :, 0, :, None] + v_half[:, :, 1, None, :]).reshape(t, PEER_HEADS, TOPK * TOPK)
        cand_idx = (i_half[:, :, 0, :, None] * N_KEYS + i_half[:, :, 1, None, :]).reshape(t, PEER_HEADS, TOPK * TOPK)
        top_v, top_pos = lax.top_k(cand, TOPK)
        idx = jnp.take_along_axis(cand_idx, top_pos, axis=-1)
        g = jax.nn.softmax(top_v, axis=-1)
        u = expert_u[idx]
        act = jax.nn.gelu(jnp.einsum('thkd,td->thk', u, xb).astype(jnp.float32))
        v = expert_v[idx]
        return jnp.einsum('thk,thkd->td', (g * act).astype(xb.dtype), v)

    return lax.map(block_fn, blocks).reshape(shape)

def _layer(x, cond, h0, lw):
    (w_ada, b_ada, n_mix_pre, n_mix_post, n_ffn_pre, n_ffn_post, w_in, w_conv, b_conv, a_log, dt_bias,
     d_skip, ssd_norm, w_fourier, w_ssd_out, w_out, peer_query, peer_sub_keys, peer_u, peer_v) = lw
    m = jax.nn.silu(cond.astype(jnp.float32)) @ w_ada.astype(jnp.float32) + b_ada.astype(jnp.float32)
    m = m.astype(x.dtype)[:, None, :]
    shift1, scale1, gate1, shift2, scale2, gate2 = jnp.split(m, 6, axis=-1)
    h = _rmsnorm(x, n_mix_pre) * (1 + scale1) + shift1
    mix, h_fin = _token_mixer(h, h0, w_in, w_conv, b_conv, a_log, dt_bias, d_skip, ssd_norm,
                              w_fourier, w_ssd_out, w_out)
    x = x + gate1 * _rmsnorm(mix, n_mix_post)
    h = _rmsnorm(x, n_ffn_pre) * (1 + scale2) + shift2
    x = x + gate2 * _rmsnorm(_peer(h, peer_query, peer_sub_keys, peer_u, peer_v), n_ffn_post)
    return x, h_fin

def setup_inputs(seed: int = 0) -> dict:
    key = jax.random.key(seed)
    ks = jax.random.split(key, 32)
    f32 = jnp.float32
    nrm = lambda k, shape, s: jax.random.normal(k, shape, f32) * s
    dt0 = jnp.exp(jax.random.uniform(ks[14], (DEPTH, 2, N_HEADS), f32, np.log(1e-3), np.log(1e-1)))
    return {
        'x_prompt': nrm(ks[0], (BATCH, SEQ, D_MODEL), 1.0),
        'x_sample': nrm(ks[1], (DEC_BATCH, DEC_SEQ, D_MODEL), 1.0),
        'state_ssd': nrm(ks[2], (DEC_BATCH, DEPTH, 2, N_HEADS, HEAD_DIM, D_STATE), 0.1),
        'c': nrm(ks[3], (DEC_BATCH, D_MODEL), 1.0),
        'c_ctx': nrm(ks[4], (D_MODEL,), 1.0),
        'w_ada': nrm(ks[5], (DEPTH, D_MODEL, 6 * D_MODEL), 0.3 * D_MODEL ** -0.5),
        'b_ada': nrm(ks[6], (DEPTH, 6 * D_MODEL), 0.02),
        'norm_mix_pre': 1.0 + nrm(ks[7], (DEPTH, D_MODEL), 0.02),
        'norm_mix_post': 1.0 + nrm(ks[8], (DEPTH, D_MODEL), 0.02),
        'norm_ffn_pre': 1.0 + nrm(ks[9], (DEPTH, D_MODEL), 0.02),
        'norm_ffn_post': 1.0 + nrm(ks[10], (DEPTH, D_MODEL), 0.02),
        'w_in': nrm(ks[11], (DEPTH, D_MODEL, D_IN_PROJ), D_MODEL ** -0.5),
        'w_conv': nrm(ks[12], (DEPTH, CONV_W, CONV_DIM), CONV_W ** -0.5),
        'b_conv': nrm(ks[13], (DEPTH, CONV_DIM), 0.02),
        'a_log': jnp.log(jax.random.uniform(ks[15], (DEPTH, 2, N_HEADS), f32, 1.0, 16.0)),
        'dt_bias': dt0 + jnp.log(-jnp.expm1(-dt0)),
        'd_skip': 1.0 + nrm(ks[16], (DEPTH, 2, N_HEADS), 0.1),
        'ssd_norm': 1.0 + nrm(ks[17], (DEPTH, D_INNER), 0.02),
        'w_fourier': nrm(ks[18], (DEPTH, FOURIER_DIM, D_MODEL), FOURIER_DIM ** -0.5),
        'w_ssd_out': nrm(ks[19], (DEPTH, D_INNER, D_MODEL), D_INNER ** -0.5),
        'w_out': nrm(ks[20], (DEPTH, D_MODEL, D_MODEL), D_MODEL ** -0.5),
        'peer_query': nrm(ks[21], (DEPTH, D_MODEL, PEER_HEADS * D_KEY), D_MODEL ** -0.5),
        'peer_sub_keys': nrm(ks[22], (DEPTH, PEER_HEADS, 2, N_KEYS, HALF_KEY), HALF_KEY ** -0.5),
        'peer_u': nrm(ks[23], (DEPTH, N_EXPERTS, D_MODEL), D_MODEL ** -0.5),
        'peer_v': nrm(ks[24], (DEPTH, N_EXPERTS, D_MODEL), D_MODEL ** -0.5),
    }

def reference(x_prompt, x_sample, state_ssd, c, c_ctx, w_ada, b_ada, norm_mix_pre, norm_mix_post,
              norm_ffn_pre, norm_ffn_post, w_in, w_conv, b_conv, a_log, dt_bias, d_skip, ssd_norm,
              w_fourier, w_ssd_out, w_out, peer_query, peer_sub_keys, peer_u, peer_v):
    rows = x_sample.shape[1] // GRID_W
    ctx = x_prompt
    lat = x_sample + _grid_posemb(rows, x_sample.dtype)[None]
    zero_state = jnp.zeros((x_prompt.shape[0], 2, N_HEADS, HEAD_DIM, D_STATE), jnp.float32)
    ctx_states = []
    for l in range(DEPTH):
        lw = (w_ada[l], b_ada[l], norm_mix_pre[l], norm_mix_post[l], norm_ffn_pre[l], norm_ffn_post[l],
              w_in[l], w_conv[l], b_conv[l], a_log[l], dt_bias[l], d_skip[l], ssd_norm[l],
              w_fourier[l], w_ssd_out[l], w_out[l], peer_query[l], peer_sub_keys[l], peer_u[l], peer_v[l])
        ctx, h_ctx = _layer(ctx, c_ctx[None, :], zero_state, lw)
        ctx_states.append(h_ctx.astype(x_prompt.dtype))
        lat, _ = _layer(lat, c, state_ssd[:, l], lw)
    y_prompt = ctx
    y_sample = lat
    new_state_ssd = jnp.stack(ctx_states, axis=1)
    return (y_prompt, y_sample, new_state_ssd)


_drawn_inputs = setup_inputs


def setup_inputs(seed=0):
    import zlib

    import numpy as np

    out = dict(_drawn_inputs(seed))
    spreads = {}
    factors = {'state_ssd': 3.555,
     'norm_mix_post': 4.766,
     'norm_ffn_post': 8.0,
     'd_skip': 2.868,
     'ssd_norm': 4.597}
    for name, (base, spread) in spreads.items():
        noise = np.random.default_rng([zlib.crc32(name.encode()), seed]).standard_normal(out[name].shape)
        drawn = base * np.exp(spread * noise) if base else spread * noise
        out[name] = __import__('jax').numpy.asarray(drawn.astype(out[name].dtype))
    for name, factor in factors.items():
        out[name] = (out[name] * factor).astype(out[name].dtype)
    return out
```

```python
from contextlib import ExitStack, contextmanager

import numpy as np

import concourse.bass as bass
from concourse import mybir
from concourse.bass import ds

F32 = mybir.dt.float32
BF16 = mybir.dt.bfloat16
U32 = mybir.dt.uint32
I32 = mybir.dt.int32
ACT = mybir.ActivationFunctionType
ALU = mybir.AluOpType
AX = mybir.AxisListType

P = 128
D = 1024
KT = D // P
NT = 5
LAT = (NT - 1) * P
TOK = NT * P
HEADS, HD, NG = 32, 64, 4
HG = HEADS // NG
GC = HG * HD
DI = HEADS * HD
TAPS = 5
COL_Z, COL_X = 1024, 3072
COL_B, COL_C = COL_X + DI, COL_X + DI + NG * P
COL_DT = COL_X + DI + 2 * NG * P
COL_GATE = COL_DT + 2 * HEADS
D_IN = COL_GATE + 2 * D
PH, TOPK, NKEY = 8, 16, 128
EPS = 1e-6
GELU_C, GELU_A = float(np.sqrt(2 / np.pi)), 0.044715
NEG = -1e30
LOWEST = -3.0e38
NSLOT = 8
NS = NT * PH

SH1, SC1, GA1, SH2, SC2, GA2 = range(6)

JOB_ADA, JOB_XBC, JOB_U, JOB_FO, JOB_GA, JOB_Z, JOB_GB, JOB_SO, JOB_WO, JOB_Q = (
    0, 12, 20, 22, 24, 26, 30, 32, 36, 38)
Q_U, Q_FO, Q_GA, Q_Z, Q_GB, Q_SO, Q_WO = 0, 10, 20, 30, 50, 60, 80
T_NORM1, T_XB, T_Y, T_MERGE, T_NORM2 = 0, 10, 38, 58, 68
XB_UNITS = 7
STATES = [(1, 4), (1, 3), (1, 2), (1, 0), (0, 0), (0, 1), (0, 2), (0, 3)]


def loaded(n):
    slot, turn = n % 2, n // 2
    extra = 0
    if slot == 1 and n >= JOB_XBC:
        extra = min((n - JOB_XBC) // 2 + 1, NG)
    return 16 * (turn + 1 + extra)


class Chain:

    def __init__(self, eng, sem):
        self.eng, self.sem, self.n, self.marks = eng, sem, 0, 0

    def __call__(self, ins, wait=None):
        ins.then_inc(self.sem, 1)
        self.n, self.marks = self.n + 1, self.marks + 1
        if wait:
            wait(self.eng, self.sem, self.n)
        else:
            self.eng.wait_ge(self.sem, self.n)

    @contextmanager
    def loop(self, count, steps):
        start, before = self.n, self.marks
        with self.eng.Fori(0, count) as i:
            self.n = i * steps + start
            yield i
            assert self.marks - before == steps, (self.marks - before, steps)
        self.n, self.marks = start + count * steps, before + count * steps


def layer_kernel(nc, a, outs):
    y_out, st_out = outs
    with ExitStack() as ctx:
        def sb(name, shape, dt=F32):
            return ctx.enter_context(nc.sbuf_tensor(name, shape, dt))

        def sem(name):
            return ctx.enter_context(nc.semaphore(name))

        bank = [ctx.enter_context(nc.psum_tensor(f"bank{i}", [P, 512], F32)) for i in range(8)]

        shp = sb("shape_consts", [P, 7, P])
        ident, tri, ones = shp[:, 0, :], [shp[:, 1, :], shp[:, 2, :]], shp[:, 3, :]
        identb = sb("identb", [P, P], BF16)
        maskb = sb("maskb", [P, 2, P], BF16)
        zerob = sb("zerob", [P, P], BF16)
        eps = sb("eps", [P, 1])
        cond = sb("cond_sb", [P, KT, 2])
        adab = sb("adab_sb", [P, 48])
        mod = sb("mod", [P, 48, 2])
        norms = sb("norms_sb", [P, 4, KT])
        scl = sb("scl", [P, 4, KT, 2])
        ssdn = sb("ssdn_sb", [P, 16])
        convw = sb("convw_sb", [P, 24, TAPS])
        convb = sb("convb_sb", [P, 24])
        hrow = sb("hrow", [P, 3, 2 * HEADS])
        dsum = sb("dsum", [P, HEADS])
        wdt = sb("wdt", [P, KT, 2 * HEADS])
        tab = sb("tab", [P, 7, NT, 2 * HEADS])
        dt_, dA, ncs, ecs, ecd, dtd, tmp = (tab[:, i] for i in range(7))
        dAg = sb("dAg", [P, NT, 2, HG])
        stat = sb("stat", [P, 64])

        KB = 256
        arena = sb("arena", [P, 189 * KB])

        def at(kb, n):
            o = int(kb * KB)
            assert o + n <= 189 * KB, (kb, n)
            return arena[:, o:o + n]

        hT = at(0, KT * TOK).rearrange("p (k t) -> p k t", k=KT)
        ring = [at(20 + 16 * s, 16 * KB) for s in range(2)]
        Y = at(52, NT * DI).rearrange("p (t c) -> p t c", t=NT)
        x0 = at(92, NT * D).rearrange("p (t c) -> p t c", t=NT)
        pos0 = at(112, 4 * D).rearrange("p (t c) -> p t c", t=4)
        xs = at(92, 4 * TOK).rearrange("p (i t) -> p i t", i=4)
        xtok = at(102, NT * GC).rearrange("p (t c) -> p t c", t=NT)
        Btok = at(112, TOK).rearrange("p (t c) -> p t c", t=NT)
        BT, CT = at(114.5, TOK), at(117, TOK)
        cin = at(119.5, 2 * 648).rearrange("p (s c) -> p s c", s=2)
        acc = at(124.625, 2 * 648).rearrange("p (s c) -> p s c", s=2)
        xd = at(129.75, 8 * 512).rearrange("p (s c) -> p s c", s=8)
        xc = at(145.75, 4 * 512).rearrange("p (s d c) -> p s d c", s=2, d=2)
        Ee = at(153.75, 2 * 512).rearrange("p (s j l) -> p s j l", s=2, j=4)
        Mm = at(157.75, 4 * 512).rearrange("p (s j l) -> p s j l", s=4, j=4)
        H = at(165.75, 8 * 512).rearrange("p (d s c) -> p d s c", d=2, s=4)
        cbT = at(181.75, TOK).rearrange("p (t c) -> p t c", t=NT)
        xD = at(184.25, 512)
        yt = xs.rearrange("p i t -> p (i t)")[:, 0:512]
        cst = xs.rearrange("p i t -> p (i t)")[:, 512:1536].rearrange("p (d c) -> p d c", d=2)
        Us = at(92, NT * D).rearrange("p (t c) -> p t c", t=NT)
        FT = at(112, KT * TOK).rearrange("p (k t) -> p k t", k=KT)
        Pq = at(132, 4 * TOK).rearrange("p (s d t) -> p s d t", s=2, d=2)
        posm = at(142, 2 * 4 * 512).rearrange("p (s k t) -> p s k t", s=2, k=4)
        a_out = at(158, NT * D).rearrange("p (t c) -> p t c", t=NT)
        gt = at(178, 4 * 512).rearrange("p (s c) -> p s c", s=4)
        chm = at(186.5, 3 * P).rearrange("p (i n) -> p i n", i=3)
        yT = at(92, 16 * TOK).rearrange("p (k t) -> p k t", k=16)
        sB = at(132, NT * D).rearrange("p (t c) -> p t c", t=NT)
        rows = at(52, 8 * D).rearrange("p (v c) -> p v c", v=8)
        mT = at(92, KT * TOK).rearrange("p (k t) -> p k t", k=KT)
        mix = at(152, NT * D).rearrange("p (t c) -> p t c", t=NT)
        x1 = at(129, NT * D).rearrange("p (t c) -> p t c", t=NT)
        pos1 = at(112, 4 * D).rearrange("p (t c) -> p t c", t=4)
        h2 = mT.rearrange("p k t -> p (k t)").rearrange("p (t c) -> p t c", t=NT)
        h2T = hT
        keys = at(84, 16 * P).rearrange("p (i n) -> p i n", i=16)
        qT = at(149, 16 * TOK).rearrange("p (i t) -> p i t", i=16)
        score = at(0, NT * 16 * P).rearrange("p (t n) -> p t n", t=NT)
        vrow = at(40, NSLOT * D).rearrange("p (s c) -> p s c", s=NSLOT)
        urow = at(152, NSLOT * D).rearrange("p (s c) -> p s c", s=NSLOT)
        h2c, pv, h2sq = at(72, D), at(84, D), at(88, D)
        steps = NT * PH * TOPK
        idx_tab = at(112, steps).bitcast(I32)
        d_tab, w_tab = at(114.5, steps), at(117, steps)
        sw, sw2 = (at(119.5 + i, 256).rearrange("p (h n) -> p h n", h=2) for i in range(2))
        cand, cand2 = at(121.5, 256), at(122.5, 256)
        eq = at(123.5, 512).rearrange("p (k n) -> p k n", n=TOPK)
        small = at(125.5, 12 * 32).rearrange("p (i n) -> p i n", i=12)
        v16, pick = small[:, 0], small[:, 1]
        i16, i16f = small[:, 2].bitcast(U32), small[:, 3]
        tv, tp = small[:, 4, 0:TOPK], small[:, 4, TOPK:].bitcast(U32)
        tij, tijf = small[:, 5].bitcast(U32), small[:, 6]
        dots, ge, ex = small[:, 7, 0:TOPK], small[:, 7, TOPK:], small[:, 8, 0:TOPK]
        esum, erec = small[:, 9, 0:1], small[:, 9, 1:2]
        pstat = small[:, 10, 0:4]
        idx_u = [small[:, 11, 16 * i:16 * i + 16].bitcast(I32) for i in range(2)]
        iota16 = shp[:, 6, 0:TOPK]
        idx_v = [at(127 + i / 16, TOPK).bitcast(I32) for i in range(2)]
        diag = at(186, 4 * P).rearrange("p (s n) -> p s n", s=4)

        S = {}

        def s(name):
            if name not in S:
                S[name] = sem(name)
            return S[name]

        NAMES = ("consts_in x_in pos_in w_free tm_full tm_free tr_full tr_free cond_ready ada_done coef_ready "
                 "identb_ready x_ready ssq1 var1 std1 xn_ready wdt_in dt_full nega v_ready softp dA_ready cs_full "
                 "tmc_ready exps_ready tabs_ready ch_full ch_free conv_done silu_done cb_full cb_done h0_in "
                 "xd_ready st_full st_free cst_out dAg_ready e_full e_done m_done xc_ready yo_full y_full "
                 "y_free xD_ready d1_full d1_act d1_dve d2_full d2_free chm_in posm_in gt_used "
                 "ssqy vary stdy rstdy mg_done row_full row_free x1_in varm stdm ssqm x1_done ssqn varn stdn h2_ready "
                 "keys_in q_done sc_full sc_free topk_done h2c ge_done w_done diag_done u_used v_used pv_full pv_done pstd out_ready out_done idx_cp dve act waited")
        for nm in NAMES.split():
            s(nm)
        w_in = [sem("w_slot0_in"), sem("w_slot1_in")]
        u_in = [sem(f"u_slot{i}_in") for i in range(NSLOT)]
        v_in = [sem(f"v_slot{i}_in") for i in range(NSLOT)]

        block = ctx.enter_context(nc.Block())

        win = a["w_in"].rearrange("(k p) n -> p k n", p=P)
        CONSTS = ["shp", "cond", "ada_b", "norms", "ssd_norm", "conv_w", "conv_b", "a_log", "dt_bias", "d_skip"]

        def wait_alone(eng, semaphore, value):
            eng.wait_ge(semaphore, value)
            if not isinstance(value, int):
                eng.sem_inc(s("waited"), 1)


        @block.sync
        def _(sp):
            for nm in ("cst_out", "out_done"):
                sp.nop().then_inc(s(nm), 16)
            for dst, name in ((shp, "shp"), (cond, "cond"), (adab, "ada_b"), (norms, "norms"), (ssdn, "ssd_norm"),
                              (convw, "conv_w"), (convb, "conv_b")):
                sp.dma_start(dst[:], a[name]).then_inc(s("consts_in"), 16)
            for i, name in enumerate(("a_log", "dt_bias", "d_skip")):
                sp.dma_start(hrow[:, i, :], a[name].partition_broadcast(P)).then_inc(s("consts_in"), 16)

            def load(n, src, cols, first=False, k=KT, off=0):
                if not first:
                    wait_alone(sp, s("w_free"), n - 1)
                dst = ring[n % 2 if isinstance(n, int) else load.slot]
                dst = dst.rearrange("p (k c) -> p k c", k=k)[:, :, off:off + cols]
                sp.dma_start(dst, src).then_inc(w_in[n % 2 if isinstance(n, int) else load.slot], 16)

            wada = a["w_ada"].rearrange("(k p) n -> p k n", p=P)
            load(0, wada[:, :, 0:512], 512, True)
            load(1, wada[:, :, 512:1024], 512, True)
            sp.dma_start(x0[:, 0, :], a["x"][0:P, :]).then_inc(s("x_in"), 16)
            sp.dma_start(x0[:, 1:, :], a["x"][P:, :].rearrange("(t p) c -> p t c", p=P)).then_inc(s("x_in"), 16)
            sp.dma_start(pos0, a["pos"].rearrange("(t p) c -> p t c", p=P)).then_inc(s("pos_in"), 16)
            sp.dma_start(wdt[:], win[:, :, COL_DT:COL_DT + 64]).then_inc(s("wdt_in"), 16)
            sp.dma_start(chm, a["chm"]).then_inc(s("chm_in"), 16)
            with sp.Fori(1, 6) as i:
                for load.slot in range(2):
                    load(i * 2 + load.slot, wada[:, :, ds(i * 1024 + 512 * load.slot, 512)], 512)
            with sp.Fori(0, NG) as g:
                load.slot = 0
                load(g * 2 + JOB_XBC, win[:, :, ds(g * GC + COL_X, GC)], GC)
                load.slot = 1
                load(g * 2 + JOB_XBC + 1, win[:, :, ds(g * P + COL_B, P)], P)
                load(g * 2 + JOB_XBC + 1, win[:, :, ds(g * P + COL_C, P)], P, True, off=P)
                wait_alone(sp, s("y_full"), g * 10 + 1)
                wait_alone(sp, s("tr_free"), g * XB_UNITS + T_XB)
                sp.dma_start(H[:, 0, 0, :], a["state"][0, :, ds(g * GC, GC)]).then_inc(s("h0_in"), 16)
                sp.dma_start(H[:, 1, 3, :], a["state"][1, :, ds(g * GC, GC)]).then_inc(s("h0_in"), 16)
                wait_alone(sp, s("st_free"), g * 8 + 5)
                for d in range(2):
                    sp.dma_start(st_out[d, :, ds(g * GC, GC)], cst[:, d, :]).then_inc(s("cst_out"), 16)
            load(JOB_U, win[:, :, 0:512], 512)
            load(JOB_U + 1, win[:, :, 512:1024], 512)
            sp.wait_ge(s("y_free"), NG * NT + 1)
            for i, name in enumerate(("posc", "poss")):
                sp.dma_start(posm[:, i], a[name].rearrange("(k p) n -> p k n", p=P)).then_inc(s("posm_in"), 16)
            wf = a["w_fourier"].rearrange("(k p) n -> p k n", p=P)
            for j in range(2):
                load(JOB_FO + j, wf[:, :, 512 * j:512 * j + 512], 512)
            for j in range(2):
                load(JOB_GA + j, win[:, :, COL_GATE + 512 * j:COL_GATE + 512 * j + 512], 512)
            for j in range(4):
                load(JOB_Z + j, win[:, :, COL_Z + 512 * j:COL_Z + 512 * j + 512], 512)
            for j in range(2):
                load(JOB_GB + j, win[:, :, COL_GATE + D + 512 * j:COL_GATE + D + 512 * j + 512], 512)
            wso = a["w_ssd_out"].rearrange("(k p) n -> p k n", p=P)
            for j in range(4):
                load(JOB_SO + j, wso[:, :, 256 * j:256 * j + 256], 256, k=16)
            wo = a["w_out"].rearrange("(k p) n -> p k n", p=P)
            for j in range(2):
                load(JOB_WO + j, wo[:, :, 512 * j:512 * j + 512], 512)
            sp.wait_ge(s("tr_free"), T_NORM2)
            sp.dma_start(x1, a["x"].rearrange("(t p) c -> p t c", p=P)).then_inc(s("x1_in"), 16)
            sp.dma_start(pos1, a["pos"].rearrange("(t p) c -> p t c", p=P)).then_inc(s("x1_in"), 16)
            sp.wait_ge(s("h2_ready"), NT)
            sp.dma_start(keys, a["keys"]).then_inc(s("keys_in"), 16)
            wq = a["w_query"].rearrange("(k p) n -> p k n", p=P)
            for j in range(4):
                load(JOB_Q + j, wq[:, :, 512 * j:512 * j + 512], 512)
            yv = y_out.rearrange("(t p) c -> p t c", p=P)
            with sp.Fori(0, NT) as t:
                wait_alone(sp, s("out_ready"), t + 1)
                sp.dma_start(yv[:, ds(t, 1), :], pv.unsqueeze(1)).then_inc(s("out_done"), 16)
            sp.wait_ge(s("out_done"), 16 * NT + 16)
            sp.wait_ge(s("cst_out"), NG * 32 + 16)

        @block.tensor
        def _(pe):
            for nm in ("y_full", "v_used"):
                pe.nop().then_inc(s(nm), 1)
            mm = nc.tensor.matmul

            def need(n):
                pe.wait_ge(w_in[n % 2], loaded(n))

            pe.wait_ge(s("cond_ready"), 1)
            with pe.Fori(0, 6) as i:
                for slot in range(2):
                    pe.wait_ge(w_in[slot], i * 16 + 16)
                    w = ring[slot].rearrange("p (k c) -> p k c", k=KT)
                    for m in range(4):
                        for k in range(KT):
                            last = mm(bank[7][:, ds(i * 16 + (slot * 4 + m) * 2, 2)], w[:, k, m * P:(m + 1) * P],
                                      cond[:, k, :], start=(k == 0), stop=(k == KT - 1))
                    last.then_inc(s("w_free"), 1)

            def transpose_unit(u, blocks, bk=None):
                if not isinstance(u, int) or u >= 2:
                    pe.wait_ge(s("tr_free"), u - 1)
                b = bank[5 + (u % 2 if isinstance(u, int) else bk)]
                for i, blk in enumerate(blocks):
                    last = nc.tensor.transpose(b[:, i * P:(i + 1) * P], blk, ident)
                last.then_inc(s("tr_full"), 1)

            pe.wait_ge(s("consts_in"), 16 * len(CONSTS))
            for t in range(NT):
                pe.wait_ge(s("xn_ready"), t + 1)
                for h in range(2):
                    transpose_unit(T_NORM1 + 2 * t + h,
                                   [x0[:, t, (4 * h + i) * P:(4 * h + i + 1) * P] for i in range(4)])

            pe.wait_ge(s("tr_free"), T_XB)
            pe.wait_ge(s("wdt_in"), 16)
            pe.wait_ge(s("coef_ready"), 1)
            for t in range(NT):
                for k in range(KT):
                    last = mm(bank[7][:, 64 * t:64 * t + 64], hT[:, k, t * P:(t + 1) * P], wdt[:, k, :],
                              start=(k == 0), stop=(k == KT - 1))
            last.then_inc(s("dt_full"), 1)
            pe.wait_ge(s("dA_ready"), 1)
            b7 = bank[7][:, 0:320].rearrange("p (t h) -> p t h", t=NT)
            for d in range(2):
                mm(b7[:, :, 32 * d:32 * d + 32], tri[d], dA[:, :, 32 * d:32 * d + 32], start=True, stop=True)
            mm(bank[0][:, 0:320], ones, dA.rearrange("p t h -> p (t h)"), start=True, stop=True).then_inc(s("cs_full"), 1)

            pe.wait_ge(s("tabs_ready"), 1)
            pe.wait_ge(s("identb_ready"), 1)
            with pe.Fori(0, NG) as g:
                if True:
                    pe.wait_ge(s("y_free"), g * NT + 1)
                for i in range(6):
                    if i == 0:
                        pe.wait_ge(w_in[0], g * 16 + loaded(JOB_XBC))
                    if i == 4:
                        pe.wait_ge(w_in[1], g * 32 + loaded(JOB_XBC + 1))
                    if i >= 2:
                        pe.wait_ge(s("ch_free"), g * 6 + i - 1)
                    w = ring[i // 4].rearrange("p (k c) -> p k c", k=KT)
                    c0 = (i % 4) * P
                    for k in range(KT):
                        mm(bank[i % 2][:, :], w[:, k, c0:c0 + P], hT[:, k, P:TOK], start=(k == 0), stop=(k == KT - 1))
                    for k in range(KT):
                        last = mm(bank[2 + i % 2][:, 0:P], w[:, k, c0:c0 + P], hT[:, k, 0:P],
                                  start=(k == 0), stop=(k == KT - 1))
                    last.then_inc(s("ch_full"), 1)
                    if i == 3 or i == 5:
                        pe.wait_ge(s("ch_full"), g * 6 + i + 1)
                        pe.nop().then_inc(s("w_free"), 1)
                pe.wait_ge(s("silu_done"), g * 6 + 6)
                for t in range(NT):
                    transpose_unit(g * XB_UNITS + T_XB + t, [xs[:, i, t * P:(t + 1) * P] for i in range(4)], t % 2)
                transpose_unit(g * XB_UNITS + T_XB + 5, [BT[:, t * P:(t + 1) * P] for t in range(4)], 1)
                transpose_unit(g * XB_UNITS + T_XB + 6, [BT[:, 4 * P:5 * P]], 0)
                for c in range(NT):
                    b = bank[4][:, c * P:(c + 1) * P] if c < 4 else bank[7][:, 0:P]
                    last = mm(b, BT[:, c * P:(c + 1) * P], CT[:, c * P:(c + 1) * P], start=True, stop=True)
                last.then_inc(s("cb_full"), 1)
                pe.wait_ge(s("tr_free"), g * XB_UNITS + T_XB + 7)
                for k, (d, c) in enumerate(STATES):
                    pe.wait_ge(s("xd_ready"), g * 8 + k + 1)
                    if k >= 2:
                        pe.wait_ge(s("st_free"), g * 8 + k - 1)
                    mm(bank[k % 2][:, :], Btok[:, c, :], xd[:, k, :], start=True, stop=True).then_inc(s("st_full"), 1)

                def decay_rows(u):
                    c, hq = divmod(u, 2)
                    for d in range(2):
                        e = 2 * u + d
                        if e >= 4:
                            pe.wait_ge(s("e_done"), g * 20 + e - 3)
                        b = bank[2 * (u % 2) + d]
                        mm(b[:, :], identb[:], maskb[:, d, :].unsqueeze(1).broadcast_to([P, 4, P]),
                           start=True, stop=False, skip_group_check=True)
                        for j in range(4):
                            last = mm(b[:, j * P:(j + 1) * P],
                                      dAg[:, c, d, 4 * hq + j:4 * hq + j + 1].broadcast_to([P, P]), tri[d],
                                      start=False, stop=(j == 3), skip_group_check=True)
                        last.then_inc(s("e_full"), 1)

                pe.wait_ge(s("st_free"), g * 8 + 8)
                pe.wait_ge(s("dAg_ready"), g + 1)
                pe.wait_ge(s("h0_in"), g * 32 + 32)
                decay_rows(0)
                for u in range(2 * NT):
                    c, hq = divmod(u, 2)
                    if u + 1 < 2 * NT:
                        decay_rows(u + 1)
                    if c and not hq:
                        pe.wait_ge(s("cb_done"), g + 1)
                        pe.wait_ge(s("y_free"), g * NT + c + 1)
                        for d in range(2):
                            last = mm(bank[(4, 7)[d]][:, :], CT[:, c * P:(c + 1) * P], H[:, d, c - 1, :],
                                      start=True, stop=True)
                        last.then_inc(s("yo_full"), 1)
                    pe.wait_ge(s("m_done"), g * 20 + 2 * u + 2)
                    if not hq:
                        pe.wait_ge(s("xc_ready"), g * NT + c + 1)
                        if c >= 2:
                            pe.wait_ge(s("y_free"), g * NT + c)
                    for j in range(4):
                        r = 4 * hq + j
                        for d in range(2):
                            last = mm(bank[5 + c % 2][:, r * HD:(r + 1) * HD], Mm[:, 2 * (u % 2) + d, j, :],
                                      xc[:, c % 2, d, r * HD:(r + 1) * HD], start=(d == 0), stop=(d == 1))
                    last.then_inc(s("y_full"), 1)

            def product_tile(q, lhs, k_tiles, w, cols=512):
                t = q % NT
                if q >= NT:
                    pe.wait_ge(s("tm_free"), q - 4)
                for k in range(k_tiles):
                    last = mm(bank[t][:, 0:cols], lhs[:, k, t * P:(t + 1) * P], w[:, k, :],
                              start=(k == 0), stop=(k == k_tiles - 1))
                last.then_inc(s("tm_full"), 1)

            def job(n, q, lhs, k_tiles=KT, cols=512):
                need(n)
                w = ring[n % 2].rearrange("p (k c) -> p k c", k=k_tiles)
                for t in range(NT):
                    product_tile(q + t, lhs, k_tiles, w, cols)
                pe.wait_ge(s("tm_full"), q + NT)
                pe.nop().then_inc(s("w_free"), 1)

            pe.wait_ge(s("y_free"), NG * NT + 1)
            for j in range(2):
                job(JOB_U + j, Q_U + 5 * j, hT)

            pe.wait_ge(s("tm_free"), Q_U + 10)
            pe.wait_ge(s("posm_in"), 32)
            pe.wait_ge(s("chm_in"), 16)

            def over_positions(f):
                if f:
                    pe.wait_ge(s("d1_act"), f)
                    pe.wait_ge(s("d1_dve"), f)
                fs = slice(f * P, (f + 1) * P)
                for i in range(2):
                    for k in range(4):
                        mm(bank[5 + i][:, :], Us[:, 1 + k, fs], posm[:, i, k, :], start=(k == 0), stop=(k == 3))
                for i in range(2):
                    last = mm(bank[(7, 4)[i]][:, 0:P], Us[:, 0, fs], chm[:, i, :], start=True, stop=True)
                last.then_inc(s("d1_full"), 1)

            over_positions(0)
            for f in range(KT):
                if f + 1 < KT:
                    over_positions(f + 1)
                if f + 1 == KT:
                    pe.wait_ge(s("d1_act"), KT)
                    pe.wait_ge(s("d1_dve"), KT)
                if f >= 2:
                    pe.wait_ge(s("d2_free"), f - 1)
                for i in range(2):
                    m = chm[:, 2 * i, :]
                    mm(bank[f % 2][:, :], m, Pq[:, f % 2, i, P:TOK], start=(i == 0), stop=(i == 1))
                for i in range(2):
                    last = mm(bank[2 + f % 2][:, 0:P], chm[:, 2 * i, :], Pq[:, f % 2, i, 0:P],
                              start=(i == 0), stop=(i == 1))
                last.then_inc(s("d2_full"), 1)
            pe.wait_ge(s("d2_free"), KT)
            for j in range(2):
                job(JOB_FO + j, Q_FO + 5 * j, FT)
            for j in range(2):
                job(JOB_GA + j, Q_GA + 5 * j, hT)

            def turn_y(j):
                for t in range(NT):
                    pe.wait_ge(s("gt_used"), 10 + 5 * j + t + 1)
                    transpose_unit(T_Y + 5 * j + t, [Y[:, t, (4 * j + i) * P:(4 * j + i + 1) * P] for i in range(4)])

            for j in range(4):
                job(JOB_Z + j, Q_Z + 5 * j, hT)
                if j:
                    turn_y(j - 1)
            job(JOB_GB, Q_GB, hT)
            turn_y(3)
            job(JOB_GB + 1, Q_GB + 5, hT)

            pe.wait_ge(s("tr_free"), T_MERGE)
            for v in range(8):
                kind, who = divmod(v, 2)
                for h in range(2):
                    u = 2 * v + h
                    if u >= 1:
                        pe.wait_ge(s("row_free"), u)
                    for i in range(4):
                        k = 4 * h + i
                        col = (scl[:, 2, k, who:who + 1], scl[:, 1, k, who:who + 1],
                               mod[:, SH2 * 8 + k, who:who + 1], scl[:, 3, k, who:who + 1])[kind]
                        last = mm(bank[7][:, i * P:(i + 1) * P], col.broadcast_to([P, P]), ident, start=True, stop=True)
                    last.then_inc(s("row_full"), 1)

            for j in range(4):
                job(JOB_SO + j, Q_SO + 5 * j, yT, 16, 256)
            pe.wait_ge(s("mg_done"), 20)
            for t in range(NT):
                for h in range(2):
                    transpose_unit(T_MERGE + 2 * t + h,
                                   [a_out[:, t, (4 * h + i) * P:(4 * h + i + 1) * P] for i in range(4)])
            pe.wait_ge(s("tr_free"), T_NORM2)
            for j in range(2):
                job(JOB_WO + j, Q_WO + 5 * j, mT)

            for t in range(NT):
                pe.wait_ge(s("h2_ready"), t + 1)
                for h in range(2):
                    transpose_unit(T_NORM2 + 2 * t + h,
                                   [h2[:, t, (4 * h + i) * P:(4 * h + i + 1) * P] for i in range(4)])
            pe.wait_ge(s("tr_free"), T_NORM2 + 10)
            pe.wait_ge(s("tm_free"), Q_WO + 10)
            for j in range(4):
                need(JOB_Q + j)
                w = ring[(JOB_Q + j) % 2].rearrange("p (k c) -> p k c", k=KT)
                for i in range(4):
                    n = 6 * NG + 4 * j + i
                    if j or i >= 2:
                        pe.wait_ge(s("ch_free"), n - 1)
                    for k in range(KT):
                        mm(bank[i % 2][:, :], w[:, k, i * P:(i + 1) * P], h2T[:, k, P:TOK],
                           start=(k == 0), stop=(k == KT - 1))
                    for k in range(KT):
                        last = mm(bank[2 + i % 2][:, 0:P], w[:, k, i * P:(i + 1) * P], h2T[:, k, 0:P],
                                  start=(k == 0), stop=(k == KT - 1))
                    last.then_inc(s("ch_full"), 1)
                pe.wait_ge(s("ch_full"), n + 1)
                pe.nop().then_inc(s("w_free"), 1)
            pe.wait_ge(s("keys_in"), 16)
            pe.wait_ge(s("ch_free"), 6 * NG + 16)
            for u in range(4 * NT):
                t, q4 = divmod(u, 4)
                if u >= 4:
                    pe.wait_ge(s("sc_free"), u - 3)
                for i in range(4):
                    hi = 4 * q4 + i
                    last = mm(bank[4 + u % 4][:, i * P:(i + 1) * P], qT[:, hi, t * P:(t + 1) * P], keys[:, hi, :],
                              start=True, stop=True)
                last.then_inc(s("sc_full"), 1)
            with pe.Fori(0, NT) as t:
                pe.wait_ge(s("pv_done"), t + 1)
                for i in range(2):
                    mm(bank[i][:, :], zerob[:], maskb[:, 0, :].unsqueeze(1).broadcast_to([P, 4, P]),
                       start=True, stop=False, skip_group_check=True)
                with pe.Fori(0, PH) as h:
                    for m in range(TOPK):
                        pe.wait_ge(s("diag_done"), t * PH * TOPK + h * TOPK + m + 1)
                        pe.wait_ge(v_in[m % NSLOT], t * PH * 32 + h * 32 + 16 * (m // NSLOT + 1))
                        for i in range(2):
                            last = mm(bank[i][:, :], diag[:, m % 4, :], vrow[:, m % NSLOT, 512 * i:512 * i + 512],
                                      start=False, stop=False, skip_group_check=True)
                        last.then_inc(s("v_used"), 1)

        @block.scalar
        def _(act):
            act.nop().then_inc(s("pv_done"), 1)
            A = nc.scalar.activation
            ch = Chain(act, s("act"))
            act.wait_ge(s("consts_in"), 16 * len(CONSTS))
            A(cond[:], cond[:], ACT.Silu).then_inc(s("cond_ready"), 1)
            A(hrow[:, 0, :], hrow[:, 0, :], ACT.Exp).then_inc(s("nega"), 1)
            sq = hT.rearrange("p k t -> p (k t)")
            for t in range(NT):
                act.wait_ge(s("x_ready"), t) if t else act.wait_ge(s("x_in"), 32)
                A(sq[:, t * D:(t + 1) * D], x0[:, t, :], ACT.Square, accum_out=stat[:, t:t + 1]).then_inc(s("ssq1"), 1)
            act.wait_ge(s("var1"), 1)
            A(stat[:, 0:NT], stat[:, 0:NT], ACT.Sqrt).then_inc(s("std1"), 1)
            act.wait_ge(s("v_ready"), 1)
            ch(A(tmp, tmp, ACT.Exp))
            A(tmp, tmp, ACT.Ln, bias=1.0).then_inc(s("softp"), 1)
            b7 = bank[7][:, 0:320].rearrange("p (t h) -> p t h", t=NT)
            b0 = bank[0][:, 0:320].rearrange("p (t h) -> p t h", t=NT)
            act.wait_ge(s("tmc_ready"), 1)
            A(ecs, b7, ACT.Exp).then_inc(s("exps_ready"), 1)
            A(ecd, b0, ACT.Exp).then_inc(s("exps_ready"), 1)
            A(tmp, tmp, ACT.Exp).then_inc(s("exps_ready"), 1)

            with act.Fori(0, NG) as g:
                def silu(i):
                    act.wait_ge(s("conv_done"), g * 6 + i + 1)
                    if i == 0:
                        act.wait_ge(s("tr_full"), g * XB_UNITS + T_XB)
                        act.wait_ge(s("cst_out"), g * 32 + 16)
                        act.wait_ge(s("y_free"), g * NT + 1)
                    if i == 4:
                        act.wait_ge(s("y_full"), g * 10 + 1)
                    dst = xs[:, i, :] if i < 4 else (BT, CT)[i - 4]
                    A(dst[:, 0:P], acc[:, i % 2, 0:P], ACT.Silu)
                    A(dst[:, P:TOK], acc[:, i % 2, 132:644], ACT.Silu).then_inc(s("silu_done"), 1)

                for i in range(6):
                    act.wait_ge(s("ch_full"), g * 6 + i + 1)
                    if i >= 2:
                        act.wait_ge(s("conv_done"), g * 6 + i - 1)
                    A(cin[:, i % 2, 2:130], bank[2 + i % 2][:, 0:P], ACT.Copy)
                    A(cin[:, i % 2, 134:646], bank[i % 2][:, :], ACT.Copy).then_inc(s("ch_free"), 1)
                    if i:
                        silu(i - 1)
                silu(5)
                act.wait_ge(s("cb_full"), g + 1)
                A(cbT[:, 0:4, :], bank[4][:, :].rearrange("p (t c) -> p t c", t=4), ACT.Copy)
                A(cbT[:, 4, :], bank[7][:, 0:P], ACT.Copy).then_inc(s("cb_done"), 1)
                for e in range(20):
                    u, d = divmod(e, 2)
                    c, hq = divmod(u, 2)
                    act.wait_ge(s("e_full"), g * 20 + e + 1)
                    if e >= 2:
                        act.wait_ge(s("m_done"), g * 20 + e - 1)
                    for j in range(4):
                        last = A(Ee[:, e % 2, j, :], bank[2 * (u % 2) + d][:, j * P:(j + 1) * P], ACT.Exp,
                                 bias=ncs[:, c, ds(g * HG + 32 * d + 4 * hq + j, 1)])
                    last.then_inc(s("e_done"), 1)

            def take(q, dst, func, cols=512, **kw):
                act.wait_ge(s("tm_full"), q + 1)
                A(dst, bank[q % NT][:, 0:cols], func, **kw).then_inc(s("tm_free"), 1)

            for q in range(Q_U, Q_U + 10):
                j, t = divmod(q - Q_U, NT)
                take(q, Us[:, t, 512 * j:512 * j + 512], ACT.Copy)
            for f in range(KT):
                act.wait_ge(s("d1_full"), f + 1)
                if f >= 2:
                    act.wait_ge(s("d2_full"), f - 1)
                A(Pq[:, f % 2, 0, 0:P], bank[7][:, 0:P], ACT.Copy)
                A(Pq[:, f % 2, 0, P:TOK], bank[5][:, :], ACT.Copy).then_inc(s("d1_act"), 1)
            for q in range(Q_FO, Q_FO + 10):
                j, t = divmod(q - Q_FO, NT)
                take(q, a_out[:, t, 512 * j:512 * j + 512], ACT.Copy)
            for n, q in enumerate(range(Q_GA, Q_GA + 10)):
                if n >= 4:
                    act.wait_ge(s("gt_used"), n - 3)
                take(q, gt[:, n % 4, :], ACT.Sigmoid)
            for n, q in enumerate(range(Q_Z, Q_Z + 20)):
                j, t = divmod(n, NT)
                act.wait_ge(s("gt_used"), 10 + n - 3)
                take(q, gt[:, (10 + n) % 4, :], ACT.Silu)
            act.wait_ge(s("gt_used"), 30)
            for t in range(NT):
                for j in range(4):
                    if t:
                        act.wait_ge(s("ssqy"), 4 * t + j - 3)
                    A(gt[:, j, :], Y[:, t, 512 * j:512 * j + 512], ACT.Square,
                      accum_out=stat[:, 10 + 4 * t + j:11 + 4 * t + j]).then_inc(s("ssqy"), 1)
            for q in range(Q_GB, Q_GB + 10):
                j, t = divmod(q - Q_GB, NT)
                take(q, sB[:, t, 512 * j:512 * j + 512], ACT.Sigmoid)
            act.wait_ge(s("vary"), 1)
            A(stat[:, 30:35], stat[:, 30:35], ACT.Sqrt).then_inc(s("stdy"), 1)
            act.wait_ge(s("rstdy"), 1)
            act.wait_ge(s("ssqy"), 20)
            for n, q in enumerate(range(Q_SO, Q_SO + 20)):
                j, t = divmod(n, NT)
                if n >= 4:
                    act.wait_ge(s("mg_done"), n - 3)
                take(q, gt[:, n % 4, 0:256], ACT.Copy, 256, scale=stat[:, 30 + t:31 + t])
            for n, q in enumerate(range(Q_WO, Q_WO + 10)):
                j, t = divmod(n, NT)
                act.wait_ge(s("tm_full"), q + 1)
                if n == 0:
                    act.wait_ge(s("mg_done"), 20)
                    act.wait_ge(s("tm_free"), Q_WO)
                if n >= 4:
                    act.wait_ge(s("ssqm"), n - 3)
                A(gt[:, n % 4, :], bank[q % NT][:, :], ACT.Square,
                  accum_out=stat[:, 36 + 2 * t + j:37 + 2 * t + j]).then_inc(s("ssqm"), 1)
                take(q, mix[:, t, 512 * j:512 * j + 512], ACT.Copy)
            act.wait_ge(s("varm"), 1)
            A(stat[:, 46:51], stat[:, 46:51], ACT.Sqrt).then_inc(s("stdm"), 1)
            for t in range(NT):
                act.wait_ge(s("x1_done"), t + 1)
                A(mix[:, t, :], x1[:, t, :], ACT.Square, accum_out=stat[:, 51 + t:52 + t]).then_inc(s("ssqn"), 1)
            act.wait_ge(s("varn"), 1)
            A(stat[:, 51:56], stat[:, 51:56], ACT.Sqrt).then_inc(s("stdn"), 1)

            for n in range(16):
                act.wait_ge(s("ch_full"), 6 * NG + n + 1)
                A(qT[:, n, 0:P], bank[2 + n % 2][:, 0:P], ACT.Copy)
                A(qT[:, n, P:TOK], bank[n % 2][:, :], ACT.Copy).then_inc(s("ch_free"), 1)
            for u in range(4 * NT):
                act.wait_ge(s("sc_full"), u + 1)
                A(score[:, u // 4, 512 * (u % 4):512 * (u % 4) + 512], bank[4 + u % 4][:, :],
                  ACT.Copy).then_inc(s("sc_free"), 1)
            with ch.loop(NT, 1) as t:
                with act.Fori(0, PH) as h:
                    n = t * PH * TOPK + h * TOPK
                    act.wait_ge(s("u_used"), n + TOPK + 1)
                    A(ex, d_tab[:, ds(n, TOPK)], ACT.Exp, accum_out=esum)
                    A(ge, dots, ACT.Gelu_apprx_tanh).then_inc(s("ge_done"), 1)
                    act.wait_ge(s("w_done"), t * PH + h + 1)
                    for m in range(TOPK):
                        act.wait_ge(s("v_used"), n + (m - 2)) if m >= 4 else act.wait_ge(s("v_used"), n + 1)
                        A(diag[:, m % 4, :], ident, ACT.Copy, scale=w_tab[:, ds(n + m, 1)]).then_inc(s("diag_done"), 1)
                act.wait_ge(s("v_used"), t * PH * TOPK + PH * TOPK + 1)
                act.wait_ge(s("out_done"), t * 16 + 16)
                for i in range(2):
                    last = A(pv[:, 512 * i:512 * i + 512], bank[i][:, :], ACT.Copy)
                last.then_inc(s("pv_full"), 1)
                act.wait_ge(s("pv_full"), t + 1)
                ch(A(h2sq, pv, ACT.Square, accum_out=pstat[:, 0:1]))
                A(pstat[:, 1:2], pstat[:, 0:1], ACT.Sqrt, bias=eps[:], scale=1.0 / D).then_inc(s("pv_done"), 1)

        @block.gpsimd
        def _(pool):
            TT = nc.gpsimd.tensor_tensor
            with pool.Fori(0, NG) as g:
                x8 = [xtok[:, c, :].rearrange("p (r w) -> p r w", r=HG) for c in range(NT)]
                pool.wait_ge(s("tabs_ready"), 1)
                pool.wait_ge(s("tr_free"), g * XB_UNITS + T_XB + 5)
                pool.wait_ge(s("y_full"), g * 10 + 1)
                for k, (d, c) in enumerate(STATES):
                    TT(xd[:, k, :].rearrange("p (r w) -> p r w", r=HG), x8[c],
                       dtd[:, c, ds(g * HG + 32 * d, HG)].unsqueeze(2).broadcast_to([P, HG, HD]),
                       ALU.mult).then_inc(s("xd_ready"), 1)
                for c in range(NT):
                    wait_alone(pool, s("y_free"), g * NT + c + 1)
                    TT(xD.rearrange("p (r w) -> p r w", r=HG), x8[c],
                       dsum[:, ds(g * HG, HG)].unsqueeze(2).broadcast_to([P, HG, HD]),
                       ALU.mult).then_inc(s("xD_ready"), 1)

            nc.gpsimd.memset(eps[:], EPS)

            def rows_of(kind, m, step):
                slots, ins, used, table, idx = ((urow, u_in, "u_used", a["peer_u"], idx_u),
                                                (vrow, v_in, "v_used", a["peer_v"], idx_v))[kind]
                if isinstance(step, int) and step == 0 and m < NSLOT:
                    pass
                else:
                    wait_alone(pool, s(used), step * TOPK + (m - NSLOT + 2))
                nc.gpsimd.indirect_dma_start(
                    slots[:, m % NSLOT, :], None, table,
                    bass.IndirectOffsetOnAxis(ap=idx[rows_of.parity][:, m:m + 1], axis=0)).then_inc(ins[m % NSLOT], 16)

            pch = Chain(pool, s("idx_cp"))
            pool.wait_ge(s("sc_free"), 4 * NT)
            pool.wait_ge(s("topk_done"), 1)
            pch(nc.gpsimd.tensor_copy(idx_u[0], idx_tab[:, 0:TOPK]))
            rows_of.parity = 0
            for m in range(TOPK):
                rows_of(0, m, 0)

            def both(step, parity, nxt, last_of_all=False):
                pool.wait_ge(s("topk_done"), nxt + 1)
                pool.wait_ge(s("u_used"), step * TOPK + 1)
                pool.wait_ge(s("v_used"), step * TOPK - TOPK + 1) if not isinstance(step, int) else None
                nc.gpsimd.tensor_copy(idx_u[1 - parity], idx_tab[:, ds(nxt * TOPK, TOPK)])
                pch(nc.gpsimd.tensor_copy(idx_v[parity], idx_tab[:, ds(step * TOPK, TOPK)]))
                for m in range(TOPK):
                    rows_of.parity = 1 - parity
                    rows_of(0, m, nxt)
                    rows_of.parity = parity
                    rows_of(1, m, step)

            both(0, 0, 1)
            with pch.loop((NS - 2) // 2, 2) as i:
                both(i * 2 + 1, 1, i * 2 + 2)
                both(i * 2 + 2, 0, i * 2 + 3)
            pool.wait_ge(s("v_used"), (NS - 2) * TOPK + 1)
            pch(nc.gpsimd.tensor_copy(idx_v[1], idx_tab[:, (NS - 1) * TOPK:]))
            rows_of.parity = 1
            for m in range(TOPK):
                rows_of(1, m, NS - 1)

        @block.vector
        def _(dve):
            for nm in ("y_free", "u_used"):
                dve.nop().then_inc(s(nm), 1)
            V = nc.vector
            TT, TS, STT, CP = V.tensor_tensor, V.tensor_scalar, V.scalar_tensor_tensor, V.tensor_copy
            ch = Chain(dve, s("dve"))

            def rstd(cols, n, std_sem, var_sem):
                TS(cols, cols, 1.0 / n, EPS, ALU.mult, ALU.add).then_inc(s(var_sem), 1)
                dve.wait_ge(s(std_sem), 1)

            dve.wait_ge(s("consts_in"), 16 * len(CONSTS))
            CP(identb[:], ident)
            V.memset(zerob[:], 0.0)
            CP(maskb[:], shp[:, 4:6, :]).then_inc(s("identb_ready"), 1)
            TT(dsum[:], hrow[:, 2, 0:HEADS], hrow[:, 2, HEADS:], ALU.add)
            dve.wait_ge(s("x_in"), 32)
            dve.wait_ge(s("pos_in"), 16)
            for t in range(1, NT):
                TT(x0[:, t, :], x0[:, t, :], pos0[:, t - 1, :], ALU.add).then_inc(s("x_ready"), 1)
            dve.wait_ge(s("ssq1"), NT)
            rstd(stat[:, 0:NT], D, "std1", "var1")
            ch(V.reciprocal(stat[:, 0:NT], stat[:, 0:NT]))
            dve.wait_ge(s("x_ready"), NT - 1)
            for t in range(NT):
                TS(x0[:, t, :], x0[:, t, :], stat[:, t:t + 1], None, ALU.mult).then_inc(s("xn_ready"), 1)
            dve.wait_ge(s("w_free"), 12)
            ch(TT(mod[:], bank[7][:, 0:96].rearrange("p (m c) -> p m c", c=2),
                  adab[:].unsqueeze(2).broadcast_to([P, 48, 2]), ALU.add))
            for i, (m, n) in enumerate(((SC1, 0), (SC2, 2))):
                STT(scl[:, i], mod[:, m * 8:m * 8 + 8, :], 1.0, norms[:, n, :].unsqueeze(2).broadcast_to([P, KT, 2]),
                    ALU.add, ALU.mult)
            for i, (m, n) in enumerate(((GA1, 1), (GA2, 3))):
                last = TT(scl[:, 2 + i], mod[:, m * 8:m * 8 + 8, :], norms[:, n, :].unsqueeze(2).broadcast_to([P, KT, 2]),
                          ALU.mult)
            last.then_inc(s("coef_ready"), 1)
            dve.wait_ge(s("coef_ready"), 1)
            for t in range(NT):
                who = 1 if t else 0
                for h in range(2):
                    u = T_NORM1 + 2 * t + h
                    dve.wait_ge(s("tr_full"), u + 1)
                    for i in range(4):
                        k = 4 * h + i
                        last = TS(hT[:, k, t * P:(t + 1) * P], bank[5 + u % 2][:, i * P:(i + 1) * P],
                                  scl[:, 0, k, who:who + 1], mod[:, SH1 * 8 + k, who:who + 1], ALU.mult, ALU.add)
                    last.then_inc(s("tr_free"), 1)
            dve.wait_ge(s("dt_full"), 1)
            dve.wait_ge(s("nega"), 1)
            v = dtd
            b7 = bank[7][:, 0:320].rearrange("p (t h) -> p t h", t=NT)
            b0 = bank[0][:, 0:320].rearrange("p (t h) -> p t h", t=NT)
            all5 = lambda r: r.unsqueeze(1).broadcast_to([P, NT, 64])
            ch(TT(v, b7, all5(hrow[:, 1, :]), ALU.add))
            STT(tmp, v, -1.0, v, ALU.mult, ALU.min).then_inc(s("v_ready"), 1)
            TS(dt_, v, 0.0, None, ALU.max)
            ch(TS(hrow[:, 0, :], hrow[:, 0, :], -1.0, None, ALU.mult))
            dve.wait_ge(s("softp"), 1)
            ch(TT(dt_, dt_, tmp, ALU.add))
            TT(dA, dt_, all5(hrow[:, 0, :]), ALU.mult).then_inc(s("dA_ready"), 1)
            dve.wait_ge(s("cs_full"), 1)
            ch(TS(ncs, b7, -1.0, None, ALU.mult))
            TT(tmp, b0, ncs, ALU.add).then_inc(s("tmc_ready"), 1)
            dve.wait_ge(s("exps_ready"), 3)
            TT(dtd, dt_, tmp, ALU.mult).then_inc(s("tabs_ready"), 1)
            for lo, hi in ((0, 2), (130, 134), (646, 648)):
                last = V.memset(cin[:, :, lo:hi], 0.0)
            ch(last)
            dve.wait_ge(s("tabs_ready"), 1)

            DVE_G = 6 * 4 + 6 + 4 * 3 + 1
            with ch.loop(NG, DVE_G) as g:
                for i in range(6):
                    tile = g * 4 + i if i < 4 else g + (16 if i == 4 else 20)
                    dve.wait_ge(s("ch_free"), g * 6 + i + 1)
                    if i >= 2:
                        dve.wait_ge(s("silu_done"), g * 6 + i - 1)
                    o = acc[:, i % 2, 0:644]
                    w = lambda k: convw[:, ds(tile, 1), k]
                    ch(TS(o, cin[:, i % 2, 0:644], w(0), convb[:, ds(tile, 1)], ALU.mult, ALU.add))
                    for k in range(1, TAPS):
                        last = STT(o, cin[:, i % 2, k:k + 644], w(k), o, ALU.mult, ALU.add)
                        if k < TAPS - 1:
                            ch(last)
                    last.then_inc(s("conv_done"), 1)
                CP(dAg[:, :, 0, :], dA[:, :, ds(g * HG, HG)])
                CP(dAg[:, :, 1, :], dA[:, :, ds(g * HG + 32, HG)]).then_inc(s("dAg_ready"), 1)
                for t in range(NT):
                    dve.wait_ge(s("tr_full"), g * XB_UNITS + T_XB + t + 1)
                    CP(xtok[:, t, :], bank[5 + t % 2][:, :]).then_inc(s("tr_free"), 1)
                dve.wait_ge(s("tr_full"), g * XB_UNITS + T_XB + 6)
                CP(Btok[:, 0:4, :], bank[6][:, :].rearrange("p (t c) -> p t c", t=4)).then_inc(s("tr_free"), 1)
                dve.wait_ge(s("tr_full"), g * XB_UNITS + T_XB + 7)
                CP(Btok[:, 4, :], bank[5][:, 0:P]).then_inc(s("tr_free"), 1)
                r8 = lambda ap: ap.rearrange("p (r w) -> p r w", r=HG)
                per_head = lambda table, c, d: table[:, c, ds(g * HG + 32 * d, HG)].unsqueeze(2).broadcast_to([P, HG, HD])
                dve.wait_ge(s("h0_in"), g * 32 + 32)
                dve.wait_ge(s("tr_free"), g * XB_UNITS + T_XB + 7)
                for k, (d, c) in enumerate(STATES):
                    if c:
                        here, there = H[:, d, c - 1, :], H[:, d, c - 2 if d else c, :]
                        if k in (1, 2, 6, 7):
                            dve.wait_ge(s("st_free"), g * 8 + k)
                        ch(TT(r8(there), r8(here), per_head(ecd, c, d), ALU.mult))
                        dve.wait_ge(s("st_full"), g * 8 + k + 1)
                        TT(there, there, bank[k % 2][:, :], ALU.add).then_inc(s("st_free"), 1)
                    else:
                        dve.wait_ge(s("st_full"), g * 8 + k + 1)
                        CP(cst[:, d, :], bank[k % 2][:, :]).then_inc(s("st_free"), 1)

                def scaled_x(c):
                    if c >= 2:
                        dve.wait_ge(s("y_full"), g * 10 + 2 * c - 1)
                    for d in range(2):
                        last = TT(r8(xc[:, c % 2, d, :]), r8(xtok[:, c, :]), per_head(dt_, c, d), ALU.mult)
                    last.then_inc(s("xc_ready"), 1)

                def chunk_out(c):
                    yc = Y[:, c, ds(g * GC, GC)]
                    dve.wait_ge(s("y_full"), g * 10 + 2 * c + 3)
                    dve.wait_ge(s("xD_ready"), g * NT + c + 1)
                    if c:
                        dve.wait_ge(s("yo_full"), g * 4 + c)
                        TT(r8(yc), r8(bank[4][:, :]), per_head(ecs, c, 0), ALU.mult)
                        ch(TT(r8(yt), r8(bank[7][:, :]), per_head(ecs, c, 1), ALU.mult))
                        ch(TT(yt, yt, xD, ALU.add))
                        ch(TT(yc, yc, yt, ALU.add))
                    else:
                        ch(CP(yc, xD))
                    TT(yc, yc, bank[5 + c % 2][:, :], ALU.add).then_inc(s("y_free"), 1)

                dve.wait_ge(s("cb_done"), g + 1)
                scaled_x(0)
                for u in range(2 * NT):
                    c, hq = divmod(u, 2)
                    for d in range(2):
                        e = 2 * u + d
                        dve.wait_ge(s("e_done"), g * 20 + e + 1)
                        if u >= 2:
                            dve.wait_ge(s("y_full"), g * 10 + u)
                        TT(Mm[:, 2 * (u % 2) + d], Ee[:, e % 2], cbT[:, c, :].unsqueeze(1).broadcast_to([P, 4, P]),
                           ALU.mult).then_inc(s("m_done"), 1)
                    if not hq:
                        if c:
                            chunk_out(c - 1)
                        if c + 1 < NT:
                            scaled_x(c + 1)
                chunk_out(NT - 1)

            for f in range(KT):
                dve.wait_ge(s("d1_full"), f + 1)
                if f >= 2:
                    dve.wait_ge(s("d2_full"), f - 1)
                CP(Pq[:, f % 2, 1, 0:P], bank[4][:, 0:P])
                CP(Pq[:, f % 2, 1, P:TOK], bank[6][:, :]).then_inc(s("d1_dve"), 1)
                if f:
                    dve.wait_ge(s("d2_full"), f)
                    CP(FT[:, f - 1, 0:P], bank[2 + (f - 1) % 2][:, 0:P])
                    CP(FT[:, f - 1, P:TOK], bank[(f - 1) % 2][:, :]).then_inc(s("d2_free"), 1)
            dve.wait_ge(s("d2_full"), KT)
            CP(FT[:, KT - 1, 0:P], bank[2 + (KT - 1) % 2][:, 0:P])
            CP(FT[:, KT - 1, P:TOK], bank[(KT - 1) % 2][:, :]).then_inc(s("d2_free"), 1)
            for n in range(10):
                j, t = divmod(n, NT)
                dve.wait_ge(s("tm_free"), Q_GA + n + 1)
                ao = a_out[:, t, 512 * j:512 * j + 512]
                TT(ao, ao, gt[:, n % 4, :], ALU.mult).then_inc(s("gt_used"), 1)

            def turned_y(j):
                for t in range(NT):
                    u = T_Y + 5 * j + t
                    dve.wait_ge(s("tr_full"), u + 1)
                    for i in range(4):
                        last = TS(yT[:, 4 * j + i, t * P:(t + 1) * P], bank[5 + u % 2][:, i * P:(i + 1) * P],
                                  ssdn[:, 4 * j + i:4 * j + i + 1], None, ALU.mult)
                    last.then_inc(s("tr_free"), 1)

            for j in range(4):
                for t in range(NT):
                    n = 5 * j + t
                    dve.wait_ge(s("tm_free"), Q_Z + n + 1)
                    yy = Y[:, t, 512 * j:512 * j + 512]
                    TT(yy, yy, gt[:, (10 + n) % 4, :], ALU.mult).then_inc(s("gt_used"), 1)
                if j:
                    turned_y(j - 1)
            turned_y(3)
            dve.wait_ge(s("ssqy"), 20)
            ch(V.tensor_reduce(stat[:, 30:35], stat[:, 10:30].rearrange("p (t j) -> p t j", j=4), AX.X, ALU.add))
            rstd(stat[:, 30:35], DI, "stdy", "vary")
            V.reciprocal(stat[:, 30:35], stat[:, 30:35]).then_inc(s("rstdy"), 1)
            for u in range(16):
                v_, h = divmod(u, 2)
                dve.wait_ge(s("row_full"), u + 1)
                CP(rows[:, v_, 512 * h:512 * h + 512], bank[7][:, :]).then_inc(s("row_free"), 1)
            for n in range(20):
                j, t = divmod(n, NT)
                dve.wait_ge(s("tm_free"), Q_SO + n + 1)
                o = slice(256 * j, 256 * j + 256)
                g_ = gt[:, n % 4, 0:256]
                ch(TT(g_, g_, sB[:, t, o], ALU.mult))
                TT(a_out[:, t, o], a_out[:, t, o], g_, ALU.add).then_inc(s("mg_done"), 1)
            for u in range(10):
                t, h = divmod(u, 2)
                dve.wait_ge(s("tr_full"), T_MERGE + u + 1)
                CP(mT[:, 4 * h:4 * h + 4, t * P:(t + 1) * P],
                   bank[5 + (T_MERGE + u) % 2][:, :].rearrange("p (k t) -> p k t", k=4)).then_inc(s("tr_free"), 1)
            dve.wait_ge(s("x1_in"), 32)
            for t in range(1, NT):
                last = TT(x1[:, t, :], x1[:, t, :], pos1[:, t - 1, :], ALU.add)
            ch(last)
            dve.wait_ge(s("ssqm"), 10)
            dve.wait_ge(s("tm_free"), Q_WO + 10)
            ch(TT(stat[:, 46:51], stat[:, 36:46].rearrange("p (t j) -> p t j", j=2)[:, :, 0],
                  stat[:, 36:46].rearrange("p (t j) -> p t j", j=2)[:, :, 1], ALU.add))
            rstd(stat[:, 46:51], D, "stdm", "varm")
            ch(V.reciprocal(stat[:, 46:51], stat[:, 46:51]))
            dve.wait_ge(s("row_free"), 16)
            for t in range(NT):
                who = 1 if t else 0
                ch(STT(mix[:, t, :], mix[:, t, :], stat[:, 46 + t:47 + t], rows[:, who, :], ALU.mult, ALU.mult))
                TT(x1[:, t, :], x1[:, t, :], mix[:, t, :], ALU.add).then_inc(s("x1_done"), 1)
            dve.wait_ge(s("ssqn"), NT)
            rstd(stat[:, 51:56], D, "stdn", "varn")
            ch(V.reciprocal(stat[:, 51:56], stat[:, 51:56]))
            for t in range(NT):
                who = 1 if t else 0
                ch(STT(h2[:, t, :], x1[:, t, :], stat[:, 51 + t:52 + t], rows[:, 2 + who, :], ALU.mult, ALU.mult))
                TT(h2[:, t, :], h2[:, t, :], rows[:, 4 + who, :], ALU.add).then_inc(s("h2_ready"), 1)
            for u in range(10):
                t, h = divmod(u, 2)
                dve.wait_ge(s("tr_full"), T_NORM2 + u + 1)
                CP(h2T[:, 4 * h:4 * h + 4, t * P:(t + 1) * P],
                   bank[5 + (T_NORM2 + u) % 2][:, :].rearrange("p (k t) -> p k t", k=4)).then_inc(s("tr_free"), 1)

            def best16(vals, idx, src, src2):
                ch(V.max(vals[:, 0:8], src), wait_alone)
                V.max_index(idx[:, 0:8], vals[:, 0:8], src)
                ch(V.match_replace(src2, vals[:, 0:8], src, LOWEST), wait_alone)
                ch(V.max(vals[:, 8:16], src2), wait_alone)
                ch(V.max_index(idx[:, 8:16], vals[:, 8:16], src2), wait_alone)

            def top(t, h):
                n = (t * PH + h) * TOPK
                ch(CP(sw, score[:, ds(t, 1), ds(h * 256, 256)].rearrange("p t (h n) -> p (t h) n", h=2)), wait_alone)
                for half in range(2):
                    best16(v16[:, 16 * half:16 * half + 16], i16[:, 16 * half:16 * half + 16],
                           sw[:, half, :], sw2[:, half, :])
                CP(i16f, i16)
                ch(TT(cand.rearrange("p (a b) -> p a b", a=TOPK),
                      v16[:, 0:16].unsqueeze(2).broadcast_to([P, 16, 16]),
                      v16[:, 16:32].unsqueeze(1).broadcast_to([P, 16, 16]), ALU.add), wait_alone)
                best16(tv, tp, cand, cand2)
                TS(d_tab[:, ds(n, TOPK)], tv, tv[:, 0:1], None, ALU.subtract)
                TS(tij[:, 0:16], tp, 4, None, ALU.logical_shift_right)
                ch(TS(tij[:, 16:32], tp, 15, None, ALU.bitwise_and))
                ch(CP(tijf, tij))
                ch(TT(eq, iota16.unsqueeze(1).broadcast_to([P, 32, 16]), tijf.unsqueeze(2).broadcast_to([P, 32, 16]),
                      ALU.is_equal))
                e4 = eq.rearrange("p (h k) n -> p h k n", h=2)
                ch(TT(e4, e4, i16f.rearrange("p (h n) -> p h n", h=2).unsqueeze(2).broadcast_to([P, 2, 16, 16]),
                      ALU.mult))
                ch(V.tensor_reduce(pick, eq, AX.X, ALU.add))
                STT(idx_tab[:, ds(n, TOPK)], pick[:, 0:16], float(NKEY), pick[:, 16:32],
                    ALU.mult, ALU.add).then_inc(s("topk_done"), 1)

            TOP = 1 + 8 + 1 + 4 + 1 + 1 + 1 + 1 + 1

            def step(t, h, with_top):
                n = t * PH + h
                for m in range(TOPK):
                    dve.wait_ge(u_in[m % NSLOT], n * 32 + 16 * (m // NSLOT + 1))
                    V.tensor_tensor_reduce(out=urow[:, m % NSLOT, :], in0=urow[:, m % NSLOT, :], in1=h2c, scale=1.0,
                                           scalar=0.0, op0=ALU.mult, op1=ALU.add,
                                           accum_out=dots[:, m:m + 1]).then_inc(s("u_used"), 1)
                if with_top:
                    top(t + 1, h)
                dve.wait_ge(s("ge_done"), n + 1)
                ch(V.reciprocal(erec, esum))
                STT(w_tab[:, ds(n * TOPK, TOPK)], ge, erec, ex, ALU.mult, ALU.mult).then_inc(s("w_done"), 1)

            def tile_of(t):
                ch(CP(h2c, h2[:, ds(t, 1), :].rearrange("p t c -> p (t c)")))

            def result(t, who):
                dve.wait_ge(s("pv_done"), t + 2)
                ch(V.reciprocal(pstat[:, 2:3], pstat[:, 1:2]))
                ch(STT(pv, pv, pstat[:, 2:3], rows[:, 6 + who, :], ALU.mult, ALU.mult))
                TT(pv, pv, x1[:, ds(t, 1), :].rearrange("p t c -> p (t c)"), ALU.add).then_inc(s("out_ready"), 1)

            dve.wait_ge(s("h2_ready"), NT)
            dve.wait_ge(s("ssqn"), NT)
            dve.wait_ge(s("sc_free"), 4)
            with ch.loop(PH, TOP) as h:
                top(0, h)
            dve.wait_ge(s("sc_free"), 4 * NT)
            tile_of(0)
            with ch.loop(PH, TOP + 1) as h:
                step(0, h, True)
            tile_of(1)
            step(1, 0, True)
            result(0, 0)
            with ch.loop(PH - 1, TOP + 1) as h:
                step(1, h + 1, True)
            with ch.loop(2, 1 + (TOP + 1) + 2 + (PH - 1) * (TOP + 1)) as i:
                tile_of(i + 2)
                step(i + 2, 0, True)
                result(i + 1, 1)
                with ch.loop(PH - 1, TOP + 1) as h:
                    step(i + 2, h + 1, True)
            tile_of(NT - 1)
            step(NT - 1, 0, False)
            result(NT - 2, 1)
            with ch.loop(PH - 1, 1) as h:
                step(NT - 1, h + 1, False)
            result(NT - 1, 1)


def shape_constants():
    f = np.float32
    i = np.arange(P)
    shp = np.zeros((P, 7, P), f)
    shp[:, 0] = np.eye(P)
    shp[:, 1] = i[:, None] <= i[None, :]
    shp[:, 2] = i[:, None] >= i[None, :]
    shp[:, 3] = 1
    shp[:, 6] = i[None, :]
    shp[:, 4] = np.where(i[:, None] <= i[None, :], 0, NEG)
    shp[:, 5] = np.where(i[:, None] >= i[None, :], 0, NEG)
    ang = 2 * np.pi * ((i[:, None] * i[None, :]) % P) / P
    chm = np.stack([np.cos(ang), np.sin(ang), -np.sin(ang)], 1) / np.sqrt(P)
    l = np.arange(LAT)
    angl = 2 * np.pi * ((l[:, None] * l[None, :]) % LAT) / LAT
    quarter = D // 4
    omega = (1.0 / (f(10000.0) ** (np.arange(quarter, dtype=f) / f(quarter)))).astype(f)
    ar = (l // 64).astype(f)[:, None] * omega
    ac = (l % 64).astype(f)[:, None] * omega
    pos = np.concatenate([np.sin(ar), np.cos(ar), np.sin(ac), np.cos(ac)], -1)
    return {"shp": shp, "chm": chm.astype(f), "posc": (np.cos(angl) / np.sqrt(LAT)).astype(f),
            "poss": (np.sin(angl) / np.sqrt(LAT)).astype(f), "pos": pos.astype(f)}


def layout(i):
    cols = lambda v, n: np.ascontiguousarray(np.asarray(v).reshape(n, P).T)
    i = {k: np.asarray(v) for k, v in i.items()}
    out = dict(shape_constants())
    out["x"] = np.concatenate([i["x_prompt"][0], i["x_sample"][0]], 0)
    out["cond"] = np.stack([cols(i["c_ctx"], KT), cols(i["c"][0], KT)], -1)
    out["ada_b"] = cols(i["b_ada"][0], 48)
    out["norms"] = np.stack([cols(i[n][0], KT) for n in
                             ("norm_mix_pre", "norm_mix_post", "norm_ffn_pre", "norm_ffn_post")], 1)
    out["ssd_norm"] = cols(i["ssd_norm"][0], 16)
    out["conv_w"] = i["w_conv"][0].reshape(TAPS, 24, P).transpose(2, 1, 0)
    out["conv_b"] = cols(i["b_conv"][0], 24)
    for n in ("a_log", "dt_bias", "d_skip"):
        out[n] = i[n].reshape(2 * HEADS)
    out["state"] = i["state_ssd"][0, 0].reshape(2, DI, P).transpose(0, 2, 1)
    for n in ("w_ada", "w_in", "w_fourier", "w_ssd_out", "w_out"):
        out[n] = i[n][0]
    out["w_query"] = i["peer_query"][0]
    out["keys"] = i["peer_sub_keys"][0].reshape(16, P, P).transpose(2, 0, 1)
    out["peer_u"], out["peer_v"] = i["peer_u"][0], i["peer_v"][0]
    return {k: np.ascontiguousarray(v) for k, v in out.items()}


def kernel(**inputs):
    import concourse.bacc as bacc
    from concourse.bass_utils import run_bass_kernel_spmd

    arrays = layout(inputs)
    nc = bacc.Bacc("TRN2", target_bir_lowering=False, num_devices=1)
    args = {k: nc.dram_tensor(f"in_{k}", v.shape, mybir.dt.from_np(v.dtype), kind="ExternalInput").ap()
            for k, v in arrays.items()}
    outs = (nc.dram_tensor("y_out", (TOK, D), F32, kind="ExternalOutput").ap(),
            nc.dram_tensor("state_out", (2, P, DI), F32, kind="ExternalOutput").ap())
    layer_kernel(nc, args, outs)
    r = run_bass_kernel_spmd(nc, [{f"in_{k}": v for k, v in arrays.items()}], core_ids=[0]).results[0]
    y, st = np.asarray(r["y_out"]), np.asarray(r["state_out"])
    return (y[0:P].reshape(1, P, D), y[P:].reshape(1, LAT, D),
            np.ascontiguousarray(st.transpose(0, 2, 1)).reshape(1, 1, 2, HEADS, HD, P))
```

```python
from contextlib import ExitStack, contextmanager

import numpy as np

import concourse.bass as bass
from concourse import mybir
from concourse.bass import ds

F32 = mybir.dt.float32
BF16 = mybir.dt.bfloat16
U32 = mybir.dt.uint32
I32 = mybir.dt.int32
ACT = mybir.ActivationFunctionType
ALU = mybir.AluOpType
AX = mybir.AxisListType

P = 128
D = 1024
KT = D // P
NT = 5
LAT = (NT - 1) * P
TOK = NT * P
HEADS, HD, NG = 32, 64, 4
HG = HEADS // NG
GC = HG * HD
DI = HEADS * HD
TAPS = 5
COL_Z, COL_X = 1024, 3072
COL_B, COL_C = COL_X + DI, COL_X + DI + NG * P
COL_DT = COL_X + DI + 2 * NG * P
COL_GATE = COL_DT + 2 * HEADS
D_IN = COL_GATE + 2 * D
PH, TOPK, NKEY = 8, 16, 128
EPS = 1e-6
GELU_C, GELU_A = float(np.sqrt(2 / np.pi)), 0.044715
NEG = -1e30
LOWEST = -3.0e38
NSLOT = 8
NS = NT * PH

SH1, SC1, GA1, SH2, SC2, GA2 = range(6)

JOB_ADA, JOB_XBC, JOB_U, JOB_FO, JOB_GA, JOB_Z, JOB_GB, JOB_SO, JOB_WO, JOB_Q = (
    0, 12, 20, 22, 24, 26, 30, 32, 36, 38)
Q_U, Q_FO, Q_GA, Q_Z, Q_GB, Q_SO, Q_WO = 0, 10, 20, 30, 50, 60, 80
T_NORM1, T_XB, T_Y, T_MERGE, T_NORM2 = 0, 10, 38, 58, 68
XB_UNITS = 7
BESIDE = {1: 2, 3: 3, 4: 4, 6: 5}
COPY_AT = {u + 1: i for u, i in BESIDE.items()}
CONV_AT = {u + 2: i for u, i in BESIDE.items()}
SILU_AT = {1: 0, 2: 1, **{u + 3: i for u, i in BESIDE.items()}}
STATES = [(1, 4), (1, 3), (1, 2), (1, 0), (0, 0), (0, 1), (0, 2), (0, 3)]


def loaded(n):
    slot, turn = n % 2, n // 2
    extra = 0
    if slot == 1 and n >= JOB_XBC:
        extra = min((n - JOB_XBC) // 2 + 1, NG)
    return 16 * (turn + 1 + extra)


class Chain:

    def __init__(self, eng, sem):
        self.eng, self.sem, self.n, self.marks = eng, sem, 0, 0

    def __call__(self, ins, wait=None):
        ins.then_inc(self.sem, 1)
        self.n, self.marks = self.n + 1, self.marks + 1
        if wait:
            wait(self.eng, self.sem, self.n)
        else:
            self.eng.wait_ge(self.sem, self.n)

    @contextmanager
    def loop(self, count, steps):
        start, before = self.n, self.marks
        with self.eng.Fori(0, count) as i:
            self.n = i * steps + start
            yield i
            assert self.marks - before == steps, (self.marks - before, steps)
        self.n, self.marks = start + count * steps, before + count * steps


def layer_kernel(nc, a, outs):
    y_out, st_out = outs
    with ExitStack() as ctx:
        def sb(name, shape, dt=F32):
            return ctx.enter_context(nc.sbuf_tensor(name, shape, dt))

        def sem(name):
            return ctx.enter_context(nc.semaphore(name))

        bank = [ctx.enter_context(nc.psum_tensor(f"bank{i}", [P, 512], F32)) for i in range(8)]

        shp = sb("shape_consts", [P, 7, P])
        ident, tri, ones = shp[:, 0, :], [shp[:, 1, :], shp[:, 2, :]], shp[:, 3, :]
        identb = sb("identb", [P, P], BF16)
        maskb = sb("maskb", [P, 2, P], BF16)
        zerob = sb("zerob", [P, P], BF16)
        eps = sb("eps", [P, 1])
        cond = sb("cond_sb", [P, KT, 2])
        adab = sb("adab_sb", [P, 48])
        mod = sb("mod", [P, 48, 2])
        norms = sb("norms_sb", [P, 4, KT])
        scl = sb("scl", [P, 4, KT, 2])
        ssdn = sb("ssdn_sb", [P, 16])
        convw = sb("convw_sb", [P, 24, TAPS])
        convb = sb("convb_sb", [P, 24])
        hrow = sb("hrow", [P, 3, 2 * HEADS])
        dsum = sb("dsum", [P, HEADS])
        wdt = sb("wdt", [P, KT, 2 * HEADS])
        tab = sb("tab", [P, 7, NT, 2 * HEADS])
        dt_, dA, ncs, ecs, ecd, dtd, tmp = (tab[:, i] for i in range(7))
        dAg = sb("dAg", [P, NT, 2, HG])
        stat = sb("stat", [P, 64])

        KB = 256
        arena = sb("arena", [P, 189 * KB])

        def at(kb, n):
            o = int(kb * KB)
            assert o + n <= 189 * KB, (kb, n)
            return arena[:, o:o + n]

        hT = at(0, KT * TOK).rearrange("p (k t) -> p k t", k=KT)
        ring = [at(20 + 16 * s, 16 * KB) for s in range(2)]
        Y = at(52, NT * DI).rearrange("p (t c) -> p t c", t=NT)
        x0 = at(92, NT * D).rearrange("p (t c) -> p t c", t=NT)
        pos0 = at(112, 4 * D).rearrange("p (t c) -> p t c", t=4)
        adar = at(52, 6 * D)
        xs = at(92, 4 * TOK).rearrange("p (i t) -> p i t", i=4)
        xtok = at(102, NT * GC).rearrange("p (t c) -> p t c", t=NT)
        Btok = at(112, TOK).rearrange("p (t c) -> p t c", t=NT)
        BT, CT = at(114.5, TOK), at(117, TOK)
        cin = at(119.5, 2 * 648).rearrange("p (s c) -> p s c", s=2)
        acc = at(124.625, 2 * 648).rearrange("p (s c) -> p s c", s=2)
        xd = at(129.75, 8 * 512).rearrange("p (s c) -> p s c", s=8)
        xc = at(145.75, 4 * 512).rearrange("p (s d c) -> p s d c", s=2, d=2)
        Ee = at(153.75, 2 * 512).rearrange("p (s j l) -> p s j l", s=2, j=4)
        Mm = at(157.75, 4 * 512).rearrange("p (s j l) -> p s j l", s=4, j=4)
        H = at(165.75, 8 * 512).rearrange("p (d s c) -> p d s c", d=2, s=4)
        cbT = at(181.75, TOK).rearrange("p (t c) -> p t c", t=NT)
        xD = at(184.25, 512)
        yt = at(186.25, 512)
        cst = xs.rearrange("p i t -> p (i t)")[:, 512:1536].rearrange("p (d c) -> p d c", d=2)
        Us = [at(kb, NT * 512).rearrange("p (t c) -> p t c", t=NT) for kb in (92, 119.5)]
        FT = at(102, KT * TOK).rearrange("p (k t) -> p k t", k=KT)
        Pq = at(132, 4 * TOK).rearrange("p (s d t) -> p s d t", s=2, d=2)
        posm = at(142, 2 * 4 * 512).rearrange("p (s k t) -> p s k t", s=2, k=4)
        a_out = at(158, NT * D).rearrange("p (t c) -> p t c", t=NT)
        gt = at(178, 4 * 512).rearrange("p (s c) -> p s c", s=4)
        chm = at(186.5, 3 * P).rearrange("p (i n) -> p i n", i=3)
        yT = at(92, 16 * TOK).rearrange("p (k t) -> p k t", k=16)
        sB = at(132, NT * D).rearrange("p (t c) -> p t c", t=NT)
        rows = at(52, 8 * D).rearrange("p (v c) -> p v c", v=8)
        mT = at(92, KT * TOK).rearrange("p (k t) -> p k t", k=KT)
        mix = at(152, NT * D).rearrange("p (t c) -> p t c", t=NT)
        x1 = at(128, NT * D).rearrange("p (t c) -> p t c", t=NT)
        pos1 = at(112, 4 * D).rearrange("p (t c) -> p t c", t=4)
        h2 = mT.rearrange("p k t -> p (k t)").rearrange("p (t c) -> p t c", t=NT)
        h2T = at(0, KT * LAT).rearrange("p (k t) -> p k t", k=KT)
        h2Tc = at(16, KT * P).rearrange("p (k t) -> p k t", k=KT)
        keys = at(84, 16 * P).rearrange("p (i n) -> p i n", i=16)
        qTc = at(112, 16 * P).rearrange("p (i t) -> p i t", i=16)
        half_in = [at(20 + 4.5 * i, (KT + 1) * P).rearrange("p (k n) -> p k n", k=KT + 1) for i in range(2)]
        half_q = [at(30 + 2 * i, LAT) for i in range(2)]
        score = at(152, 4 * 16 * P).rearrange("p (t n) -> p t n", t=4)
        urow = [at(kb, D) for kb in (34, 38, 42, 46, 50, 54, 58, 148)]
        vrow = [at(kb, D) for kb in (84, 88, 92, 96, 100, 104, 108, 184)]
        h2c, pv, h2sq = at(68, D), at(16, D), at(20, D)
        steps = NT * PH * TOPK
        idx_tab = at(112, steps).bitcast(I32)
        d_tab, w_tab = at(114.5, steps), at(117, steps)
        sw, sw2 = (at(119.5 + i, 256).rearrange("p (h n) -> p h n", h=2) for i in range(2))
        cand, cand2 = at(121.5, 256), at(122.5, 256)
        eq = at(123.5, 512).rearrange("p (k n) -> p k n", n=TOPK)
        small = at(125.5, 12 * 32).rearrange("p (i n) -> p i n", i=12)
        v16, pick = small[:, 0], small[:, 1]
        i16, i16f = small[:, 2].bitcast(U32), small[:, 3]
        tv, tp = small[:, 4, 0:TOPK], small[:, 4, TOPK:].bitcast(U32)
        tij, tijf = small[:, 5].bitcast(U32), small[:, 6]
        dots, ge, ex = small[:, 7, 0:TOPK], small[:, 7, TOPK:], small[:, 8, 0:TOPK]
        esum, erec = small[:, 9, 0:1], small[:, 9, 1:2]
        pstat = small[:, 10, 0:4]
        idx_u = [small[:, 11, 16 * i:16 * i + 16].bitcast(I32) for i in range(2)]
        iota16 = shp[:, 6, 0:TOPK]
        idx_v = [at(127 + i / 16, TOPK).bitcast(I32) for i in range(2)]
        diag = at(62, 4 * P).rearrange("p (s n) -> p s n", s=4)

        S = {}

        def s(name):
            if name not in S:
                S[name] = sem(name)
            return S[name]

        NAMES = ("consts_in x_in pos_in w_free tm_full tm_free tr_full tr_free cond_ready ada_rows ada_done coef_ready "
                 "identb_ready x_ready ssq1 var1 std1 xn_ready wdt_in dt_full nega v_ready softp dA_ready cs_full "
                 "tmc_ready exps_ready tabs_ready ch_full ch_free conv_done silu_done cb_full cb_done h0_in "
                 "xd_ready st_full st_free cst_out dAg_ready e_full e_done m_done xc_ready yo_full y_full "
                 "y_free xD_ready d1_full d1_act d1_dve d2_full d2_free chm_in posm_in gt_used "
                 "ssqy vary stdy rstdy mg_done row_full row_free x1_in varm stdm ssqm x1_done ssqn varn stdn h2_ready "
                 "keys_in fq_full fq_out fs_full fs_out sc_full sc_free topk0_done topk_done h2c ge_done w_done diag_done u_used v_used pv_full pv_done pstd out_ready out_done idx_cp dve act waited")
        for nm in NAMES.split():
            s(nm)
        w_in = [sem("w_slot0_in"), sem("w_slot1_in")]
        u_in = [sem(f"u_slot{i}_in") for i in range(NSLOT)]
        half_w = [sem(f"half_head{i}_in") for i in range(2)]
        v_in = [sem(f"v_slot{i}_in") for i in range(NSLOT)]

        block = ctx.enter_context(nc.Block())

        win = a["w_in"].rearrange("(k p) n -> p k n", p=P)
        CONSTS = ["shp", "cond", "ada_b", "norms", "ssd_norm", "conv_w", "conv_b", "a_log", "dt_bias", "d_skip"]

        def wait_alone(eng, semaphore, value):
            eng.wait_ge(semaphore, value)
            if not isinstance(value, int):
                eng.sem_inc(s("waited"), 1)


        @block.sync
        def _(sp):
            for nm in ("cst_out", "out_done"):
                sp.nop().then_inc(s(nm), 16)
            for dst, name in ((shp, "shp"), (cond, "cond"), (adab, "ada_b"), (norms, "norms"), (ssdn, "ssd_norm"),
                              (convw, "conv_w"), (convb, "conv_b")):
                sp.dma_start(dst[:], a[name]).then_inc(s("consts_in"), 16)
            for i, name in enumerate(("a_log", "dt_bias", "d_skip")):
                sp.dma_start(hrow[:, i, :], a[name].partition_broadcast(P)).then_inc(s("consts_in"), 16)

            def load(n, src, cols, first=False, k=KT, off=0):
                if not first:
                    wait_alone(sp, s("w_free"), n - 1)
                dst = ring[n % 2 if isinstance(n, int) else load.slot]
                dst = dst.rearrange("p (k c) -> p k c", k=k)[:, :, off:off + cols]
                sp.dma_start(dst, src).then_inc(w_in[n % 2 if isinstance(n, int) else load.slot], 16)

            wada = a["w_ada"].rearrange("(k p) n -> p k n", p=P)
            load(0, wada[:, :, 0:512], 512, True)
            load(1, wada[:, :, 512:1024], 512, True)
            sp.dma_start(x0[:, 0, :], a["x"][0:P, :]).then_inc(s("x_in"), 16)
            sp.dma_start(x0[:, 1:, :], a["x"][P:, :].rearrange("(t p) c -> p t c", p=P)).then_inc(s("x_in"), 16)
            sp.dma_start(pos0, a["pos"].rearrange("(t p) c -> p t c", p=P)).then_inc(s("pos_in"), 16)
            sp.dma_start(wdt[:], win[:, :, COL_DT:COL_DT + 64]).then_inc(s("wdt_in"), 16)
            with sp.Fori(1, 6) as i:
                for load.slot in range(2):
                    load(i * 2 + load.slot, wada[:, :, ds(i * 1024 + 512 * load.slot, 512)], 512)
            def load_group(g):
                load.slot = 0
                load(g * 2 + JOB_XBC, win[:, :, ds(g * GC + COL_X, GC)], GC)
                load.slot = 1
                load(g * 2 + JOB_XBC + 1, win[:, :, ds(g * P + COL_B, P)], P)
                load(g * 2 + JOB_XBC + 1, win[:, :, ds(g * P + COL_C, P)], P, True, off=P)

            def group_states(g, next_weights):
                wait_alone(sp, s("y_full"), g * 10 + 1)
                wait_alone(sp, s("tr_free"), g * XB_UNITS + T_XB)
                sp.dma_start(H[:, 0, 0, :], a["state"][0, :, ds(g * GC, GC)]).then_inc(s("h0_in"), 16)
                sp.dma_start(H[:, 1, 3, :], a["state"][1, :, ds(g * GC, GC)]).then_inc(s("h0_in"), 16)
                next_weights()
                wait_alone(sp, s("st_free"), g * 8 + 5)
                for d in range(2):
                    sp.dma_start(st_out[d, :, ds(g * GC, GC)], cst[:, d, :]).then_inc(s("cst_out"), 16)

            def load_u():
                load(JOB_U, win[:, :, 0:512], 512)
                load(JOB_U + 1, win[:, :, 512:1024], 512)

            load_group(0)
            with sp.Fori(0, NG - 1) as g:
                group_states(g, lambda: load_group(g + 1))
            group_states(NG - 1, load_u)
            sp.wait_ge(s("y_free"), NG * NT + 1)
            sp.dma_start(chm, a["chm"]).then_inc(s("chm_in"), 16)
            for i, name in enumerate(("posc", "poss")):
                sp.dma_start(posm[:, i], a[name].rearrange("(k p) n -> p k n", p=P)).then_inc(s("posm_in"), 16)
            wf = a["w_fourier"].rearrange("(k p) n -> p k n", p=P)
            for j in range(2):
                load(JOB_FO + j, wf[:, :, 512 * j:512 * j + 512], 512)
            for j in range(2):
                load(JOB_GA + j, win[:, :, COL_GATE + 512 * j:COL_GATE + 512 * j + 512], 512)
            for j in range(4):
                load(JOB_Z + j, win[:, :, COL_Z + 512 * j:COL_Z + 512 * j + 512], 512)
            for j in range(2):
                load(JOB_GB + j, win[:, :, COL_GATE + D + 512 * j:COL_GATE + D + 512 * j + 512], 512)
            wso = a["w_ssd_out"].rearrange("(k p) n -> p k n", p=P)
            for j in range(4):
                load(JOB_SO + j, wso[:, :, 256 * j:256 * j + 256], 256, k=16)
            wo = a["w_out"].rearrange("(k p) n -> p k n", p=P)
            for j in range(2):
                load(JOB_WO + j, wo[:, :, 512 * j:512 * j + 512], 512)
            sp.wait_ge(s("tr_free"), T_NORM2)
            sp.dma_start(x1, a["x"].rearrange("(t p) c -> p t c", p=P)).then_inc(s("x1_in"), 16)
            sp.dma_start(pos1, a["pos"].rearrange("(t p) c -> p t c", p=P)).then_inc(s("x1_in"), 16)
            sp.wait_ge(s("h2_ready"), NT)
            sp.dma_start(keys, a["keys"]).then_inc(s("keys_in"), 16)
            wq = a["w_query"].rearrange("(k p) n -> p k n", p=P)
            for j in range(4):
                load(JOB_Q + j, wq[:, :, 512 * j:512 * j + 512], 512)

            def half_head(h, i):
                sp.dma_start(half_in[i][:, 0:KT, :], wq[:, :, ds(h * 256 + P * i, P)]).then_inc(half_w[i], 16)
                sp.dma_start(half_in[i][:, KT:, :], a["keys"][:, ds(h * 2 + i, 1), :]).then_inc(half_w[i], 16)

            sp.wait_ge(s("w_free"), JOB_Q + 4)
            for i in range(2):
                half_head(0, i)
            with sp.Fori(1, PH) as h:
                for i in range(2):
                    wait_alone(sp, s("fs_full"), h * 2 + i - 1)
                    half_head(h, i)
            yv = y_out.rearrange("(t p) c -> p t c", p=P)
            with sp.Fori(0, NT) as t:
                wait_alone(sp, s("out_ready"), t + 1)
                sp.dma_start(yv[:, ds(t, 1), :], pv.unsqueeze(1)).then_inc(s("out_done"), 16)
            sp.wait_ge(s("out_done"), 16 * NT + 16)
            sp.wait_ge(s("cst_out"), NG * 32 + 16)

        @block.tensor
        def _(pe):
            for nm in ("y_full", "v_used"):
                pe.nop().then_inc(s(nm), 1)
            mm = nc.tensor.matmul

            def need(n):
                pe.wait_ge(w_in[n % 2], loaded(n))

            pe.wait_ge(s("cond_ready"), 1)
            pe.wait_ge(s("consts_in"), 16 * len(CONSTS))

            def ada_rows(n, slot, first=False):
                pe.wait_ge(w_in[slot], (n - slot) * 8 + 16)
                if not first:
                    pe.wait_ge(s("ada_rows"), n - 1)
                w = ring[slot].rearrange("p (k c) -> p k c", k=KT)
                for k in range(KT):
                    last = mm(bank[slot][0:2, :], cond[:, k, :], w[:, k, :], start=(k == 0), stop=(k == KT - 1))
                last.then_inc(s("w_free"), 1)

            ada_rows(0, 0, True)
            ada_rows(1, 1, True)
            with pe.Fori(1, 6) as i:
                ada_rows(i * 2, 0)
                ada_rows(i * 2 + 1, 1)
            for m in range(48):
                if m % 4 == 0:
                    pe.wait_ge(s("ada_rows"), m // 4 + 1)
                last = nc.tensor.transpose(bank[7][:, 2 * m:2 * m + 2], adar[0:2, m * P:(m + 1) * P], ident[0:2, 0:2])
            last.then_inc(s("ada_done"), 1)

            def transpose_unit(u, blocks, bk=None):
                if not isinstance(u, int) or u >= 2:
                    pe.wait_ge(s("tr_free"), u - 1)
                b = bank[5 + (u % 2 if bk is None else bk)]
                for i, blk in enumerate(blocks):
                    last = nc.tensor.transpose(b[:, i * P:(i + 1) * P], blk, ident)
                last.then_inc(s("tr_full"), 1)

            for t in range(NT):
                pe.wait_ge(s("xn_ready"), t + 1)
                for h in range(2):
                    transpose_unit(T_NORM1 + 2 * t + h,
                                   [x0[:, t, (4 * h + i) * P:(4 * h + i + 1) * P] for i in range(4)])

            pe.wait_ge(s("tr_free"), T_XB)
            pe.wait_ge(s("wdt_in"), 16)
            pe.wait_ge(s("coef_ready"), 1)
            for t in range(NT):
                for k in range(KT):
                    last = mm(bank[7][:, 64 * t:64 * t + 64], hT[:, k, t * P:(t + 1) * P], wdt[:, k, :],
                              start=(k == 0), stop=(k == KT - 1))
            last.then_inc(s("dt_full"), 1)
            pe.wait_ge(s("dA_ready"), 1)
            b7 = bank[7][:, 0:320].rearrange("p (t h) -> p t h", t=NT)
            for d in range(2):
                mm(b7[:, :, 32 * d:32 * d + 32], tri[d], dA[:, :, 32 * d:32 * d + 32], start=True, stop=True)
            mm(bank[0][:, 0:320], ones, dA.rearrange("p t h -> p (t h)"), start=True, stop=True).then_inc(s("cs_full"), 1)

            pe.wait_ge(s("tabs_ready"), 1)
            pe.wait_ge(s("identb_ready"), 1)
            def xbc_tile(g, i):
                if i == 0:
                    pe.wait_ge(w_in[0], g * 16 + loaded(JOB_XBC))
                if i == 4:
                    pe.wait_ge(w_in[1], g * 32 + loaded(JOB_XBC + 1))
                if i or not isinstance(g, int):
                    pe.wait_ge(s("ch_free"), g * 6 + i)
                w = ring[i // 4].rearrange("p (k c) -> p k c", k=KT)
                c0 = (i % 4) * P
                for k in range(KT):
                    mm(bank[2][:, :], w[:, k, c0:c0 + P], hT[:, k, P:TOK], start=(k == 0), stop=(k == KT - 1))
                for k in range(KT):
                    last = mm(bank[3][:, 0:P], w[:, k, c0:c0 + P], hT[:, k, 0:P],
                              start=(k == 0), stop=(k == KT - 1))
                last.then_inc(s("ch_full"), 1)
                if i == 3 or i == 5:
                    pe.wait_ge(s("ch_full"), g * 6 + i + 1)
                    pe.nop().then_inc(s("w_free"), 1)

            def fourier_tile(q):
                j, t = divmod(q, NT)
                if t == 0:
                    need(JOB_U + j)
                if q == 0:
                    pe.wait_ge(s("ch_free"), NG * 6)
                if q >= 2:
                    pe.wait_ge(s("tm_free"), q - 1)
                w = ring[(JOB_U + j) % 2].rearrange("p (k c) -> p k c", k=KT)
                for k in range(KT):
                    last = mm(bank[2 + q % 2][:, :], hT[:, k, t * P:(t + 1) * P], w[:, k, :],
                              start=(k == 0), stop=(k == KT - 1))
                last.then_inc(s("tm_full"), 1)
                if t == NT - 1:
                    pe.wait_ge(s("tm_full"), q + 1)
                    pe.nop().then_inc(s("w_free"), 1)

            def scan_group(g, overlap):
                def beside(i):
                    xbc_tile(g + 1, i) if overlap else fourier_tile(i)

                pe.wait_ge(s("y_free"), g * NT + 1)
                pe.wait_ge(s("silu_done"), g * 6 + 4)
                for t in range(NT):
                    transpose_unit(g * XB_UNITS + T_XB + t, [xs[:, i, t * P:(t + 1) * P] for i in range(4)], t % 2)
                pe.wait_ge(s("silu_done"), g * 6 + 5)
                transpose_unit(g * XB_UNITS + T_XB + 5, [BT[:, t * P:(t + 1) * P] for t in range(4)], 1)
                transpose_unit(g * XB_UNITS + T_XB + 6, [BT[:, 4 * P:5 * P]], 0)
                pe.wait_ge(s("silu_done"), g * 6 + 6)
                for c in range(NT):
                    b = bank[4][:, c * P:(c + 1) * P] if c < 4 else bank[7][:, 0:P]
                    last = mm(b, BT[:, c * P:(c + 1) * P], CT[:, c * P:(c + 1) * P], start=True, stop=True)
                last.then_inc(s("cb_full"), 1)
                beside(0)
                pe.wait_ge(s("tr_free"), g * XB_UNITS + T_XB + 7)
                for k, (d, c) in enumerate(STATES):
                    if k == 4:
                        beside(1)
                    pe.wait_ge(s("xd_ready"), g * 8 + k + 1)
                    if k >= 2:
                        pe.wait_ge(s("st_free"), g * 8 + k - 1)
                    mm(bank[k % 2][:, :], Btok[:, c, :], xd[:, k, :], start=True, stop=True).then_inc(s("st_full"), 1)

                def decay_rows(u):
                    c, hq = divmod(u, 2)
                    for d in range(2):
                        e = 2 * u + d
                        if e >= 2:
                            pe.wait_ge(s("e_done"), g * 20 + e - 1)
                        b = bank[d]
                        mm(b[:, :], identb[:], maskb[:, d, :].unsqueeze(1).broadcast_to([P, 4, P]),
                           start=True, stop=False, skip_group_check=True)
                        for j in range(4):
                            last = mm(b[:, j * P:(j + 1) * P],
                                      dAg[:, c, d, 4 * hq + j:4 * hq + j + 1].broadcast_to([P, P]), tri[d],
                                      start=False, stop=(j == 3), skip_group_check=True)
                        last.then_inc(s("e_full"), 1)

                pe.wait_ge(s("st_free"), g * 8 + 8)
                pe.wait_ge(s("dAg_ready"), g + 1)
                pe.wait_ge(s("h0_in"), g * 32 + 32)
                decay_rows(0)
                for u in range(2 * NT):
                    c, hq = divmod(u, 2)
                    if u + 1 < 2 * NT:
                        decay_rows(u + 1)
                    if overlap and u in BESIDE:
                        beside(BESIDE[u])
                    if not overlap and u < 8:
                        beside(u + 2)
                    if c and not hq:
                        pe.wait_ge(s("cb_done"), g + 1)
                        pe.wait_ge(s("y_free"), g * NT + c + 1)
                        for d in range(2):
                            last = mm(bank[(4, 7)[d]][:, :], CT[:, c * P:(c + 1) * P], H[:, d, c - 1, :],
                                      start=True, stop=True)
                        last.then_inc(s("yo_full"), 1)
                    pe.wait_ge(s("m_done"), g * 20 + 2 * u + 2)
                    if not hq:
                        pe.wait_ge(s("xc_ready"), g * NT + c + 1)
                        if c >= 2:
                            pe.wait_ge(s("y_free"), g * NT + c)
                    for j in range(4):
                        r = 4 * hq + j
                        for d in range(2):
                            last = mm(bank[5 + c % 2][:, r * HD:(r + 1) * HD], Mm[:, 2 * (u % 2) + d, j, :],
                                      xc[:, c % 2, d, r * HD:(r + 1) * HD], start=(d == 0), stop=(d == 1))
                    last.then_inc(s("y_full"), 1)

            for i in range(6):
                xbc_tile(0, i)
            with pe.Fori(0, NG - 1) as g:
                scan_group(g, True)
            scan_group(NG - 1, False)

            def product_tile(q, lhs, k_tiles, w, cols=512):
                t = q % NT
                if q >= NT:
                    pe.wait_ge(s("tm_free"), q - 4)
                for k in range(k_tiles):
                    last = mm(bank[t][:, 0:cols], lhs[:, k, t * P:(t + 1) * P], w[:, k, :],
                              start=(k == 0), stop=(k == k_tiles - 1))
                last.then_inc(s("tm_full"), 1)

            def job(n, q, lhs, k_tiles=KT, cols=512):
                need(n)
                w = ring[n % 2].rearrange("p (k c) -> p k c", k=k_tiles)
                for t in range(NT):
                    product_tile(q + t, lhs, k_tiles, w, cols)
                pe.wait_ge(s("tm_full"), q + NT)
                pe.nop().then_inc(s("w_free"), 1)

            pe.wait_ge(s("y_free"), NG * NT + 1)
            pe.wait_ge(s("tm_free"), Q_U + 10)
            pe.wait_ge(s("posm_in"), 32)
            pe.wait_ge(s("chm_in"), 16)

            def over_positions(f):
                if f:
                    pe.wait_ge(s("d1_act"), f)
                    pe.wait_ge(s("d1_dve"), f)
                fs = slice(f % 4 * P, (f % 4 + 1) * P)
                half = Us[f // 4]
                for i in range(2):
                    for k in range(4):
                        mm(bank[5 + i][:, :], half[:, 1 + k, fs], posm[:, i, k, :], start=(k == 0), stop=(k == 3))
                for i in range(2):
                    last = mm(bank[(7, 4)[i]][:, 0:P], half[:, 0, fs], chm[:, i, :], start=True, stop=True)
                last.then_inc(s("d1_full"), 1)

            over_positions(0)
            for f in range(KT):
                if f + 1 < KT:
                    over_positions(f + 1)
                if f + 1 == KT:
                    pe.wait_ge(s("d1_act"), KT)
                    pe.wait_ge(s("d1_dve"), KT)
                if f >= 2:
                    pe.wait_ge(s("d2_free"), f - 1)
                for i in range(2):
                    m = chm[:, 2 * i, :]
                    mm(bank[f % 2][:, :], m, Pq[:, f % 2, i, P:TOK], start=(i == 0), stop=(i == 1))
                for i in range(2):
                    last = mm(bank[2 + f % 2][:, 0:P], chm[:, 2 * i, :], Pq[:, f % 2, i, 0:P],
                              start=(i == 0), stop=(i == 1))
                last.then_inc(s("d2_full"), 1)
            pe.wait_ge(s("d2_free"), KT)
            for j in range(2):
                job(JOB_FO + j, Q_FO + 5 * j, FT)
            for j in range(2):
                job(JOB_GA + j, Q_GA + 5 * j, hT)

            def turn_y(j):
                for t in range(NT):
                    pe.wait_ge(s("gt_used"), 10 + 5 * j + t + 1)
                    transpose_unit(T_Y + 5 * j + t, [Y[:, t, (4 * j + i) * P:(4 * j + i + 1) * P] for i in range(4)])

            for j in range(4):
                job(JOB_Z + j, Q_Z + 5 * j, hT)
                if j:
                    turn_y(j - 1)
            job(JOB_GB, Q_GB, hT)
            turn_y(3)
            job(JOB_GB + 1, Q_GB + 5, hT)

            pe.wait_ge(s("tr_free"), T_MERGE)
            for v in range(8):
                kind, who = divmod(v, 2)
                for h in range(2):
                    u = 2 * v + h
                    if u >= 1:
                        pe.wait_ge(s("row_free"), u)
                    for i in range(4):
                        k = 4 * h + i
                        col = (scl[:, 2, k, who:who + 1], scl[:, 1, k, who:who + 1],
                               mod[:, SH2 * 8 + k, who:who + 1], scl[:, 3, k, who:who + 1])[kind]
                        last = mm(bank[7][:, i * P:(i + 1) * P], col.broadcast_to([P, P]), ident, start=True, stop=True)
                    last.then_inc(s("row_full"), 1)

            for j in range(4):
                job(JOB_SO + j, Q_SO + 5 * j, yT, 16, 256)
            pe.wait_ge(s("mg_done"), 20)
            for t in range(NT):
                for h in range(2):
                    transpose_unit(T_MERGE + 2 * t + h,
                                   [a_out[:, t, (4 * h + i) * P:(4 * h + i + 1) * P] for i in range(4)])
            pe.wait_ge(s("tr_free"), T_NORM2)
            for j in range(2):
                job(JOB_WO + j, Q_WO + 5 * j, mT)

            def turn_h2(t):
                pe.wait_ge(s("h2_ready"), t + 1)
                for h in range(2):
                    transpose_unit(T_NORM2 + 2 * t + h,
                                   [h2[:, t, (4 * h + i) * P:(4 * h + i + 1) * P] for i in range(4)])

            turn_h2(0)
            pe.wait_ge(s("tr_free"), T_NORM2 + 2)
            pe.wait_ge(s("tm_free"), Q_WO + 10)
            for j in range(4):
                need(JOB_Q + j)
                w = ring[(JOB_Q + j) % 2].rearrange("p (k c) -> p k c", k=KT)
                if j >= 2:
                    pe.wait_ge(s("ch_free"), 6 * NG + j - 1)
                for i in range(4):
                    for k in range(KT):
                        last = mm(bank[j % 2][:, i * P:(i + 1) * P], w[:, k, i * P:(i + 1) * P], h2Tc[:, k, :],
                                  start=(k == 0), stop=(k == KT - 1))
                last.then_inc(s("ch_full"), 1)
                pe.wait_ge(s("ch_full"), 6 * NG + j + 1)
                pe.nop().then_inc(s("w_free"), 1)
            pe.wait_ge(s("keys_in"), 16)
            for q4 in range(4):
                pe.wait_ge(s("ch_free"), 6 * NG + q4 + 1)
                for i in range(4):
                    hi = 4 * q4 + i
                    last = mm(bank[(2, 3, 4, 7)[q4]][:, i * P:(i + 1) * P], qTc[:, hi, :], keys[:, hi, :],
                              start=True, stop=True)
                last.then_inc(s("sc_full"), 1)
            for t in range(1, NT):
                turn_h2(t)

            def latent_query(h, piece):
                i, k = divmod(piece, KT)
                if k == 0:
                    pe.wait_ge(half_w[i], h * 32 + 32)
                last = mm(bank[2 + i][:, :], half_in[i][:, k, :], h2T[:, k, :], start=(k == 0), stop=(k == KT - 1),
                          skip_group_check=True)
                if k == KT - 1:
                    last.then_inc(s("fq_full"), 1)

            def latent_scores(h):
                for i in range(2):
                    pe.wait_ge(s("fq_out"), h * 2 + i + 1)
                    pe.wait_ge(s("fs_out"), h * 2 + 1)
                    for t in range(4):
                        last = mm(bank[4 + i][:, t * P:(t + 1) * P], half_q[i][:, t * P:(t + 1) * P],
                                  half_in[i][:, KT, :], start=True, stop=True)
                    last.then_inc(s("fs_full"), 1)

            def zero_sums(t):
                pe.wait_ge(s("pv_done"), t + 1)
                for i in range(2):
                    mm(bank[i][:, :], zerob[:], maskb[:, 0, :].unsqueeze(1).broadcast_to([P, 4, P]),
                       start=True, stop=False, skip_group_check=True)

            def add_rows(t, h, queries=False):
                for m in range(TOPK):
                    pe.wait_ge(s("diag_done"), t * PH * TOPK + h * TOPK + m + 1)
                    pe.wait_ge(v_in[m % NSLOT], t * PH * 32 + h * 32 + 16 * (m // NSLOT + 1))
                    for i in range(2):
                        last = mm(bank[i][:, :], diag[:, m % 4, :], vrow[m % NSLOT][:, 512 * i:512 * i + 512],
                                  start=False, stop=False, skip_group_check=True)
                    last.then_inc(s("v_used"), 1)
                    if queries and m >= 2:
                        for piece in ([m - 2] if m < 14 else [2 * m - 16, 2 * m - 15]):
                            latent_query(h + 1, piece)

            pe.wait_ge(s("sc_free"), 4)
            pe.wait_ge(s("tr_free"), T_NORM2 + 10)
            zero_sums(0)
            for piece in range(2 * KT):
                latent_query(0, piece)
            latent_scores(0)
            with pe.Fori(0, PH - 1) as h:
                add_rows(0, h, True)
                latent_scores(h + 1)
            add_rows(0, PH - 1)
            with pe.Fori(1, NT) as t:
                zero_sums(t)
                with pe.Fori(0, PH) as h:
                    add_rows(t, h)

        @block.scalar
        def _(act):
            for nm in ("pv_done", "fs_out"):
                act.nop().then_inc(s(nm), 1)
            A = nc.scalar.activation
            ch = Chain(act, s("act"))
            act.wait_ge(s("consts_in"), 16 * len(CONSTS))
            A(cond[:], cond[:], ACT.Silu).then_inc(s("cond_ready"), 1)
            A(hrow[:, 0, :], hrow[:, 0, :], ACT.Exp).then_inc(s("nega"), 1)

            def take_ada(n):
                act.wait_ge(s("w_free"), n + 1)
                A(adar[0:2, 512 * n:512 * n + 512], bank[n % 2][0:2, :], ACT.Copy).then_inc(s("ada_rows"), 1)

            sq = hT.rearrange("p k t -> p (k t)")
            for t in range(NT):
                act.wait_ge(s("x_ready"), t) if t else act.wait_ge(s("x_in"), 32)
                A(sq[:, t * D:(t + 1) * D], x0[:, t, :], ACT.Square, accum_out=stat[:, t:t + 1]).then_inc(s("ssq1"), 1)
                take_ada(t)
            act.wait_ge(s("var1"), 1)
            A(stat[:, 0:NT], stat[:, 0:NT], ACT.Sqrt).then_inc(s("std1"), 1)
            for n in range(NT, 12):
                take_ada(n)
            act.wait_ge(s("v_ready"), 1)
            ch(A(tmp, tmp, ACT.Exp))
            A(tmp, tmp, ACT.Ln, bias=1.0).then_inc(s("softp"), 1)
            b7 = bank[7][:, 0:320].rearrange("p (t h) -> p t h", t=NT)
            b0 = bank[0][:, 0:320].rearrange("p (t h) -> p t h", t=NT)
            act.wait_ge(s("tmc_ready"), 1)
            A(ecs, b7, ACT.Exp).then_inc(s("exps_ready"), 1)
            A(ecd, b0, ACT.Exp).then_inc(s("exps_ready"), 1)
            A(tmp, tmp, ACT.Exp).then_inc(s("exps_ready"), 1)

            def into_cin(g, i):
                act.wait_ge(s("ch_full"), g * 6 + i + 1)
                if i >= 2:
                    act.wait_ge(s("conv_done"), g * 6 + i - 1)
                A(cin[:, i % 2, 2:130], bank[3][:, 0:P], ACT.Copy)
                A(cin[:, i % 2, 134:646], bank[2][:, :], ACT.Copy).then_inc(s("ch_free"), 1)

            def silu(g, i, first=False):
                act.wait_ge(s("conv_done"), g * 6 + i + 1)
                if i == 0 and not first:
                    act.wait_ge(s("tr_full"), g * XB_UNITS + T_XB)
                    act.wait_ge(s("cst_out"), g * 32 + 16)
                if i == 5 and not first:
                    act.wait_ge(s("yo_full"), g * 4)
                dst = xs[:, i, :] if i < 4 else (BT, CT)[i - 4]
                A(dst[:, 0:P], acc[:, i % 2, 0:P], ACT.Silu)
                A(dst[:, P:TOK], acc[:, i % 2, 132:644], ACT.Silu).then_inc(s("silu_done"), 1)

            def take(q, dst, func, cols=512, **kw):
                act.wait_ge(s("tm_full"), q + 1)
                A(dst, bank[q % NT][:, 0:cols], func, **kw).then_inc(s("tm_free"), 1)

            def take_fourier(q):
                j, t = divmod(q, NT)
                act.wait_ge(s("tm_full"), q + 1)
                if q == 1:
                    act.wait_ge(s("cst_out"), NG * 32 + 16)
                A(Us[j][:, t, :], bank[2 + q % 2][:, :], ACT.Copy).then_inc(s("tm_free"), 1)

            def scan_exps(g, overlap):
                act.wait_ge(s("cb_full"), g + 1)
                A(cbT[:, 0:4, :], bank[4][:, :].rearrange("p (t c) -> p t c", t=4), ACT.Copy)
                A(cbT[:, 4, :], bank[7][:, 0:P], ACT.Copy).then_inc(s("cb_done"), 1)
                if overlap:
                    into_cin(g + 1, 0)
                    into_cin(g + 1, 1)
                else:
                    take_fourier(0)
                for e in range(20):
                    u, d = divmod(e, 2)
                    c, hq = divmod(u, 2)
                    act.wait_ge(s("e_full"), g * 20 + e + 1)
                    if e >= 2:
                        act.wait_ge(s("m_done"), g * 20 + e - 1)
                    for j in range(4):
                        last = A(Ee[:, e % 2, j, :], bank[d][:, j * P:(j + 1) * P], ACT.Exp,
                                 bias=ncs[:, c, ds(g * HG + 32 * d + 4 * hq + j, 1)])
                    last.then_inc(s("e_done"), 1)
                    if overlap and d:
                        if u in COPY_AT:
                            into_cin(g + 1, COPY_AT[u])
                        if u in SILU_AT:
                            silu(g + 1, SILU_AT[u])
                    if not overlap and d and u < 9:
                        take_fourier(u + 1)

            for i in range(6):
                into_cin(0, i)
                if i:
                    silu(0, i - 1, True)
            silu(0, 5, True)
            with act.Fori(0, NG - 1) as g:
                scan_exps(g, True)
            scan_exps(NG - 1, False)

            for f in range(KT):
                act.wait_ge(s("d1_full"), f + 1)
                if f >= 2:
                    act.wait_ge(s("d2_full"), f - 1)
                A(Pq[:, f % 2, 0, 0:P], bank[7][:, 0:P], ACT.Copy)
                A(Pq[:, f % 2, 0, P:TOK], bank[5][:, :], ACT.Copy).then_inc(s("d1_act"), 1)
            for q in range(Q_FO, Q_FO + 10):
                j, t = divmod(q - Q_FO, NT)
                take(q, a_out[:, t, 512 * j:512 * j + 512], ACT.Copy)
            for n, q in enumerate(range(Q_GA, Q_GA + 10)):
                if n >= 4:
                    act.wait_ge(s("gt_used"), n - 3)
                take(q, gt[:, n % 4, :], ACT.Sigmoid)
            for n, q in enumerate(range(Q_Z, Q_Z + 20)):
                j, t = divmod(n, NT)
                act.wait_ge(s("gt_used"), 10 + n - 3)
                take(q, gt[:, (10 + n) % 4, :], ACT.Silu)
            act.wait_ge(s("gt_used"), 30)
            for t in range(NT):
                for j in range(4):
                    if t:
                        act.wait_ge(s("ssqy"), 4 * t + j - 3)
                    A(gt[:, j, :], Y[:, t, 512 * j:512 * j + 512], ACT.Square,
                      accum_out=stat[:, 10 + 4 * t + j:11 + 4 * t + j]).then_inc(s("ssqy"), 1)
            for q in range(Q_GB, Q_GB + 10):
                j, t = divmod(q - Q_GB, NT)
                take(q, sB[:, t, 512 * j:512 * j + 512], ACT.Sigmoid)
            act.wait_ge(s("vary"), 1)
            A(stat[:, 30:35], stat[:, 30:35], ACT.Sqrt).then_inc(s("stdy"), 1)
            act.wait_ge(s("rstdy"), 1)
            act.wait_ge(s("ssqy"), 20)
            for n, q in enumerate(range(Q_SO, Q_SO + 20)):
                j, t = divmod(n, NT)
                if n >= 4:
                    act.wait_ge(s("mg_done"), n - 3)
                take(q, gt[:, n % 4, 0:256], ACT.Copy, 256, scale=stat[:, 30 + t:31 + t])
            for n, q in enumerate(range(Q_WO, Q_WO + 10)):
                j, t = divmod(n, NT)
                act.wait_ge(s("tm_full"), q + 1)
                if n == 0:
                    act.wait_ge(s("mg_done"), 20)
                    act.wait_ge(s("tm_free"), Q_WO)
                if n >= 4:
                    act.wait_ge(s("ssqm"), n - 3)
                A(gt[:, n % 4, :], bank[q % NT][:, :], ACT.Square,
                  accum_out=stat[:, 36 + 2 * t + j:37 + 2 * t + j]).then_inc(s("ssqm"), 1)
                take(q, mix[:, t, 512 * j:512 * j + 512], ACT.Copy)
            act.wait_ge(s("varm"), 1)
            A(stat[:, 46:51], stat[:, 46:51], ACT.Sqrt).then_inc(s("stdm"), 1)
            for t in range(NT):
                act.wait_ge(s("x1_done"), t + 1)
                A(mix[:, t, :], x1[:, t, :], ACT.Square, accum_out=stat[:, 51 + t:52 + t]).then_inc(s("ssqn"), 1)
            act.wait_ge(s("varn"), 1)
            A(stat[:, 51:56], stat[:, 51:56], ACT.Sqrt).then_inc(s("stdn"), 1)

            for j in range(4):
                act.wait_ge(s("ch_full"), 6 * NG + j + 1)
                if j == 0:
                    act.wait_ge(s("h2_ready"), NT)
                    act.wait_ge(s("tr_full"), T_NORM2 + 2)
                A(qTc[:, 4 * j:4 * j + 4, :], bank[j % 2][:, :].rearrange("p (i t) -> p i t", i=4),
                  ACT.Copy).then_inc(s("ch_free"), 1)
            for u in range(4):
                act.wait_ge(s("sc_full"), u + 1)
                A(score[:, 3, 512 * u:512 * u + 512], bank[(2, 3, 4, 7)[u]][:, :], ACT.Copy).then_inc(s("sc_free"), 1)

            def take_queries(h):
                for i in range(2):
                    act.wait_ge(s("fq_full"), h * 2 + i + 1)
                    A(half_q[i], bank[2 + i][:, :], ACT.Copy).then_inc(s("fq_out"), 1)

            def take_scores(h):
                act.wait_ge(s("topk0_done"), h + 1)
                for i in range(2):
                    act.wait_ge(s("fs_full"), h * 2 + i + 1)
                    A(score[:, :, ds(h * 256 + P * i, P)], bank[4 + i][:, :].rearrange("p (t n) -> p t n", t=4),
                      ACT.Copy).then_inc(s("fs_out"), 1)

            def gates(t, h):
                n = t * PH * TOPK + h * TOPK
                act.wait_ge(s("u_used"), n + TOPK + 1)
                A(ex, d_tab[:, ds(n, TOPK)], ACT.Exp, accum_out=esum)
                A(ge, dots, ACT.Gelu_apprx_tanh).then_inc(s("ge_done"), 1)

            def spread(t, h):
                n = t * PH * TOPK + h * TOPK
                act.wait_ge(s("w_done"), t * PH + h + 1)
                for m in range(TOPK):
                    act.wait_ge(s("v_used"), n + (m - 2)) if m >= 4 else act.wait_ge(s("v_used"), n + 1)
                    A(diag[:, m % 4, :], ident, ACT.Copy, scale=w_tab[:, ds(n + m, 1)]).then_inc(s("diag_done"), 1)

            def tile_sum(t):
                act.wait_ge(s("v_used"), t * PH * TOPK + PH * TOPK + 1)
                act.wait_ge(s("out_done"), t * 16 + 16)
                for i in range(2):
                    last = A(pv[:, 512 * i:512 * i + 512], bank[i][:, :], ACT.Copy)
                last.then_inc(s("pv_full"), 1)
                act.wait_ge(s("pv_full"), t + 1)
                ch(A(h2sq, pv, ACT.Square, accum_out=pstat[:, 0:1]))
                A(pstat[:, 1:2], pstat[:, 0:1], ACT.Sqrt, bias=eps[:], scale=1.0 / D).then_inc(s("pv_done"), 1)

            act.wait_ge(s("w_free"), JOB_Q + 4)
            take_queries(0)
            take_scores(0)
            gates(0, 0)
            with act.Fori(0, PH - 1) as h:
                spread(0, h)
                gates(0, h + 1)
                take_queries(h + 1)
                take_scores(h + 1)
            spread(0, PH - 1)
            tile_sum(0)
            with ch.loop(NT - 1, 1) as i:
                with act.Fori(0, PH) as h:
                    gates(i + 1, h)
                    spread(i + 1, h)
                tile_sum(i + 1)

        @block.gpsimd
        def _(pool):
            TT = nc.gpsimd.tensor_tensor
            with pool.Fori(0, NG) as g:
                x8 = [xtok[:, c, :].rearrange("p (r w) -> p r w", r=HG) for c in range(NT)]
                pool.wait_ge(s("tabs_ready"), 1)
                pool.wait_ge(s("tr_free"), g * XB_UNITS + T_XB + 5)
                pool.wait_ge(s("y_full"), g * 10 + 1)
                for k, (d, c) in enumerate(STATES):
                    TT(xd[:, k, :].rearrange("p (r w) -> p r w", r=HG), x8[c],
                       dtd[:, c, ds(g * HG + 32 * d, HG)].unsqueeze(2).broadcast_to([P, HG, HD]),
                       ALU.mult).then_inc(s("xd_ready"), 1)
                for c in range(NT):
                    wait_alone(pool, s("y_free"), g * NT + c + 1)
                    TT(xD.rearrange("p (r w) -> p r w", r=HG), x8[c],
                       dsum[:, ds(g * HG, HG)].unsqueeze(2).broadcast_to([P, HG, HD]),
                       ALU.mult).then_inc(s("xD_ready"), 1)

            nc.gpsimd.memset(eps[:], EPS)

            def rows_of(kind, m, step):
                slots, ins, used, table, idx = ((urow, u_in, "u_used", a["peer_u"], idx_u),
                                                (vrow, v_in, "v_used", a["peer_v"], idx_v))[kind]
                if isinstance(step, int) and step == 0 and m < NSLOT:
                    pass
                else:
                    wait_alone(pool, s(used), step * TOPK + (m - NSLOT + 2))
                nc.gpsimd.indirect_dma_start(
                    slots[m % NSLOT], None, table,
                    bass.IndirectOffsetOnAxis(ap=idx[rows_of.parity][:, m:m + 1], axis=0)).then_inc(ins[m % NSLOT], 16)

            pch = Chain(pool, s("idx_cp"))
            pool.wait_ge(s("h2_ready"), NT)
            pool.wait_ge(s("sc_free"), 4)
            pool.wait_ge(s("topk0_done"), 1)
            pch(nc.gpsimd.tensor_copy(idx_u[0], idx_tab[:, 0:TOPK]))
            rows_of.parity = 0
            for m in range(TOPK):
                rows_of(0, m, 0)

            def both(step, parity, nxt, first_tile=False):
                if first_tile:
                    pool.wait_ge(s("topk0_done"), nxt + 1)
                else:
                    pool.wait_ge(s("topk_done"), nxt - PH + 1)
                pool.wait_ge(s("u_used"), step * TOPK + 1)
                pool.wait_ge(s("v_used"), step * TOPK - TOPK + 1) if not isinstance(step, int) else None
                nc.gpsimd.tensor_copy(idx_u[1 - parity], idx_tab[:, ds(nxt * TOPK, TOPK)])
                pch(nc.gpsimd.tensor_copy(idx_v[parity], idx_tab[:, ds(step * TOPK, TOPK)]))
                for m in range(TOPK):
                    rows_of.parity = 1 - parity
                    rows_of(0, m, nxt)
                    rows_of.parity = parity
                    rows_of(1, m, step)

            pool.wait_ge(s("tr_free"), T_NORM2 + 10)
            both(0, 0, 1, True)
            with pch.loop((PH - 2) // 2, 2) as i:
                both(i * 2 + 1, 1, i * 2 + 2, True)
                both(i * 2 + 2, 0, i * 2 + 3, True)
            with pch.loop((NS - PH) // 2, 2) as i:
                both(i * 2 + (PH - 1), 1, i * 2 + PH)
                both(i * 2 + PH, 0, i * 2 + (PH + 1))
            pool.wait_ge(s("v_used"), (NS - 2) * TOPK + 1)
            pch(nc.gpsimd.tensor_copy(idx_v[1], idx_tab[:, (NS - 1) * TOPK:]))
            rows_of.parity = 1
            for m in range(TOPK):
                rows_of(1, m, NS - 1)

        @block.vector
        def _(dve):
            for nm in ("y_free", "u_used"):
                dve.nop().then_inc(s(nm), 1)
            V = nc.vector
            TT, TS, STT, CP = V.tensor_tensor, V.tensor_scalar, V.scalar_tensor_tensor, V.tensor_copy
            ch = Chain(dve, s("dve"))

            def rstd(cols, n, std_sem, var_sem):
                TS(cols, cols, 1.0 / n, EPS, ALU.mult, ALU.add).then_inc(s(var_sem), 1)
                dve.wait_ge(s(std_sem), 1)

            dve.wait_ge(s("consts_in"), 16 * len(CONSTS))
            CP(identb[:], ident)
            V.memset(zerob[:], 0.0)
            CP(maskb[:], shp[:, 4:6, :]).then_inc(s("identb_ready"), 1)
            TT(dsum[:], hrow[:, 2, 0:HEADS], hrow[:, 2, HEADS:], ALU.add)
            dve.wait_ge(s("x_in"), 32)
            dve.wait_ge(s("pos_in"), 16)
            for t in range(1, NT):
                TT(x0[:, t, :], x0[:, t, :], pos0[:, t - 1, :], ALU.add).then_inc(s("x_ready"), 1)
            dve.wait_ge(s("ssq1"), NT)
            rstd(stat[:, 0:NT], D, "std1", "var1")
            ch(V.reciprocal(stat[:, 0:NT], stat[:, 0:NT]))
            dve.wait_ge(s("x_ready"), NT - 1)
            for t in range(NT):
                TS(x0[:, t, :], x0[:, t, :], stat[:, t:t + 1], None, ALU.mult).then_inc(s("xn_ready"), 1)
            dve.wait_ge(s("ada_done"), 1)
            ch(TT(mod[:], bank[7][:, 0:96].rearrange("p (m c) -> p m c", c=2),
                  adab[:].unsqueeze(2).broadcast_to([P, 48, 2]), ALU.add))
            for i, (m, n) in enumerate(((SC1, 0), (SC2, 2))):
                STT(scl[:, i], mod[:, m * 8:m * 8 + 8, :], 1.0, norms[:, n, :].unsqueeze(2).broadcast_to([P, KT, 2]),
                    ALU.add, ALU.mult)
            for i, (m, n) in enumerate(((GA1, 1), (GA2, 3))):
                last = TT(scl[:, 2 + i], mod[:, m * 8:m * 8 + 8, :], norms[:, n, :].unsqueeze(2).broadcast_to([P, KT, 2]),
                          ALU.mult)
            last.then_inc(s("coef_ready"), 1)
            dve.wait_ge(s("coef_ready"), 1)
            for t in range(NT):
                who = 1 if t else 0
                for h in range(2):
                    u = T_NORM1 + 2 * t + h
                    dve.wait_ge(s("tr_full"), u + 1)
                    for i in range(4):
                        k = 4 * h + i
                        last = TS(hT[:, k, t * P:(t + 1) * P], bank[5 + u % 2][:, i * P:(i + 1) * P],
                                  scl[:, 0, k, who:who + 1], mod[:, SH1 * 8 + k, who:who + 1], ALU.mult, ALU.add)
                    last.then_inc(s("tr_free"), 1)
            dve.wait_ge(s("dt_full"), 1)
            dve.wait_ge(s("nega"), 1)
            v = dtd
            b7 = bank[7][:, 0:320].rearrange("p (t h) -> p t h", t=NT)
            b0 = bank[0][:, 0:320].rearrange("p (t h) -> p t h", t=NT)
            all5 = lambda r: r.unsqueeze(1).broadcast_to([P, NT, 64])
            ch(TT(v, b7, all5(hrow[:, 1, :]), ALU.add))
            STT(tmp, v, -1.0, v, ALU.mult, ALU.min).then_inc(s("v_ready"), 1)
            TS(dt_, v, 0.0, None, ALU.max)
            ch(TS(hrow[:, 0, :], hrow[:, 0, :], -1.0, None, ALU.mult))
            dve.wait_ge(s("softp"), 1)
            ch(TT(dt_, dt_, tmp, ALU.add))
            TT(dA, dt_, all5(hrow[:, 0, :]), ALU.mult).then_inc(s("dA_ready"), 1)
            dve.wait_ge(s("cs_full"), 1)
            ch(TS(ncs, b7, -1.0, None, ALU.mult))
            TT(tmp, b0, ncs, ALU.add).then_inc(s("tmc_ready"), 1)
            dve.wait_ge(s("exps_ready"), 3)
            TT(dtd, dt_, tmp, ALU.mult).then_inc(s("tabs_ready"), 1)
            for lo, hi in ((0, 2), (130, 134), (646, 648)):
                last = V.memset(cin[:, :, lo:hi], 0.0)
            ch(last)
            dve.wait_ge(s("tabs_ready"), 1)

            def convolve(g, i):
                tile = g * 4 + i if i < 4 else g + (16 if i == 4 else 20)
                dve.wait_ge(s("ch_free"), g * 6 + i + 1)
                if i >= 2:
                    dve.wait_ge(s("silu_done"), g * 6 + i - 1)
                o = acc[:, i % 2, 0:644]
                w = lambda k: convw[:, ds(tile, 1), k]
                ch(TS(o, cin[:, i % 2, 0:644], w(0), convb[:, ds(tile, 1)], ALU.mult, ALU.add))
                for k in range(1, TAPS):
                    last = STT(o, cin[:, i % 2, k:k + 644], w(k), o, ALU.mult, ALU.add)
                    if k < TAPS - 1:
                        ch(last)
                last.then_inc(s("conv_done"), 1)

            def scan_group(g, overlap):
                CP(dAg[:, :, 0, :], dA[:, :, ds(g * HG, HG)])
                CP(dAg[:, :, 1, :], dA[:, :, ds(g * HG + 32, HG)]).then_inc(s("dAg_ready"), 1)
                for t in range(NT):
                    dve.wait_ge(s("tr_full"), g * XB_UNITS + T_XB + t + 1)
                    CP(xtok[:, t, :], bank[5 + t % 2][:, :]).then_inc(s("tr_free"), 1)
                dve.wait_ge(s("tr_full"), g * XB_UNITS + T_XB + 6)
                CP(Btok[:, 0:4, :], bank[6][:, :].rearrange("p (t c) -> p t c", t=4)).then_inc(s("tr_free"), 1)
                dve.wait_ge(s("tr_full"), g * XB_UNITS + T_XB + 7)
                CP(Btok[:, 4, :], bank[5][:, 0:P]).then_inc(s("tr_free"), 1)
                r8 = lambda ap: ap.rearrange("p (r w) -> p r w", r=HG)
                per_head = lambda table, c, d: table[:, c, ds(g * HG + 32 * d, HG)].unsqueeze(2).broadcast_to([P, HG, HD])
                dve.wait_ge(s("h0_in"), g * 32 + 32)
                dve.wait_ge(s("tr_free"), g * XB_UNITS + T_XB + 7)
                for k, (d, c) in enumerate(STATES):
                    if c:
                        here, there = H[:, d, c - 1, :], H[:, d, c - 2 if d else c, :]
                        if k in (1, 2, 6, 7):
                            dve.wait_ge(s("st_free"), g * 8 + k)
                        ch(TT(r8(there), r8(here), per_head(ecd, c, d), ALU.mult))
                        dve.wait_ge(s("st_full"), g * 8 + k + 1)
                        TT(there, there, bank[k % 2][:, :], ALU.add).then_inc(s("st_free"), 1)
                    else:
                        dve.wait_ge(s("st_full"), g * 8 + k + 1)
                        CP(cst[:, d, :], bank[k % 2][:, :]).then_inc(s("st_free"), 1)
                    if k == 3 and overlap:
                        convolve(g + 1, 0)
                if overlap:
                    convolve(g + 1, 1)

                def scaled_x(c):
                    if c >= 2:
                        dve.wait_ge(s("y_full"), g * 10 + 2 * c - 1)
                    for d in range(2):
                        last = TT(r8(xc[:, c % 2, d, :]), r8(xtok[:, c, :]), per_head(dt_, c, d), ALU.mult)
                    last.then_inc(s("xc_ready"), 1)

                def chunk_out(c):
                    yc = Y[:, c, ds(g * GC, GC)]
                    dve.wait_ge(s("y_full"), g * 10 + 2 * c + 3)
                    dve.wait_ge(s("xD_ready"), g * NT + c + 1)
                    if c:
                        dve.wait_ge(s("yo_full"), g * 4 + c)
                        TT(r8(yc), r8(bank[4][:, :]), per_head(ecs, c, 0), ALU.mult)
                        ch(TT(r8(yt), r8(bank[7][:, :]), per_head(ecs, c, 1), ALU.mult))
                        ch(TT(yt, yt, xD, ALU.add))
                        ch(TT(yc, yc, yt, ALU.add))
                    else:
                        ch(CP(yc, xD))
                    TT(yc, yc, bank[5 + c % 2][:, :], ALU.add).then_inc(s("y_free"), 1)

                dve.wait_ge(s("cb_done"), g + 1)
                scaled_x(0)
                for u in range(2 * NT):
                    c, hq = divmod(u, 2)
                    for d in range(2):
                        e = 2 * u + d
                        dve.wait_ge(s("e_done"), g * 20 + e + 1)
                        if u >= 2:
                            dve.wait_ge(s("y_full"), g * 10 + u)
                        TT(Mm[:, 2 * (u % 2) + d], Ee[:, e % 2], cbT[:, c, :].unsqueeze(1).broadcast_to([P, 4, P]),
                           ALU.mult).then_inc(s("m_done"), 1)
                    if not hq:
                        if c:
                            chunk_out(c - 1)
                        if c + 1 < NT:
                            scaled_x(c + 1)
                    if overlap and u in CONV_AT:
                        convolve(g + 1, CONV_AT[u])
                chunk_out(NT - 1)

            for i in range(6):
                convolve(0, i)
            with ch.loop(NG - 1, 6 * 4 + 6 + 4 * 3 + 1) as g:
                scan_group(g, True)
            scan_group(NG - 1, False)

            for f in range(KT):
                dve.wait_ge(s("d1_full"), f + 1)
                if f >= 2:
                    dve.wait_ge(s("d2_full"), f - 1)
                CP(Pq[:, f % 2, 1, 0:P], bank[4][:, 0:P])
                CP(Pq[:, f % 2, 1, P:TOK], bank[6][:, :]).then_inc(s("d1_dve"), 1)
                if f:
                    dve.wait_ge(s("d2_full"), f)
                    CP(FT[:, f - 1, 0:P], bank[2 + (f - 1) % 2][:, 0:P])
                    CP(FT[:, f - 1, P:TOK], bank[(f - 1) % 2][:, :]).then_inc(s("d2_free"), 1)
            dve.wait_ge(s("d2_full"), KT)
            CP(FT[:, KT - 1, 0:P], bank[2 + (KT - 1) % 2][:, 0:P])
            CP(FT[:, KT - 1, P:TOK], bank[(KT - 1) % 2][:, :]).then_inc(s("d2_free"), 1)
            for n in range(10):
                j, t = divmod(n, NT)
                dve.wait_ge(s("tm_free"), Q_GA + n + 1)
                ao = a_out[:, t, 512 * j:512 * j + 512]
                TT(ao, ao, gt[:, n % 4, :], ALU.mult).then_inc(s("gt_used"), 1)

            def turned_y(j):
                for t in range(NT):
                    u = T_Y + 5 * j + t
                    dve.wait_ge(s("tr_full"), u + 1)
                    for i in range(4):
                        last = TS(yT[:, 4 * j + i, t * P:(t + 1) * P], bank[5 + u % 2][:, i * P:(i + 1) * P],
                                  ssdn[:, 4 * j + i:4 * j + i + 1], None, ALU.mult)
                    last.then_inc(s("tr_free"), 1)

            for j in range(4):
                for t in range(NT):
                    n = 5 * j + t
                    dve.wait_ge(s("tm_free"), Q_Z + n + 1)
                    yy = Y[:, t, 512 * j:512 * j + 512]
                    TT(yy, yy, gt[:, (10 + n) % 4, :], ALU.mult).then_inc(s("gt_used"), 1)
                if j:
                    turned_y(j - 1)
            turned_y(3)
            dve.wait_ge(s("ssqy"), 20)
            ch(V.tensor_reduce(stat[:, 30:35], stat[:, 10:30].rearrange("p (t j) -> p t j", j=4), AX.X, ALU.add))
            rstd(stat[:, 30:35], DI, "stdy", "vary")
            V.reciprocal(stat[:, 30:35], stat[:, 30:35]).then_inc(s("rstdy"), 1)
            for u in range(16):
                v_, h = divmod(u, 2)
                dve.wait_ge(s("row_full"), u + 1)
                CP(rows[:, v_, 512 * h:512 * h + 512], bank[7][:, :]).then_inc(s("row_free"), 1)
            for n in range(20):
                j, t = divmod(n, NT)
                dve.wait_ge(s("tm_free"), Q_SO + n + 1)
                o = slice(256 * j, 256 * j + 256)
                g_ = gt[:, n % 4, 0:256]
                ch(TT(g_, g_, sB[:, t, o], ALU.mult))
                TT(a_out[:, t, o], a_out[:, t, o], g_, ALU.add).then_inc(s("mg_done"), 1)
            for u in range(10):
                t, h = divmod(u, 2)
                dve.wait_ge(s("tr_full"), T_MERGE + u + 1)
                CP(mT[:, 4 * h:4 * h + 4, t * P:(t + 1) * P],
                   bank[5 + (T_MERGE + u) % 2][:, :].rearrange("p (k t) -> p k t", k=4)).then_inc(s("tr_free"), 1)
            dve.wait_ge(s("x1_in"), 32)
            for t in range(1, NT):
                last = TT(x1[:, t, :], x1[:, t, :], pos1[:, t - 1, :], ALU.add)
            ch(last)
            dve.wait_ge(s("ssqm"), 10)
            dve.wait_ge(s("tm_free"), Q_WO + 10)
            ch(TT(stat[:, 46:51], stat[:, 36:46].rearrange("p (t j) -> p t j", j=2)[:, :, 0],
                  stat[:, 36:46].rearrange("p (t j) -> p t j", j=2)[:, :, 1], ALU.add))
            rstd(stat[:, 46:51], D, "stdm", "varm")
            ch(V.reciprocal(stat[:, 46:51], stat[:, 46:51]))
            dve.wait_ge(s("row_free"), 16)
            for t in range(NT):
                who = 1 if t else 0
                ch(STT(mix[:, t, :], mix[:, t, :], stat[:, 46 + t:47 + t], rows[:, who, :], ALU.mult, ALU.mult))
                TT(x1[:, t, :], x1[:, t, :], mix[:, t, :], ALU.add).then_inc(s("x1_done"), 1)
            dve.wait_ge(s("ssqn"), NT)
            rstd(stat[:, 51:56], D, "stdn", "varn")
            ch(V.reciprocal(stat[:, 51:56], stat[:, 51:56]))
            for t in range(NT):
                who = 1 if t else 0
                ch(STT(h2[:, t, :], x1[:, t, :], stat[:, 51 + t:52 + t], rows[:, 2 + who, :], ALU.mult, ALU.mult))
                TT(h2[:, t, :], h2[:, t, :], rows[:, 4 + who, :], ALU.add).then_inc(s("h2_ready"), 1)

            def turned_h2(t):
                for h in range(2):
                    u = T_NORM2 + 2 * t + h
                    dve.wait_ge(s("tr_full"), u + 1)
                    dst = h2T[:, 4 * h:4 * h + 4, (t - 1) * P:t * P] if t else h2Tc[:, 4 * h:4 * h + 4, :]
                    CP(dst, bank[5 + u % 2][:, :].rearrange("p (k t) -> p k t", k=4)).then_inc(s("tr_free"), 1)

            turned_h2(0)
            ch(CP(h2c, h2[:, 0, :]))

            def best16(vals, idx, src, src2):
                ch(V.max(vals[:, 0:8], src), wait_alone)
                V.max_index(idx[:, 0:8], vals[:, 0:8], src)
                ch(V.match_replace(src2, vals[:, 0:8], src, LOWEST), wait_alone)
                ch(V.max(vals[:, 8:16], src2), wait_alone)
                ch(V.max_index(idx[:, 8:16], vals[:, 8:16], src2), wait_alone)

            def top(slot, n, h, done="topk_done"):
                ch(CP(sw, score[:, slot:slot + 1, ds(h * 256, 256)].rearrange("p t (h n) -> p (t h) n", h=2)
                      if isinstance(slot, int) else score[:, ds(slot, 1), ds(h * 256, 256)].rearrange("p t (h n) -> p (t h) n", h=2)), wait_alone)
                for half in range(2):
                    best16(v16[:, 16 * half:16 * half + 16], i16[:, 16 * half:16 * half + 16],
                           sw[:, half, :], sw2[:, half, :])
                CP(i16f, i16)
                ch(TT(cand.rearrange("p (a b) -> p a b", a=TOPK),
                      v16[:, 0:16].unsqueeze(2).broadcast_to([P, 16, 16]),
                      v16[:, 16:32].unsqueeze(1).broadcast_to([P, 16, 16]), ALU.add), wait_alone)
                best16(tv, tp, cand, cand2)
                TS(d_tab[:, ds(n, TOPK)], tv, tv[:, 0:1], None, ALU.subtract)
                TS(tij[:, 0:16], tp, 4, None, ALU.logical_shift_right)
                ch(TS(tij[:, 16:32], tp, 15, None, ALU.bitwise_and))
                ch(CP(tijf, tij))
                ch(TT(eq, iota16.unsqueeze(1).broadcast_to([P, 32, 16]), tijf.unsqueeze(2).broadcast_to([P, 32, 16]),
                      ALU.is_equal))
                e4 = eq.rearrange("p (h k) n -> p h k n", h=2)
                ch(TT(e4, e4, i16f.rearrange("p (h n) -> p h n", h=2).unsqueeze(2).broadcast_to([P, 2, 16, 16]),
                      ALU.mult))
                ch(V.tensor_reduce(pick, eq, AX.X, ALU.add))
                STT(idx_tab[:, ds(n, TOPK)], pick[:, 0:16], float(NKEY), pick[:, 16:32],
                    ALU.mult, ALU.add).then_inc(s(done), 1)

            TOP = 1 + 8 + 1 + 4 + 1 + 1 + 1 + 1 + 1

            def step(t, h, tops):
                n = t * PH + h
                for m in range(TOPK):
                    dve.wait_ge(u_in[m % NSLOT], n * 32 + 16 * (m // NSLOT + 1))
                    V.tensor_tensor_reduce(out=urow[m % NSLOT], in0=urow[m % NSLOT], in1=h2c, scale=1.0,
                                           scalar=0.0, op0=ALU.mult, op1=ALU.add,
                                           accum_out=dots[:, m:m + 1]).then_inc(s("u_used"), 1)
                    if m in tops:
                        tops[m]()
                dve.wait_ge(s("ge_done"), n + 1)
                ch(V.reciprocal(erec, esum))
                STT(w_tab[:, ds(n * TOPK, TOPK)], ge, erec, ex, ALU.mult, ALU.mult).then_inc(s("w_done"), 1)

            def top_context(h):
                top(3, h * TOPK, h, "topk0_done")

            def top_first_latents(h):
                dve.wait_ge(s("fs_out"), h * 2 + 3)
                top(0, (h + PH) * TOPK, h)

            def after_half(t, h):
                return {8: lambda: top(t, ((t + 1) * PH + h) * TOPK, h)}

            def tile_of(t):
                ch(CP(h2c, x1[:, ds(t, 1), :].rearrange("p t c -> p (t c)")))
                ch(STT(h2c, h2c, stat[:, ds(t + 51, 1)], rows[:, 3, :], ALU.mult, ALU.mult))
                ch(TT(h2c, h2c, rows[:, 5, :], ALU.add))

            def result(t, who):
                dve.wait_ge(s("pv_done"), t + 2)
                ch(V.reciprocal(pstat[:, 2:3], pstat[:, 1:2]))
                ch(STT(pv, pv, pstat[:, 2:3], rows[:, 6 + who, :], ALU.mult, ALU.mult))
                TT(pv, pv, x1[:, ds(t, 1), :].rearrange("p t c -> p (t c)"), ALU.add).then_inc(s("out_ready"), 1)

            dve.wait_ge(s("h2_ready"), NT)
            dve.wait_ge(s("ssqn"), NT)
            dve.wait_ge(s("sc_free"), 4)
            top_context(0)
            for t in range(1, NT):
                turned_h2(t)
            top_context(1)
            step(0, 0, {4: lambda: top_context(2)})
            with ch.loop(PH - 3, 2 * TOP + 1) as h:
                step(0, h + 1, {4: lambda: top_context(h + 3), 11: lambda: top_first_latents(h)})
            with ch.loop(2, TOP + 1) as h:
                step(0, h + (PH - 2), {8: lambda: top_first_latents(h + (PH - 3))})
            top_first_latents(PH - 1)
            tile_of(1)
            step(1, 0, after_half(1, 0))
            result(0, 0)
            with ch.loop(PH - 1, TOP + 1) as h:
                step(1, h + 1, after_half(1, h + 1))
            with ch.loop(2, 3 + (TOP + 1) + 2 + (PH - 1) * (TOP + 1)) as i:
                tile_of(i + 2)
                step(i + 2, 0, after_half(i + 2, 0))
                result(i + 1, 1)
                with ch.loop(PH - 1, TOP + 1) as h:
                    step(i + 2, h + 1, after_half(i + 2, h + 1))
            tile_of(NT - 1)
            step(NT - 1, 0, {})
            result(NT - 2, 1)
            with ch.loop(PH - 1, 1) as h:
                step(NT - 1, h + 1, {})
            result(NT - 1, 1)


def shape_constants():
    f = np.float32
    i = np.arange(P)
    shp = np.zeros((P, 7, P), f)
    shp[:, 0] = np.eye(P)
    shp[:, 1] = i[:, None] <= i[None, :]
    shp[:, 2] = i[:, None] >= i[None, :]
    shp[:, 3] = 1
    shp[:, 6] = i[None, :]
    shp[:, 4] = np.where(i[:, None] <= i[None, :], 0, NEG)
    shp[:, 5] = np.where(i[:, None] >= i[None, :], 0, NEG)
    ang = 2 * np.pi * ((i[:, None] * i[None, :]) % P) / P
    chm = np.stack([np.cos(ang), np.sin(ang), -np.sin(ang)], 1) / np.sqrt(P)
    l = np.arange(LAT)
    angl = 2 * np.pi * ((l[:, None] * l[None, :]) % LAT) / LAT
    quarter = D // 4
    omega = (1.0 / (f(10000.0) ** (np.arange(quarter, dtype=f) / f(quarter)))).astype(f)
    ar = (l // 64).astype(f)[:, None] * omega
    ac = (l % 64).astype(f)[:, None] * omega
    pos = np.concatenate([np.sin(ar), np.cos(ar), np.sin(ac), np.cos(ac)], -1)
    return {"shp": shp, "chm": chm.astype(f), "posc": (np.cos(angl) / np.sqrt(LAT)).astype(f),
            "poss": (np.sin(angl) / np.sqrt(LAT)).astype(f), "pos": pos.astype(f)}


def layout(i):
    cols = lambda v, n: np.ascontiguousarray(np.asarray(v).reshape(n, P).T)
    i = {k: np.asarray(v) for k, v in i.items()}
    out = dict(shape_constants())
    out["x"] = np.concatenate([i["x_prompt"][0], i["x_sample"][0]], 0)
    out["cond"] = np.stack([cols(i["c_ctx"], KT), cols(i["c"][0], KT)], -1)
    out["ada_b"] = cols(i["b_ada"][0], 48)
    out["norms"] = np.stack([cols(i[n][0], KT) for n in
                             ("norm_mix_pre", "norm_mix_post", "norm_ffn_pre", "norm_ffn_post")], 1)
    out["ssd_norm"] = cols(i["ssd_norm"][0], 16)
    out["conv_w"] = i["w_conv"][0].reshape(TAPS, 24, P).transpose(2, 1, 0)
    out["conv_b"] = cols(i["b_conv"][0], 24)
    for n in ("a_log", "dt_bias", "d_skip"):
        out[n] = i[n].reshape(2 * HEADS)
    out["state"] = i["state_ssd"][0, 0].reshape(2, DI, P).transpose(0, 2, 1)
    for n in ("w_ada", "w_in", "w_fourier", "w_ssd_out", "w_out"):
        out[n] = i[n][0]
    out["w_query"] = i["peer_query"][0]
    out["keys"] = i["peer_sub_keys"][0].reshape(16, P, P).transpose(2, 0, 1)
    out["peer_u"], out["peer_v"] = i["peer_u"][0], i["peer_v"][0]
    return {k: np.ascontiguousarray(v) for k, v in out.items()}


def kernel(**inputs):
    import concourse.bacc as bacc
    from concourse.bass_utils import run_bass_kernel_spmd

    arrays = layout(inputs)
    nc = bacc.Bacc("TRN2", target_bir_lowering=False, num_devices=1)
    args = {k: nc.dram_tensor(f"in_{k}", v.shape, mybir.dt.from_np(v.dtype), kind="ExternalInput").ap()
            for k, v in arrays.items()}
    outs = (nc.dram_tensor("y_out", (TOK, D), F32, kind="ExternalOutput").ap(),
            nc.dram_tensor("state_out", (2, P, DI), F32, kind="ExternalOutput").ap())
    layer_kernel(nc, args, outs)
    r = run_bass_kernel_spmd(nc, [{f"in_{k}": v for k, v in arrays.items()}], core_ids=[0]).results[0]
    y, st = np.asarray(r["y_out"]), np.asarray(r["state_out"])
    return (y[0:P].reshape(1, P, D), y[P:].reshape(1, LAT, D),
            np.ascontiguousarray(st.transpose(0, 2, 1)).reshape(1, 1, 2, HEADS, HD, P))
```

```python
from contextlib import ExitStack, contextmanager

import numpy as np

import concourse.bass as bass
from concourse import mybir
from concourse.bass import ds

F32 = mybir.dt.float32
BF16 = mybir.dt.bfloat16
U32 = mybir.dt.uint32
I32 = mybir.dt.int32
ACT = mybir.ActivationFunctionType
ALU = mybir.AluOpType
AX = mybir.AxisListType

P = 128
D = 1024
KT = D // P
NT = 5
LAT = (NT - 1) * P
TOK = NT * P
HEADS, HD, NG = 32, 64, 4
HG = HEADS // NG
GC = HG * HD
DI = HEADS * HD
TAPS = 5
COL_Z, COL_X = 1024, 3072
COL_B, COL_C = COL_X + DI, COL_X + DI + NG * P
COL_DT = COL_X + DI + 2 * NG * P
COL_GATE = COL_DT + 2 * HEADS
D_IN = COL_GATE + 2 * D
PH, TOPK, NKEY = 8, 16, 128
EPS = 1e-6
GELU_C, GELU_A = float(np.sqrt(2 / np.pi)), 0.044715
NEG = -1e30
LOWEST = -3.0e38
NSLOT = 8
NS = NT * PH

SH1, SC1, GA1, SH2, SC2, GA2 = range(6)

JOB_ADA, JOB_XBC, JOB_U, JOB_FO, JOB_GA, JOB_GB, JOB_SO, JOB_WO, JOB_Q = (
    0, 12, 20, 24, 26, 30, 32, 36, 38)
JOB_Z = (22, 23, 28, 29)
Q_U, Q_FO, Q_GA, Q_GB, Q_SO, Q_WO = 0, 20, 30, 50, 60, 80
Q_Z = (10, 15, 40, 45)
G_GA, G_Z = 10, (0, 5, 20, 25)
T_NORM1, T_XB, T_Y, T_MERGE, T_NORM2 = 0, 10, 38, 58, 68
XB_UNITS = 7
BESIDE = {2: 3, 5: 4, 8: 5}
THIRDS = (0, 3, 6, KT)
COPY_AT = {u + 1: i for u, i in BESIDE.items()}
CONV_AT = {2: 2, 4: 3, 7: 4}
SILU_AT = {1: 0, 2: 1, 3: 2, 5: 3, 8: 4}
FOURIER_BESIDE = {0: 3, 1: 4, 2: 5, 3: 6, 4: 7, 6: 8, 8: 9}
TURN = (4, 3, 2, 1, 0)
STATES = [(1, 4), (1, 3), (1, 2), (1, 0), (0, 0), (0, 1), (0, 2), (0, 3)]


def loaded(n):
    slot, turn = n % 2, n // 2
    extra = 0
    if slot == 1 and n >= JOB_XBC:
        extra = min((n - JOB_XBC) // 2 + 1, NG)
    return 16 * (turn + 1 + extra)


class Chain:

    def __init__(self, eng, sem):
        self.eng, self.sem, self.n, self.marks = eng, sem, 0, 0

    def __call__(self, ins, wait=None):
        ins.then_inc(self.sem, 1)
        self.n, self.marks = self.n + 1, self.marks + 1
        if wait:
            wait(self.eng, self.sem, self.n)
        else:
            self.eng.wait_ge(self.sem, self.n)

    @contextmanager
    def loop(self, count, steps):
        start, before = self.n, self.marks
        with self.eng.Fori(0, count) as i:
            self.n = i * steps + start
            yield i
            assert self.marks - before == steps, (self.marks - before, steps)
        self.n, self.marks = start + count * steps, before + count * steps


def layer_kernel(nc, a, outs):
    y_out, st_out = outs
    with ExitStack() as ctx:
        def sb(name, shape, dt=F32):
            return ctx.enter_context(nc.sbuf_tensor(name, shape, dt))

        def sem(name):
            return ctx.enter_context(nc.semaphore(name))

        bank = [ctx.enter_context(nc.psum_tensor(f"bank{i}", [P, 512], F32)) for i in range(8)]

        shp = sb("shape_consts", [P, 7, P])
        ident, tri, ones = shp[:, 0, :], [shp[:, 1, :], shp[:, 2, :]], shp[:, 3, :]
        identb = sb("identb", [P, P], BF16)
        maskb = sb("maskb", [P, 2, P], BF16)
        zerob = sb("zerob", [P, P], BF16)
        eps = sb("eps", [P, 1])
        cond = sb("cond_sb", [P, KT, 2])
        adab = sb("adab_sb", [P, 48])
        mod = sb("mod", [P, 48, 2])
        norms = sb("norms_sb", [P, 4, KT])
        scl = sb("scl", [P, 4, KT, 2])
        ssdn = sb("ssdn_sb", [P, 16])
        convw = sb("convw_sb", [P, 24, TAPS])
        convb = sb("convb_sb", [P, 24])
        hrow = sb("hrow", [P, 3, 2 * HEADS])
        dsum = sb("dsum", [P, HEADS])
        wdt = sb("wdt", [P, KT, 2 * HEADS])
        tab = sb("tab", [P, 7, NT, 2 * HEADS])
        dt_, dA, ncs, ecs, ecd, dtd, tmp = (tab[:, i] for i in range(7))
        dAg = sb("dAg", [P, NT, 2, HG])
        stat = sb("stat", [P, 64])

        KB = 256
        arena = sb("arena", [P, 189 * KB])

        def at(kb, n):
            o = int(kb * KB)
            assert o + n <= 189 * KB, (kb, n)
            return arena[:, o:o + n]

        hT = at(0, KT * TOK).rearrange("p (k t) -> p k t", k=KT)
        ring = [at(20 + 16 * s, 16 * KB) for s in range(2)]
        Y = at(52, NT * DI).rearrange("p (t c) -> p t c", t=NT)
        x0 = at(92, NT * D).rearrange("p (t c) -> p t c", t=NT)
        pos0 = at(112, 4 * D).rearrange("p (t c) -> p t c", t=4)
        adar = at(52, 6 * D)
        xs = at(92, 4 * TOK).rearrange("p (i t) -> p i t", i=4)
        xtok = at(102, NT * GC).rearrange("p (t c) -> p t c", t=NT)
        Btok = at(112, TOK).rearrange("p (t c) -> p t c", t=NT)
        BT, CT = at(114.5, TOK), at(117, TOK)
        cin = at(119.5, 2 * 648).rearrange("p (s c) -> p s c", s=2)
        acc = at(124.625, 2 * 648).rearrange("p (s c) -> p s c", s=2)
        xd = at(129.75, 8 * 512).rearrange("p (s c) -> p s c", s=8)
        Ee = at(145.75, 4 * 512).rearrange("p (s j l) -> p s j l", s=4, j=4)
        Mm = at(153.75, 2 * 512).rearrange("p (s j l) -> p s j l", s=2, j=4)
        H = at(165.75, 8 * 512).rearrange("p (d s c) -> p d s c", d=2, s=4)
        cbT = at(181.75, TOK).rearrange("p (t c) -> p t c", t=NT)
        xD = at(184.25, 512)
        yt = at(186.25, 512)
        cst = xs.rearrange("p i t -> p (i t)")[:, 512:1536].rearrange("p (d c) -> p d c", d=2)
        Us = [at(kb, NT * 512).rearrange("p (t c) -> p t c", t=NT) for kb in (92, 119.5)]
        FT = at(102, KT * TOK).rearrange("p (k t) -> p k t", k=KT)
        Pq = at(132, 4 * TOK).rearrange("p (s d t) -> p s d t", s=2, d=2)
        posm = at(142, 2 * 4 * 512).rearrange("p (s k t) -> p s k t", s=2, k=4)
        a_out = at(158, NT * D).rearrange("p (t c) -> p t c", t=NT)
        gt = at(178, 4 * 512).rearrange("p (s c) -> p s c", s=4)
        chm = at(186.5, 3 * P).rearrange("p (i n) -> p i n", i=3)
        yT = at(92, 16 * TOK).rearrange("p (k t) -> p k t", k=16)
        sB = at(132, NT * D).rearrange("p (t c) -> p t c", t=NT)
        rows = at(52, 8 * D).rearrange("p (v c) -> p v c", v=8)
        mT = at(92, KT * TOK).rearrange("p (k t) -> p k t", k=KT)
        mix = at(152, NT * D).rearrange("p (t c) -> p t c", t=NT)
        x1 = at(128, NT * D).rearrange("p (t c) -> p t c", t=NT)
        pos1 = at(112, 4 * D).rearrange("p (t c) -> p t c", t=4)
        h2 = mT.rearrange("p k t -> p (k t)").rearrange("p (t c) -> p t c", t=NT)
        h2T = at(0, KT * LAT).rearrange("p (k t) -> p k t", k=KT)
        h2Tc = at(16, KT * P).rearrange("p (k t) -> p k t", k=KT)
        keys = at(84, 16 * P).rearrange("p (i n) -> p i n", i=16)
        qTc = at(112, 16 * P).rearrange("p (i t) -> p i t", i=16)
        half_in = [at(20 + 4.5 * i, (KT + 1) * P).rearrange("p (k n) -> p k n", k=KT + 1) for i in range(2)]
        half_q = [at(30 + 2 * i, LAT) for i in range(2)]
        score = at(152, 4 * 16 * P).rearrange("p (t n) -> p t n", t=4)
        urow = [at(kb, D) for kb in (34, 38, 42, 46, 50, 54, 58, 148)]
        vrow = [at(kb, D) for kb in (84, 88, 92, 96, 100, 104, 108, 184)]
        h2c, pv, h2sq = at(68, D), at(16, D), at(20, D)
        steps = NT * PH * TOPK
        idx_tab = at(112, steps).bitcast(I32)
        d_tab, w_tab = at(114.5, steps), at(117, steps)
        sw, sw2 = (at(119.5 + i, 256).rearrange("p (h n) -> p h n", h=2) for i in range(2))
        cand, cand2 = at(121.5, 256), at(122.5, 256)
        eq = at(123.5, 512).rearrange("p (k n) -> p k n", n=TOPK)
        small = at(125.5, 12 * 32).rearrange("p (i n) -> p i n", i=12)
        v16, pick = small[:, 0], small[:, 1]
        i16, i16f = small[:, 2].bitcast(U32), small[:, 3]
        tv, tp = small[:, 4, 0:TOPK], small[:, 4, TOPK:].bitcast(U32)
        tij, tijf = small[:, 5].bitcast(U32), small[:, 6]
        dots, ge, ex = small[:, 7, 0:TOPK], small[:, 7, TOPK:], small[:, 8, 0:TOPK]
        esum, erec = small[:, 9, 0:1], small[:, 9, 1:2]
        pstat = small[:, 10, 0:4]
        idx_u = [small[:, 11, 16 * i:16 * i + 16].bitcast(I32) for i in range(2)]
        iota16 = shp[:, 6, 0:TOPK]
        idx_v = [at(127 + i / 16, TOPK).bitcast(I32) for i in range(2)]
        diag = at(62, 4 * P).rearrange("p (s n) -> p s n", s=4)

        S = {}

        def s(name):
            if name not in S:
                S[name] = sem(name)
            return S[name]

        NAMES = ("consts_in x_in pos_in w_free tm_full tm_free tr_full tr_free cond_ready ada_rows ada_done coef_ready "
                 "identb_ready x_ready ssq1 var1 std1 xn_ready wdt_in dt_full nega v_ready softp dA_ready cs_full "
                 "tmc_ready exps_ready tabs_ready ch_full ch_free conv_done silu_done cb_full cb_done h0_in "
                 "xd_ready st_full st_free cst_out eb_ready dAg_ready e_full e_done m_done yo_full y_full "
                 "y_free xD_ready d1_full d1_act d1_dve d2_full d2_free chm_in posm_in gt_used "
                 "ssqy vary stdy rstdy mg_done row_full row_free x1_in varm stdm ssqm x1_done ssqn varn stdn h2_ready "
                 "keys_in fq_full fq_out fs_full fs_out sc_full sc_free topk0_done topk_done ge_done w_done diag_done u_used v_used pv_full pv_done pstd out_ready out_done idx_cp dve act waited")
        for nm in NAMES.split():
            s(nm)
        w_in = [sem("w_slot0_in"), sem("w_slot1_in")]
        u_in = [sem(f"u_slot{i}_in") for i in range(NSLOT)]
        half_w = [sem(f"half_head{i}_in") for i in range(2)]
        v_in = [sem(f"v_slot{i}_in") for i in range(NSLOT)]

        block = ctx.enter_context(nc.Block())

        win = a["w_in"].rearrange("(k p) n -> p k n", p=P)
        CONSTS = ["shp", "cond", "ada_b", "norms", "ssd_norm", "conv_w", "conv_b", "a_log", "dt_bias", "d_skip"]

        def wait_alone(eng, semaphore, value):
            eng.wait_ge(semaphore, value)
            if not isinstance(value, int):
                eng.sem_inc(s("waited"), 1)


        @block.sync
        def _(sp):
            for nm in ("cst_out", "out_done"):
                sp.nop().then_inc(s(nm), 16)
            for dst, name in ((shp, "shp"), (cond, "cond"), (adab, "ada_b"), (norms, "norms"), (ssdn, "ssd_norm"),
                              (convw, "conv_w"), (convb, "conv_b")):
                sp.dma_start(dst[:], a[name]).then_inc(s("consts_in"), 16)
            for i, name in enumerate(("a_log", "dt_bias", "d_skip")):
                sp.dma_start(hrow[:, i, :], a[name].partition_broadcast(P)).then_inc(s("consts_in"), 16)

            def load(n, src, cols, first=False, k=KT, off=0):
                if not first:
                    wait_alone(sp, s("w_free"), n - 1)
                dst = ring[n % 2 if isinstance(n, int) else load.slot]
                dst = dst.rearrange("p (k c) -> p k c", k=k)[:, :, off:off + cols]
                sp.dma_start(dst, src).then_inc(w_in[n % 2 if isinstance(n, int) else load.slot], 16)

            wada = a["w_ada"].rearrange("(k p) n -> p k n", p=P)
            load(0, wada[:, :, 0:512], 512, True)
            load(1, wada[:, :, 512:1024], 512, True)
            sp.dma_start(x0[:, 0, :], a["x"][0:P, :]).then_inc(s("x_in"), 16)
            x_tiles, pos_tiles = (a[n].rearrange("(t p) c -> p t c", p=P) for n in ("x", "pos"))
            with sp.Fori(1, NT) as i:
                for load.slot in range(2):
                    load(i * 2 + load.slot, wada[:, :, ds(i * 1024 + 512 * load.slot, 512)], 512)
                sp.dma_start(x0[:, ds(i, 1), :], x_tiles[:, ds(i, 1), :]).then_inc(s("x_in"), 16)
                sp.dma_start(pos0[:, ds(i - 1, 1), :], pos_tiles[:, ds(i - 1, 1), :]).then_inc(s("pos_in"), 16)
            for n in (10, 11):
                load(n, wada[:, :, 512 * n:512 * n + 512], 512)
            sp.dma_start(wdt[:], win[:, :, COL_DT:COL_DT + 64]).then_inc(s("wdt_in"), 16)
            def load_group(g):
                load.slot = 0
                load(g * 2 + JOB_XBC, win[:, :, ds(g * GC + COL_X, GC)], GC)
                load.slot = 1
                load(g * 2 + JOB_XBC + 1, win[:, :, ds(g * P + COL_B, P)], P)
                load(g * 2 + JOB_XBC + 1, win[:, :, ds(g * P + COL_C, P)], P, True, off=P)

            def group_states(g, next_weights):
                next_weights()
                wait_alone(sp, s("y_full"), g * 10 + 1)
                wait_alone(sp, s("tr_free"), g * XB_UNITS + T_XB)
                sp.dma_start(H[:, 0, 0, :], a["state"][0, :, ds(g * GC, GC)]).then_inc(s("h0_in"), 16)
                sp.dma_start(H[:, 1, 3, :], a["state"][1, :, ds(g * GC, GC)]).then_inc(s("h0_in"), 16)
                wait_alone(sp, s("st_free"), g * 8 + 5)
                for d in range(2):
                    sp.dma_start(st_out[d, :, ds(g * GC, GC)], cst[:, d, :]).then_inc(s("cst_out"), 16)

            def load_u():
                load(JOB_U, win[:, :, 0:512], 512)
                load(JOB_U + 1, win[:, :, 512:1024], 512)

            load_group(0)
            with sp.Fori(0, NG - 1) as g:
                group_states(g, lambda: load_group(g + 1))
            group_states(NG - 1, load_u)
            def load_z(j):
                load(JOB_Z[j], win[:, :, COL_Z + 512 * j:COL_Z + 512 * j + 512], 512)

            load_z(0)
            load_z(1)
            sp.wait_ge(s("y_free"), NG * NT + 1)
            sp.dma_start(chm, a["chm"]).then_inc(s("chm_in"), 16)
            for i, name in enumerate(("posc", "poss")):
                sp.dma_start(posm[:, i], a[name].rearrange("(k p) n -> p k n", p=P)).then_inc(s("posm_in"), 16)
            wf = a["w_fourier"].rearrange("(k p) n -> p k n", p=P)
            for j in range(2):
                load(JOB_FO + j, wf[:, :, 512 * j:512 * j + 512], 512)
            for j in range(2):
                load(JOB_GA + j, win[:, :, COL_GATE + 512 * j:COL_GATE + 512 * j + 512], 512)
            load_z(2)
            load_z(3)
            for j in range(2):
                load(JOB_GB + j, win[:, :, COL_GATE + D + 512 * j:COL_GATE + D + 512 * j + 512], 512)
            wso = a["w_ssd_out"].rearrange("(k p) n -> p k n", p=P)
            for j in range(4):
                load(JOB_SO + j, wso[:, :, 256 * j:256 * j + 256], 256, k=16)
            wo = a["w_out"].rearrange("(k p) n -> p k n", p=P)
            for j in range(2):
                load(JOB_WO + j, wo[:, :, 512 * j:512 * j + 512], 512)
            sp.wait_ge(s("tr_free"), T_NORM2)
            sp.dma_start(x1, a["x"].rearrange("(t p) c -> p t c", p=P)).then_inc(s("x1_in"), 16)
            sp.dma_start(pos1, a["pos"].rearrange("(t p) c -> p t c", p=P)).then_inc(s("x1_in"), 16)
            sp.dma_start(keys, a["keys"]).then_inc(s("keys_in"), 16)
            wq = a["w_query"].rearrange("(k p) n -> p k n", p=P)
            for j in range(4):
                load(JOB_Q + j, wq[:, :, 512 * j:512 * j + 512], 512)

            def half_head(h, i):
                sp.dma_start(half_in[i][:, 0:KT, :], wq[:, :, ds(h * 256 + P * i, P)]).then_inc(half_w[i], 16)
                sp.dma_start(half_in[i][:, KT:, :], a["keys"][:, ds(h * 2 + i, 1), :]).then_inc(half_w[i], 16)

            sp.wait_ge(s("w_free"), JOB_Q + 4)
            for i in range(2):
                half_head(0, i)
            with sp.Fori(1, PH) as h:
                for i in range(2):
                    wait_alone(sp, s("fs_full"), h * 2 + i - 1)
                    half_head(h, i)
            yv = y_out.rearrange("(t p) c -> p t c", p=P)
            with sp.Fori(0, NT) as t:
                wait_alone(sp, s("out_ready"), t + 1)
                sp.dma_start(yv[:, ds(t, 1), :], pv.unsqueeze(1)).then_inc(s("out_done"), 16)
            sp.wait_ge(s("out_done"), 16 * NT + 16)
            sp.wait_ge(s("cst_out"), NG * 32 + 16)

        @block.tensor
        def _(pe):
            for nm in ("y_full", "v_used"):
                pe.nop().then_inc(s(nm), 1)
            mm = nc.tensor.matmul

            def need(n):
                pe.wait_ge(w_in[n % 2], loaded(n))

            pe.wait_ge(s("cond_ready"), 1)
            pe.wait_ge(s("consts_in"), 16 * len(CONSTS))

            def ada_rows(n, slot, first=False):
                pe.wait_ge(w_in[slot], (n - slot) * 8 + 16)
                if not first:
                    pe.wait_ge(s("ada_rows"), n - 1)
                w = ring[slot].rearrange("p (k c) -> p k c", k=KT)
                for k in range(KT):
                    last = mm(bank[slot][0:2, :], cond[:, k, :], w[:, k, :], start=(k == 0), stop=(k == KT - 1))
                last.then_inc(s("w_free"), 1)

            ada_rows(0, 0, True)
            ada_rows(1, 1, True)
            with pe.Fori(1, 6) as i:
                ada_rows(i * 2, 0)
                ada_rows(i * 2 + 1, 1)
            for m in range(48):
                if m % 4 == 0:
                    pe.wait_ge(s("ada_rows"), m // 4 + 1)
                last = nc.tensor.transpose(bank[7][:, 2 * m:2 * m + 2], adar[0:2, m * P:(m + 1) * P], ident[0:2, 0:2])
            last.then_inc(s("ada_done"), 1)

            def transpose_unit(u, blocks, bk=None):
                if not isinstance(u, int) or u >= 2:
                    pe.wait_ge(s("tr_free"), u - 1)
                b = bank[5 + (u % 2 if bk is None else bk)]
                for i, blk in enumerate(blocks):
                    last = nc.tensor.transpose(b[:, i * P:(i + 1) * P], blk, ident)
                last.then_inc(s("tr_full"), 1)

            for t in range(NT):
                pe.wait_ge(s("xn_ready"), t + 1)
                for h in range(2):
                    transpose_unit(T_NORM1 + 2 * t + h,
                                   [x0[:, t, (4 * h + i) * P:(4 * h + i + 1) * P] for i in range(4)])

            def xbc_tile(g, i, thirds=(0, 1, 2)):
                ks = range(THIRDS[thirds[0]], THIRDS[thirds[-1] + 1])
                if i == 0:
                    pe.wait_ge(w_in[0], g * 16 + loaded(JOB_XBC))
                if i == 4:
                    pe.wait_ge(w_in[1], g * 32 + loaded(JOB_XBC + 1))
                if thirds[0] == 0 and (i or not isinstance(g, int)):
                    pe.wait_ge(s("ch_free"), g * 6 + i)
                w = ring[i // 4].rearrange("p (k c) -> p k c", k=KT)
                c0 = (i % 4) * P
                for k in ks:
                    mm(bank[2][:, :], w[:, k, c0:c0 + P], hT[:, k, P:TOK], start=(k == 0), stop=(k == KT - 1),
                       skip_group_check=True)
                if thirds[-1] < 2:
                    return
                for k in range(KT):
                    last = mm(bank[3][:, 0:P], w[:, k, c0:c0 + P], hT[:, k, 0:P],
                              start=(k == 0), stop=(k == KT - 1))
                last.then_inc(s("ch_full"), 1)
                if i == 3 or i == 5:
                    pe.wait_ge(s("ch_full"), g * 6 + i + 1)
                    pe.nop().then_inc(s("w_free"), 1)

            pe.wait_ge(s("tr_free"), T_XB)
            pe.wait_ge(s("wdt_in"), 16)
            pe.wait_ge(s("coef_ready"), 1)
            for t in range(NT):
                for k in range(KT):
                    last = mm(bank[7][:, 64 * t:64 * t + 64], hT[:, k, t * P:(t + 1) * P], wdt[:, k, :],
                              start=(k == 0), stop=(k == KT - 1))
            last.then_inc(s("dt_full"), 1)
            xbc_tile(0, 0)
            pe.wait_ge(s("dA_ready"), 1)
            b7 = bank[7][:, 0:320].rearrange("p (t h) -> p t h", t=NT)
            for d in range(2):
                mm(b7[:, :, 32 * d:32 * d + 32], tri[d], dA[:, :, 32 * d:32 * d + 32], start=True, stop=True)
            mm(bank[0][:, 0:320], ones, dA.rearrange("p t h -> p (t h)"), start=True, stop=True).then_inc(s("cs_full"), 1)

            pe.wait_ge(s("identb_ready"), 1)
            def fourier_tile(q):
                j, t = divmod(q, NT)
                if t == 0:
                    need(JOB_U + j)
                if q == 0:
                    pe.wait_ge(s("ch_free"), NG * 6)
                if q >= 2:
                    pe.wait_ge(s("tm_free"), q - 1)
                w = ring[(JOB_U + j) % 2].rearrange("p (k c) -> p k c", k=KT)
                for k in range(KT):
                    last = mm(bank[2 + q % 2][:, :], hT[:, k, t * P:(t + 1) * P], w[:, k, :],
                              start=(k == 0), stop=(k == KT - 1))
                last.then_inc(s("tm_full"), 1)
                if t == NT - 1:
                    pe.wait_ge(s("tm_full"), q + 1)
                    pe.nop().then_inc(s("w_free"), 1)

            def scan_group(g, overlap):
                def beside(i):
                    xbc_tile(g + 1, i) if overlap else fourier_tile(i)

                beside(0)
                pe.wait_ge(s("y_free"), g * NT + 1)
                pe.wait_ge(s("silu_done"), g * 6 + 4)
                for n, t in enumerate(TURN):
                    transpose_unit(g * XB_UNITS + T_XB + n, [xs[:, i, t * P:(t + 1) * P] for i in range(4)], n % 2)
                pe.wait_ge(s("silu_done"), g * 6 + 5)
                transpose_unit(g * XB_UNITS + T_XB + 5, [BT[:, t * P:(t + 1) * P] for t in range(4)], 1)
                transpose_unit(g * XB_UNITS + T_XB + 6, [BT[:, 4 * P:5 * P]], 0)
                beside(1)
                pe.wait_ge(s("silu_done"), g * 6 + 6)
                for c in range(NT):
                    b = bank[4][:, c * P:(c + 1) * P] if c < 4 else bank[7][:, 0:P]
                    last = mm(b, BT[:, c * P:(c + 1) * P], CT[:, c * P:(c + 1) * P], start=True, stop=True)
                last.then_inc(s("cb_full"), 1)
                pe.wait_ge(s("tr_free"), g * XB_UNITS + T_XB + 7)
                for k, (d, c) in enumerate(STATES):
                    if k == 3:
                        beside(2)
                    pe.wait_ge(s("xd_ready"), g * 8 + k + 1)
                    if k >= 2:
                        pe.wait_ge(s("st_free"), g * 8 + k - 1)
                    mm(bank[k % 2][:, :], Btok[:, c, :], xd[:, k, :], start=True, stop=True).then_inc(s("st_full"), 1)

                def decay_rows(u):
                    c, hq = divmod(u, 2)
                    for d in range(2):
                        e = 2 * u + d
                        if e >= 2:
                            pe.wait_ge(s("e_done"), g * 20 + e - 1)
                        b = bank[d]
                        mm(b[:, :], identb[:], maskb[:, d, :].unsqueeze(1).broadcast_to([P, 4, P]),
                           start=True, stop=False, skip_group_check=True)
                        for j in range(4):
                            last = mm(b[:, j * P:(j + 1) * P],
                                      dAg[:, c, d, 4 * hq + j:4 * hq + j + 1].broadcast_to([P, P]), tri[d],
                                      start=False, stop=(j == 3), skip_group_check=True)
                        last.then_inc(s("e_full"), 1)

                pe.wait_ge(s("st_free"), g * 8 + 8)
                pe.wait_ge(s("dAg_ready"), g + 1)
                pe.wait_ge(s("h0_in"), g * 32 + 32)
                decay_rows(0)
                for u in range(2 * NT):
                    c, hq = divmod(u, 2)
                    if u + 1 < 2 * NT:
                        decay_rows(u + 1)
                    if overlap and u < 9:
                        xbc_tile(g + 1, 3 + u // 3, (u % 3,))
                    if not overlap and u in FOURIER_BESIDE:
                        beside(FOURIER_BESIDE[u])
                    if c and not hq:
                        pe.wait_ge(s("cb_done"), g + 1)
                        pe.wait_ge(s("y_free"), g * NT + c + 1)
                        for d in range(2):
                            last = mm(bank[(4, 7)[d]][:, :], CT[:, c * P:(c + 1) * P], H[:, d, c - 1, :],
                                      start=True, stop=True)
                        last.then_inc(s("yo_full"), 1)
                    pe.wait_ge(s("m_done"), g * 10 + u + 1)
                    if c >= 2 and not hq:
                        pe.wait_ge(s("y_free"), g * NT + c)
                    for j in range(4):
                        o = slice((4 * hq + j) * HD, (4 * hq + j + 1) * HD)
                        last = mm(bank[5 + c % 2][:, o], Mm[:, u % 2, j, :], xtok[:, c, o], start=True, stop=True)
                    last.then_inc(s("y_full"), 1)

            for i in range(1, 6):
                xbc_tile(0, i)
            pe.wait_ge(s("tabs_ready"), 1)
            with pe.Fori(0, NG - 1) as g:
                scan_group(g, True)
            scan_group(NG - 1, False)

            def product_tile(q, lhs, k_tiles, w, cols=512):
                t = q % NT
                if q >= NT:
                    pe.wait_ge(s("tm_free"), q - 4)
                for k in range(k_tiles):
                    last = mm(bank[t][:, 0:cols], lhs[:, k, t * P:(t + 1) * P], w[:, k, :],
                              start=(k == 0), stop=(k == k_tiles - 1))
                last.then_inc(s("tm_full"), 1)

            def job(n, q, lhs, k_tiles=KT, cols=512):
                need(n)
                w = ring[n % 2].rearrange("p (k c) -> p k c", k=k_tiles)
                for t in range(NT):
                    product_tile(q + t, lhs, k_tiles, w, cols)
                pe.wait_ge(s("tm_full"), q + NT)
                pe.nop().then_inc(s("w_free"), 1)

            pe.wait_ge(s("y_free"), NG * NT + 1)
            pe.wait_ge(s("tm_free"), Q_U + 10)
            for j in range(2):
                job(JOB_Z[j], Q_Z[j], hT)

            pe.wait_ge(s("tm_free"), Q_Z[1] + 5)
            pe.wait_ge(s("posm_in"), 32)
            pe.wait_ge(s("chm_in"), 16)

            def over_positions(f):
                if f:
                    pe.wait_ge(s("d1_act"), f)
                    pe.wait_ge(s("d1_dve"), f)
                fs = slice(f % 4 * P, (f % 4 + 1) * P)
                half = Us[f // 4]
                for i in range(2):
                    for k in range(4):
                        mm(bank[5 + i][:, :], half[:, 1 + k, fs], posm[:, i, k, :], start=(k == 0), stop=(k == 3))
                for i in range(2):
                    last = mm(bank[(7, 4)[i]][:, 0:P], half[:, 0, fs], chm[:, i, :], start=True, stop=True)
                last.then_inc(s("d1_full"), 1)

            over_positions(0)
            for f in range(KT):
                if f + 1 < KT:
                    over_positions(f + 1)
                if f + 1 == KT:
                    pe.wait_ge(s("d1_act"), KT)
                    pe.wait_ge(s("d1_dve"), KT)
                if f >= 2:
                    pe.wait_ge(s("d2_free"), f - 1)
                for i in range(2):
                    m = chm[:, 2 * i, :]
                    mm(bank[f % 2][:, :], m, Pq[:, f % 2, i, P:TOK], start=(i == 0), stop=(i == 1))
                for i in range(2):
                    last = mm(bank[2 + f % 2][:, 0:P], chm[:, 2 * i, :], Pq[:, f % 2, i, 0:P],
                              start=(i == 0), stop=(i == 1))
                last.then_inc(s("d2_full"), 1)
            pe.wait_ge(s("d2_free"), KT)
            for j in range(2):
                job(JOB_FO + j, Q_FO + 5 * j, FT)
            for j in range(2):
                job(JOB_GA + j, Q_GA + 5 * j, hT)

            def turn_y(j):
                for t in range(NT):
                    pe.wait_ge(s("gt_used"), G_Z[j] + t + 1)
                    transpose_unit(T_Y + 5 * j + t, [Y[:, t, (4 * j + i) * P:(4 * j + i + 1) * P] for i in range(4)])

            turn_y(0)
            job(JOB_Z[2], Q_Z[2], hT)
            turn_y(1)
            job(JOB_Z[3], Q_Z[3], hT)
            turn_y(2)
            job(JOB_GB, Q_GB, hT)
            turn_y(3)
            job(JOB_GB + 1, Q_GB + 5, hT)

            pe.wait_ge(s("tr_free"), T_MERGE)
            for v in range(8):
                kind, who = divmod(v, 2)
                for h in range(2):
                    u = 2 * v + h
                    if u >= 2:
                        pe.wait_ge(s("row_free"), u - 1)
                    for i in range(4):
                        k = 4 * h + i
                        col = (scl[:, 2, k, who:who + 1], scl[:, 1, k, who:who + 1],
                               mod[:, SH2 * 8 + k, who:who + 1], scl[:, 3, k, who:who + 1])[kind]
                        last = mm(bank[6 + h][:, i * P:(i + 1) * P], col.broadcast_to([P, P]), ident, start=True, stop=True)
                    last.then_inc(s("row_full"), 1)

            for j in range(4):
                job(JOB_SO + j, Q_SO + 5 * j, yT, 16, 256)
            pe.wait_ge(s("mg_done"), 20)
            pe.wait_ge(s("row_free"), 16)
            for t in range(NT):
                for h in range(2):
                    transpose_unit(T_MERGE + 2 * t + h,
                                   [a_out[:, t, (4 * h + i) * P:(4 * h + i + 1) * P] for i in range(4)])
            pe.wait_ge(s("tr_free"), T_NORM2)
            for j in range(2):
                job(JOB_WO + j, Q_WO + 5 * j, mT)

            def turn_h2(t):
                pe.wait_ge(s("h2_ready"), t + 1)
                for h in range(2):
                    src = h2[:, t, :] if t else h2c
                    transpose_unit(T_NORM2 + 2 * t + h, [src[:, (4 * h + i) * P:(4 * h + i + 1) * P] for i in range(4)])

            turn_h2(0)
            pe.wait_ge(s("tr_free"), T_NORM2 + 2)
            pe.wait_ge(s("tm_free"), Q_WO + 10)
            for j in range(4):
                need(JOB_Q + j)
                w = ring[(JOB_Q + j) % 2].rearrange("p (k c) -> p k c", k=KT)
                if j >= 2:
                    pe.wait_ge(s("ch_free"), 6 * NG + j - 1)
                for i in range(4):
                    for k in range(KT):
                        last = mm(bank[j % 2][:, i * P:(i + 1) * P], w[:, k, i * P:(i + 1) * P], h2Tc[:, k, :],
                                  start=(k == 0), stop=(k == KT - 1))
                last.then_inc(s("ch_full"), 1)
                pe.wait_ge(s("ch_full"), 6 * NG + j + 1)
                pe.nop().then_inc(s("w_free"), 1)
            pe.wait_ge(s("keys_in"), 16)
            for q4 in range(4):
                pe.wait_ge(s("ch_free"), 6 * NG + q4 + 1)
                for i in range(4):
                    hi = 4 * q4 + i
                    last = mm(bank[(2, 3, 4, 7)[q4]][:, i * P:(i + 1) * P], qTc[:, hi, :], keys[:, hi, :],
                              start=True, stop=True)
                last.then_inc(s("sc_full"), 1)
            for t in range(1, NT):
                turn_h2(t)

            def latent_query(h, piece):
                i, k = divmod(piece, KT)
                if k == 0:
                    pe.wait_ge(half_w[i], h * 32 + 32)
                last = mm(bank[2 + i][:, :], half_in[i][:, k, :], h2T[:, k, :], start=(k == 0), stop=(k == KT - 1),
                          skip_group_check=True)
                if k == KT - 1:
                    last.then_inc(s("fq_full"), 1)

            def latent_scores(h):
                for i in range(2):
                    pe.wait_ge(s("fq_out"), h * 2 + i + 1)
                    pe.wait_ge(s("fs_out"), h * 2 + 1)
                    for t in range(4):
                        last = mm(bank[4 + i][:, t * P:(t + 1) * P], half_q[i][:, t * P:(t + 1) * P],
                                  half_in[i][:, KT, :], start=True, stop=True)
                    last.then_inc(s("fs_full"), 1)

            def zero_sums(t):
                pe.wait_ge(s("pv_done"), t + 1)
                for i in range(2):
                    mm(bank[i][:, :], zerob[:], maskb[:, 0, :].unsqueeze(1).broadcast_to([P, 4, P]),
                       start=True, stop=False, skip_group_check=True)

            def add_rows(t, h, queries=False):
                for m in range(TOPK):
                    pe.wait_ge(s("diag_done"), t * PH * TOPK + h * TOPK + m + 1)
                    pe.wait_ge(v_in[m % NSLOT], t * PH * 32 + h * 32 + 16 * (m // NSLOT + 1))
                    for i in range(2):
                        last = mm(bank[i][:, :], diag[:, m % 4, :], vrow[m % NSLOT][:, 512 * i:512 * i + 512],
                                  start=False, stop=False, skip_group_check=True)
                    last.then_inc(s("v_used"), 1)
                    if queries and m >= 2:
                        for piece in ([m - 2] if m < 14 else [2 * m - 16, 2 * m - 15]):
                            latent_query(h + 1, piece)

            pe.wait_ge(s("sc_free"), 4)
            pe.wait_ge(s("tr_free"), T_NORM2 + 10)
            zero_sums(0)
            for piece in range(2 * KT):
                latent_query(0, piece)
            latent_scores(0)
            with pe.Fori(0, PH - 1) as h:
                add_rows(0, h, True)
                latent_scores(h + 1)
            add_rows(0, PH - 1)
            with pe.Fori(1, NT) as t:
                zero_sums(t)
                with pe.Fori(0, PH) as h:
                    add_rows(t, h)

        @block.scalar
        def _(act):
            for nm in ("pv_done", "fs_out"):
                act.nop().then_inc(s(nm), 1)
            A = nc.scalar.activation
            ch = Chain(act, s("act"))
            act.wait_ge(s("consts_in"), 16 * len(CONSTS))
            A(cond[:], cond[:], ACT.Silu).then_inc(s("cond_ready"), 1)
            A(hrow[:, 0, :], hrow[:, 0, :], ACT.Exp).then_inc(s("nega"), 1)

            def take_ada(n):
                act.wait_ge(s("w_free"), n + 1)
                A(adar[0:2, 512 * n:512 * n + 512], bank[n % 2][0:2, :], ACT.Copy).then_inc(s("ada_rows"), 1)

            for n in range(9):
                take_ada(n)
            sq = hT.rearrange("p k t -> p (k t)")
            for t in range(NT):
                act.wait_ge(s("x_ready"), t) if t else act.wait_ge(s("x_in"), 16 * NT)
                A(sq[:, t * D:(t + 1) * D], x0[:, t, :], ACT.Square, accum_out=stat[:, t:t + 1]).then_inc(s("ssq1"), 1)
            take_ada(9)
            act.wait_ge(s("var1"), 1)
            A(stat[:, 0:NT], stat[:, 0:NT], ACT.Sqrt).then_inc(s("std1"), 1)
            for n in (10, 11):
                take_ada(n)
            act.wait_ge(s("v_ready"), 1)
            ch(A(tmp, tmp, ACT.Exp))
            A(tmp, tmp, ACT.Ln, bias=1.0).then_inc(s("softp"), 1)
            b7 = bank[7][:, 0:320].rearrange("p (t h) -> p t h", t=NT)
            b0 = bank[0][:, 0:320].rearrange("p (t h) -> p t h", t=NT)
            act.wait_ge(s("tmc_ready"), 1)
            A(ecs, b7, ACT.Exp).then_inc(s("exps_ready"), 1)
            A(ecd, b0, ACT.Exp).then_inc(s("exps_ready"), 1)
            A(tmp, tmp, ACT.Exp).then_inc(s("exps_ready"), 1)

            def into_cin(g, i):
                act.wait_ge(s("ch_full"), g * 6 + i + 1)
                if i >= 2:
                    act.wait_ge(s("conv_done"), g * 6 + i - 1)
                A(cin[:, i % 2, 2:130], bank[3][:, 0:P], ACT.Copy)
                A(cin[:, i % 2, 134:646], bank[2][:, :], ACT.Copy).then_inc(s("ch_free"), 1)

            def silu(g, i, first=False):
                act.wait_ge(s("conv_done"), g * 6 + i + 1)
                if i == 0 and not first:
                    act.wait_ge(s("tr_full"), g * XB_UNITS + T_XB)
                    act.wait_ge(s("cst_out"), g * 32 + 16)
                if i == 5:
                    act.wait_ge(s("y_full"), g * 10 + 1)
                dst = xs[:, i, :] if i < 4 else (BT, CT)[i - 4]
                A(dst[:, 0:P], acc[:, i % 2, 0:P], ACT.Silu)
                A(dst[:, P:TOK], acc[:, i % 2, 132:644], ACT.Silu).then_inc(s("silu_done"), 1)

            def take(q, dst, func, cols=512, **kw):
                act.wait_ge(s("tm_full"), q + 1)
                A(dst, bank[q % NT][:, 0:cols], func, **kw).then_inc(s("tm_free"), 1)

            def take_fourier(q):
                j, t = divmod(q, NT)
                act.wait_ge(s("tm_full"), q + 1)
                if q == 1:
                    act.wait_ge(s("cst_out"), NG * 32 + 16)
                A(Us[j][:, t, :], bank[2 + q % 2][:, :], ACT.Copy).then_inc(s("tm_free"), 1)

            def scan_exps(g, overlap):
                if overlap:
                    into_cin(g + 1, 0)
                silu(g, 5)
                if overlap:
                    into_cin(g + 1, 1)
                else:
                    act.wait_ge(s("tr_full"), g * XB_UNITS + T_XB + NT)
                    take_fourier(0)
                act.wait_ge(s("cb_full"), g + 1)
                A(cbT[:, 0:4, :], bank[4][:, :].rearrange("p (t c) -> p t c", t=4), ACT.Copy)
                A(cbT[:, 4, :], bank[7][:, 0:P], ACT.Copy).then_inc(s("cb_done"), 1)
                if overlap:
                    into_cin(g + 1, 2)
                for e in range(20):
                    u, d = divmod(e, 2)
                    c, hq = divmod(u, 2)
                    act.wait_ge(s("e_full"), g * 20 + e + 1)
                    if e >= 4:
                        act.wait_ge(s("m_done"), g * 10 + u - 1)
                    for j in range(4):
                        last = A(Ee[:, e % 4, j, :], bank[d][:, j * P:(j + 1) * P], ACT.Exp,
                                 bias=ncs[:, c, ds(g * HG + 32 * d + 4 * hq + j, 1)])
                    last.then_inc(s("e_done"), 1)
                    if overlap and d:
                        if u in COPY_AT:
                            into_cin(g + 1, COPY_AT[u])
                        if u in SILU_AT:
                            silu(g + 1, SILU_AT[u])
                    if not overlap and e == 1:
                        take_fourier(1)
                    if not overlap and d and u == 0:
                        take_fourier(2)
                    if not overlap and d and u - 1 in FOURIER_BESIDE:
                        take_fourier(FOURIER_BESIDE[u - 1])

            for i in range(6):
                into_cin(0, i)
                if i:
                    silu(0, i - 1, True)
            with act.Fori(0, NG - 1) as g:
                scan_exps(g, True)
            scan_exps(NG - 1, False)

            def gate(q, n, func):
                if n >= 4:
                    act.wait_ge(s("gt_used"), n - 3)
                take(q, gt[:, n % 4, :], func)

            def gate_z(j):
                for t in range(NT):
                    gate(Q_Z[j] + t, G_Z[j] + t, ACT.Silu)

            gate_z(0)
            gate_z(1)
            for f in range(KT):
                act.wait_ge(s("d1_full"), f + 1)
                if f >= 2:
                    act.wait_ge(s("d2_full"), f - 1)
                A(Pq[:, f % 2, 0, 0:P], bank[7][:, 0:P], ACT.Copy)
                A(Pq[:, f % 2, 0, P:TOK], bank[5][:, :], ACT.Copy).then_inc(s("d1_act"), 1)
            for q in range(Q_FO, Q_FO + 10):
                j, t = divmod(q - Q_FO, NT)
                take(q, a_out[:, t, 512 * j:512 * j + 512], ACT.Copy)
            for n in range(10):
                gate(Q_GA + n, G_GA + n, ACT.Sigmoid)
            gate_z(2)
            gate_z(3)
            act.wait_ge(s("gt_used"), 30)
            for t in range(NT):
                for j in range(4):
                    if t:
                        act.wait_ge(s("ssqy"), 4 * t + j - 3)
                    A(gt[:, j, :], Y[:, t, 512 * j:512 * j + 512], ACT.Square,
                      accum_out=stat[:, 10 + 4 * t + j:11 + 4 * t + j]).then_inc(s("ssqy"), 1)
            for q in range(Q_GB, Q_GB + 10):
                j, t = divmod(q - Q_GB, NT)
                take(q, sB[:, t, 512 * j:512 * j + 512], ACT.Sigmoid)
            act.wait_ge(s("vary"), 1)
            A(stat[:, 30:35], stat[:, 30:35], ACT.Sqrt).then_inc(s("stdy"), 1)
            act.wait_ge(s("rstdy"), 1)
            act.wait_ge(s("ssqy"), 20)
            for n, q in enumerate(range(Q_SO, Q_SO + 20)):
                j, t = divmod(n, NT)
                if n >= 4:
                    act.wait_ge(s("mg_done"), n - 3)
                take(q, gt[:, n % 4, 0:256], ACT.Copy, 256, scale=stat[:, 30 + t:31 + t])
            def root(cols, var_sem, std_sem, n):
                act.wait_ge(s(var_sem), n)
                A(stat[:, cols], stat[:, cols], ACT.Sqrt).then_inc(s(std_sem), 1)

            def square_x1(t):
                act.wait_ge(s("x1_done"), t + 1)
                A(mix[:, t, :], x1[:, t, :], ACT.Square, accum_out=stat[:, 51 + t:52 + t]).then_inc(s("ssqn"), 1)

            for n, q in enumerate(range(Q_WO, Q_WO + 10)):
                j, t = divmod(n, NT)
                act.wait_ge(s("tm_full"), q + 1)
                if n == 0:
                    act.wait_ge(s("mg_done"), 20)
                    act.wait_ge(s("tm_free"), Q_WO)
                if n >= 4:
                    act.wait_ge(s("ssqm"), n - 3)
                A(gt[:, n % 4, :], bank[q % NT][:, :], ACT.Square,
                  accum_out=stat[:, 36 + 2 * t + j:37 + 2 * t + j]).then_inc(s("ssqm"), 1)
                take(q, mix[:, t, 512 * j:512 * j + 512], ACT.Copy)
                if n == NT:
                    root(slice(46, 47), "varm", "stdm", 1)
                if n == NT + 1:
                    square_x1(0)
                    root(slice(51, 52), "varn", "stdn", 1)
            root(slice(47, 51), "varm", "stdm", 2)
            for t in range(1, NT):
                square_x1(t)
            root(slice(52, 56), "varn", "stdn", 2)

            for j in range(4):
                act.wait_ge(s("ch_full"), 6 * NG + j + 1)
                if j == 0:
                    act.wait_ge(s("x1_done"), NT)
                A(qTc[:, 4 * j:4 * j + 4, :], bank[j % 2][:, :].rearrange("p (i t) -> p i t", i=4),
                  ACT.Copy).then_inc(s("ch_free"), 1)
            for u in range(4):
                act.wait_ge(s("sc_full"), u + 1)
                A(score[:, 3, 512 * u:512 * u + 512], bank[(2, 3, 4, 7)[u]][:, :], ACT.Copy).then_inc(s("sc_free"), 1)

            for u in range(T_NORM2 + 2, T_NORM2 + 10):
                t, h = divmod(u - T_NORM2, 2)
                act.wait_ge(s("tr_full"), u + 1)
                A(h2T[:, 4 * h:4 * h + 4, (t - 1) * P:t * P],
                  bank[5 + u % 2][:, :].rearrange("p (k t) -> p k t", k=4), ACT.Copy).then_inc(s("tr_free"), 1)

            def take_queries(h):
                for i in range(2):
                    act.wait_ge(s("fq_full"), h * 2 + i + 1)
                    A(half_q[i], bank[2 + i][:, :], ACT.Copy).then_inc(s("fq_out"), 1)

            def take_scores(h):
                act.wait_ge(s("topk0_done"), h + 1)
                for i in range(2):
                    act.wait_ge(s("fs_full"), h * 2 + i + 1)
                    A(score[:, :, ds(h * 256 + P * i, P)], bank[4 + i][:, :].rearrange("p (t n) -> p t n", t=4),
                      ACT.Copy).then_inc(s("fs_out"), 1)

            def gates(t, h):
                n = t * PH * TOPK + h * TOPK
                act.wait_ge(s("u_used"), n + TOPK + 1)
                A(ex, d_tab[:, ds(n, TOPK)], ACT.Exp, accum_out=esum)
                A(ge, dots, ACT.Gelu_apprx_tanh).then_inc(s("ge_done"), 1)

            def spread(t, h):
                n = t * PH * TOPK + h * TOPK
                act.wait_ge(s("w_done"), t * PH + h + 1)
                for m in range(TOPK):
                    act.wait_ge(s("v_used"), n + (m - 2)) if m >= 4 else act.wait_ge(s("v_used"), n + 1)
                    A(diag[:, m % 4, :], ident, ACT.Copy, scale=w_tab[:, ds(n + m, 1)]).then_inc(s("diag_done"), 1)

            def tile_sum(t):
                act.wait_ge(s("v_used"), t * PH * TOPK + PH * TOPK + 1)
                act.wait_ge(s("out_done"), t * 16 + 16)
                for i in range(2):
                    last = A(pv[:, 512 * i:512 * i + 512], bank[i][:, :], ACT.Copy)
                last.then_inc(s("pv_full"), 1)
                act.wait_ge(s("pv_full"), t + 1)
                ch(A(h2sq, pv, ACT.Square, accum_out=pstat[:, 0:1]))
                A(pstat[:, 1:2], pstat[:, 0:1], ACT.Sqrt, bias=eps[:], scale=1.0 / D).then_inc(s("pv_done"), 1)

            act.wait_ge(s("w_free"), JOB_Q + 4)
            take_queries(0)
            take_scores(0)
            gates(0, 0)
            with act.Fori(0, PH - 1) as h:
                spread(0, h)
                gates(0, h + 1)
                take_queries(h + 1)
                take_scores(h + 1)
            spread(0, PH - 1)
            tile_sum(0)
            with ch.loop(NT - 1, 1) as i:
                with act.Fori(0, PH) as h:
                    gates(i + 1, h)
                    spread(i + 1, h)
                tile_sum(i + 1)

        @block.gpsimd
        def _(pool):
            TT = nc.gpsimd.tensor_tensor
            with pool.Fori(0, NG) as g:
                x8 = [xtok[:, c, :].rearrange("p (r w) -> p r w", r=HG) for c in range(NT)]
                pool.wait_ge(s("tabs_ready"), 1)
                wait_alone(pool, s("y_full"), g * 10 + 1)
                for k, (d, c) in enumerate(STATES):
                    if k < 4:
                        wait_alone(pool, s("tr_free"), g * XB_UNITS + T_XB + TURN.index(c) + 1)
                    TT(xd[:, k, :].rearrange("p (r w) -> p r w", r=HG), x8[c],
                       dtd[:, c, ds(g * HG + 32 * d, HG)].unsqueeze(2).broadcast_to([P, HG, HD]),
                       ALU.mult).then_inc(s("xd_ready"), 1)

                def decay_dt(u):
                    c, hq = divmod(u, 2)
                    wait_alone(pool, s("e_done"), g * 20 + 2 * u + 2)
                    eb = Ee[:, 2 * (u % 2) + 1]
                    TT(eb, eb, dt_[:, c, ds(g * HG + 32 + 4 * hq, 4)].unsqueeze(2).broadcast_to([P, 4, P]),
                       ALU.mult).then_inc(s("eb_ready"), 1)

                def x_skip(c):
                    wait_alone(pool, s("y_free"), g * NT + c + 1)
                    TT(xD.rearrange("p (r w) -> p r w", r=HG), x8[c],
                       dsum[:, ds(g * HG, HG)].unsqueeze(2).broadcast_to([P, HG, HD]),
                       ALU.mult).then_inc(s("xD_ready"), 1)

                for c in range(NT):
                    decay_dt(2 * c)
                    decay_dt(2 * c + 1)
                    x_skip(c)

            nc.gpsimd.memset(eps[:], EPS)

            def rows_of(kind, m, step):
                slots, ins, used, table, idx = ((urow, u_in, "u_used", a["peer_u"], idx_u),
                                                (vrow, v_in, "v_used", a["peer_v"], idx_v))[kind]
                if isinstance(step, int) and step == 0 and m < NSLOT:
                    pass
                else:
                    wait_alone(pool, s(used), step * TOPK + (m - NSLOT + 2))
                nc.gpsimd.indirect_dma_start(
                    slots[m % NSLOT], None, table,
                    bass.IndirectOffsetOnAxis(ap=idx[rows_of.parity][:, m:m + 1], axis=0)).then_inc(ins[m % NSLOT], 16)

            pch = Chain(pool, s("idx_cp"))
            pool.wait_ge(s("h2_ready"), NT)
            pool.wait_ge(s("sc_free"), 4)
            pool.wait_ge(s("topk0_done"), 1)
            pch(nc.gpsimd.tensor_copy(idx_u[0], idx_tab[:, 0:TOPK]))
            rows_of.parity = 0
            for m in range(TOPK):
                rows_of(0, m, 0)

            def both(step, parity, nxt, first_tile=False):
                if first_tile:
                    pool.wait_ge(s("topk0_done"), nxt + 1)
                else:
                    pool.wait_ge(s("topk_done"), nxt - PH + 1)
                pool.wait_ge(s("u_used"), step * TOPK + 1)
                pool.wait_ge(s("v_used"), step * TOPK - TOPK + 1) if not isinstance(step, int) else None
                nc.gpsimd.tensor_copy(idx_u[1 - parity], idx_tab[:, ds(nxt * TOPK, TOPK)])
                pch(nc.gpsimd.tensor_copy(idx_v[parity], idx_tab[:, ds(step * TOPK, TOPK)]))
                for m in range(TOPK):
                    rows_of.parity = 1 - parity
                    rows_of(0, m, nxt)
                    rows_of.parity = parity
                    rows_of(1, m, step)

            pool.wait_ge(s("tr_free"), T_NORM2 + 10)
            both(0, 0, 1, True)
            with pch.loop((PH - 2) // 2, 2) as i:
                both(i * 2 + 1, 1, i * 2 + 2, True)
                both(i * 2 + 2, 0, i * 2 + 3, True)
            with pch.loop((NS - PH) // 2, 2) as i:
                both(i * 2 + (PH - 1), 1, i * 2 + PH)
                both(i * 2 + PH, 0, i * 2 + (PH + 1))
            pool.wait_ge(s("v_used"), (NS - 2) * TOPK + 1)
            pch(nc.gpsimd.tensor_copy(idx_v[1], idx_tab[:, (NS - 1) * TOPK:]))
            rows_of.parity = 1
            for m in range(TOPK):
                rows_of(1, m, NS - 1)

        @block.vector
        def _(dve):
            for nm in ("y_free", "u_used"):
                dve.nop().then_inc(s(nm), 1)
            V = nc.vector
            TT, TS, STT, CP = V.tensor_tensor, V.tensor_scalar, V.scalar_tensor_tensor, V.tensor_copy
            ch = Chain(dve, s("dve"))

            def rstd(cols, n, std_sem, var_sem, turn=1):
                TS(cols, cols, 1.0 / n, EPS, ALU.mult, ALU.add).then_inc(s(var_sem), 1)
                dve.wait_ge(s(std_sem), turn)

            dve.wait_ge(s("consts_in"), 16 * len(CONSTS))
            CP(identb[:], ident)
            V.memset(zerob[:], 0.0)
            CP(maskb[:], shp[:, 4:6, :]).then_inc(s("identb_ready"), 1)
            TT(dsum[:], hrow[:, 2, 0:HEADS], hrow[:, 2, HEADS:], ALU.add)
            dve.wait_ge(s("x_in"), 16 * NT)
            dve.wait_ge(s("pos_in"), 64)
            for t in range(1, NT):
                TT(x0[:, t, :], x0[:, t, :], pos0[:, t - 1, :], ALU.add).then_inc(s("x_ready"), 1)
            dve.wait_ge(s("ssq1"), NT)
            rstd(stat[:, 0:NT], D, "std1", "var1")
            ch(V.reciprocal(stat[:, 0:NT], stat[:, 0:NT]))
            dve.wait_ge(s("x_ready"), NT - 1)
            for t in range(NT):
                TS(x0[:, t, :], x0[:, t, :], stat[:, t:t + 1], None, ALU.mult).then_inc(s("xn_ready"), 1)
            dve.wait_ge(s("ada_done"), 1)
            ch(TT(mod[:], bank[7][:, 0:96].rearrange("p (m c) -> p m c", c=2),
                  adab[:].unsqueeze(2).broadcast_to([P, 48, 2]), ALU.add))
            for i, (m, n) in enumerate(((SC1, 0), (SC2, 2))):
                STT(scl[:, i], mod[:, m * 8:m * 8 + 8, :], 1.0, norms[:, n, :].unsqueeze(2).broadcast_to([P, KT, 2]),
                    ALU.add, ALU.mult)
            for i, (m, n) in enumerate(((GA1, 1), (GA2, 3))):
                last = TT(scl[:, 2 + i], mod[:, m * 8:m * 8 + 8, :], norms[:, n, :].unsqueeze(2).broadcast_to([P, KT, 2]),
                          ALU.mult)
            last.then_inc(s("coef_ready"), 1)
            dve.wait_ge(s("coef_ready"), 1)
            for t in range(NT):
                who = 1 if t else 0
                for h in range(2):
                    u = T_NORM1 + 2 * t + h
                    dve.wait_ge(s("tr_full"), u + 1)
                    for i in range(4):
                        k = 4 * h + i
                        last = TS(hT[:, k, t * P:(t + 1) * P], bank[5 + u % 2][:, i * P:(i + 1) * P],
                                  scl[:, 0, k, who:who + 1], mod[:, SH1 * 8 + k, who:who + 1], ALU.mult, ALU.add)
                    last.then_inc(s("tr_free"), 1)
            dve.wait_ge(s("dt_full"), 1)
            dve.wait_ge(s("nega"), 1)
            v = dtd
            b7 = bank[7][:, 0:320].rearrange("p (t h) -> p t h", t=NT)
            b0 = bank[0][:, 0:320].rearrange("p (t h) -> p t h", t=NT)
            all5 = lambda r: r.unsqueeze(1).broadcast_to([P, NT, 64])
            ch(TT(v, b7, all5(hrow[:, 1, :]), ALU.add))
            STT(tmp, v, -1.0, v, ALU.mult, ALU.min).then_inc(s("v_ready"), 1)
            TS(dt_, v, 0.0, None, ALU.max)
            ch(TS(hrow[:, 0, :], hrow[:, 0, :], -1.0, None, ALU.mult))
            dve.wait_ge(s("softp"), 1)
            ch(TT(dt_, dt_, tmp, ALU.add))
            TT(dA, dt_, all5(hrow[:, 0, :]), ALU.mult).then_inc(s("dA_ready"), 1)
            dve.wait_ge(s("cs_full"), 1)
            ch(TS(ncs, b7, -1.0, None, ALU.mult))
            TT(tmp, b0, ncs, ALU.add).then_inc(s("tmc_ready"), 1)
            dve.wait_ge(s("exps_ready"), 3)
            TT(dtd, dt_, tmp, ALU.mult).then_inc(s("tabs_ready"), 1)
            for lo, hi in ((0, 2), (130, 134), (646, 648)):
                last = V.memset(cin[:, :, lo:hi], 0.0)
            ch(last)
            dve.wait_ge(s("tabs_ready"), 1)

            def convolve(g, i):
                tile = g * 4 + i if i < 4 else g + (16 if i == 4 else 20)
                dve.wait_ge(s("ch_free"), g * 6 + i + 1)
                if i >= 2:
                    dve.wait_ge(s("silu_done"), g * 6 + i - 1)
                o = acc[:, i % 2, 0:644]
                w = lambda k: convw[:, ds(tile, 1), k]
                ch(TS(o, cin[:, i % 2, 0:644], w(0), convb[:, ds(tile, 1)], ALU.mult, ALU.add))
                for k in range(1, TAPS):
                    last = STT(o, cin[:, i % 2, k:k + 644], w(k), o, ALU.mult, ALU.add)
                    if k < TAPS - 1:
                        ch(last)
                last.then_inc(s("conv_done"), 1)

            def scan_group(g, overlap):
                CP(dAg[:, :, 0, :], dA[:, :, ds(g * HG, HG)])
                CP(dAg[:, :, 1, :], dA[:, :, ds(g * HG + 32, HG)]).then_inc(s("dAg_ready"), 1)
                for n, t in enumerate(TURN):
                    dve.wait_ge(s("tr_full"), g * XB_UNITS + T_XB + n + 1)
                    CP(xtok[:, t, :], bank[5 + n % 2][:, :]).then_inc(s("tr_free"), 1)
                convolve(g, 5)
                dve.wait_ge(s("tr_full"), g * XB_UNITS + T_XB + 6)
                CP(Btok[:, 0:4, :], bank[6][:, :].rearrange("p (t c) -> p t c", t=4)).then_inc(s("tr_free"), 1)
                dve.wait_ge(s("tr_full"), g * XB_UNITS + T_XB + 7)
                CP(Btok[:, 4, :], bank[5][:, 0:P]).then_inc(s("tr_free"), 1)
                if overlap:
                    convolve(g + 1, 0)
                r8 = lambda ap: ap.rearrange("p (r w) -> p r w", r=HG)
                per_head = lambda table, c, d: table[:, c, ds(g * HG + 32 * d, HG)].unsqueeze(2).broadcast_to([P, HG, HD])
                dve.wait_ge(s("h0_in"), g * 32 + 32)
                dve.wait_ge(s("tr_free"), g * XB_UNITS + T_XB + 7)
                for k, (d, c) in enumerate(STATES):
                    if c:
                        here, there = H[:, d, c - 1, :], H[:, d, c - 2 if d else c, :]
                        if k in (1, 2, 6, 7):
                            dve.wait_ge(s("st_free"), g * 8 + k)
                        ch(TT(r8(there), r8(here), per_head(ecd, c, d), ALU.mult))
                        dve.wait_ge(s("st_full"), g * 8 + k + 1)
                        TT(there, there, bank[k % 2][:, :], ALU.add).then_inc(s("st_free"), 1)
                    else:
                        dve.wait_ge(s("st_full"), g * 8 + k + 1)
                        CP(cst[:, d, :], bank[k % 2][:, :]).then_inc(s("st_free"), 1)
                    if k == 2 and overlap:
                        convolve(g + 1, 1)

                def chunk_out(c):
                    yc = Y[:, c, ds(g * GC, GC)]
                    dve.wait_ge(s("y_full"), g * 10 + 2 * c + 3)
                    dve.wait_ge(s("xD_ready"), g * NT + c + 1)
                    if c:
                        dve.wait_ge(s("yo_full"), g * 4 + c)
                        TT(r8(yc), r8(bank[4][:, :]), per_head(ecs, c, 0), ALU.mult)
                        ch(TT(r8(yt), r8(bank[7][:, :]), per_head(ecs, c, 1), ALU.mult))
                        ch(TT(yt, yt, xD, ALU.add))
                        ch(TT(yc, yc, yt, ALU.add))
                    else:
                        ch(CP(yc, xD))
                    TT(yc, yc, bank[5 + c % 2][:, :], ALU.add).then_inc(s("y_free"), 1)

                dve.wait_ge(s("cb_done"), g + 1)
                for u in range(2 * NT):
                    c, hq = divmod(u, 2)
                    ef, eb = Ee[:, 2 * (u % 2)], Ee[:, 2 * (u % 2) + 1]
                    dve.wait_ge(s("e_done"), g * 20 + 2 * u + 1)
                    ch(TT(ef, ef, dt_[:, c, ds(g * HG + 4 * hq, 4)].unsqueeze(2).broadcast_to([P, 4, P]), ALU.mult))
                    dve.wait_ge(s("eb_ready"), g * 10 + u + 1)
                    ch(TT(ef, ef, eb, ALU.add))
                    if u >= 2:
                        dve.wait_ge(s("y_full"), g * 10 + u)
                    TT(Mm[:, u % 2], ef, cbT[:, c, :].unsqueeze(1).broadcast_to([P, 4, P]),
                       ALU.mult).then_inc(s("m_done"), 1)
                    if not hq:
                        if c:
                            chunk_out(c - 1)
                    if overlap and u in CONV_AT:
                        convolve(g + 1, CONV_AT[u])
                chunk_out(NT - 1)

            for i in range(5):
                convolve(0, i)
            with ch.loop(NG - 1, 6 * 4 + 6 + 4 * 3 + 1 + 20) as g:
                scan_group(g, True)
            scan_group(NG - 1, False)

            def times_z(j):
                for t in range(NT):
                    dve.wait_ge(s("tm_free"), Q_Z[j] + t + 1)
                    yy = Y[:, t, 512 * j:512 * j + 512]
                    TT(yy, yy, gt[:, (G_Z[j] + t) % 4, :], ALU.mult).then_inc(s("gt_used"), 1)

            dve.wait_ge(s("y_free"), NG * NT + 1)
            times_z(0)
            times_z(1)
            for f in range(KT):
                dve.wait_ge(s("d1_full"), f + 1)
                if f >= 2:
                    dve.wait_ge(s("d2_full"), f - 1)
                CP(Pq[:, f % 2, 1, 0:P], bank[4][:, 0:P])
                CP(Pq[:, f % 2, 1, P:TOK], bank[6][:, :]).then_inc(s("d1_dve"), 1)
                if f:
                    dve.wait_ge(s("d2_full"), f)
                    CP(FT[:, f - 1, 0:P], bank[2 + (f - 1) % 2][:, 0:P])
                    CP(FT[:, f - 1, P:TOK], bank[(f - 1) % 2][:, :]).then_inc(s("d2_free"), 1)
            dve.wait_ge(s("d2_full"), KT)
            CP(FT[:, KT - 1, 0:P], bank[2 + (KT - 1) % 2][:, 0:P])
            CP(FT[:, KT - 1, P:TOK], bank[(KT - 1) % 2][:, :]).then_inc(s("d2_free"), 1)
            for n in range(10):
                j, t = divmod(n, NT)
                dve.wait_ge(s("tm_free"), Q_GA + n + 1)
                ao = a_out[:, t, 512 * j:512 * j + 512]
                TT(ao, ao, gt[:, (G_GA + n) % 4, :], ALU.mult).then_inc(s("gt_used"), 1)

            def turned_y(j):
                for t in range(NT):
                    u = T_Y + 5 * j + t
                    dve.wait_ge(s("tr_full"), u + 1)
                    for i in range(4):
                        last = TS(yT[:, 4 * j + i, t * P:(t + 1) * P], bank[5 + u % 2][:, i * P:(i + 1) * P],
                                  ssdn[:, 4 * j + i:4 * j + i + 1], None, ALU.mult)
                    last.then_inc(s("tr_free"), 1)

            turned_y(0)
            times_z(2)
            turned_y(1)
            times_z(3)
            turned_y(2)
            turned_y(3)
            dve.wait_ge(s("ssqy"), 20)
            ch(V.tensor_reduce(stat[:, 30:35], stat[:, 10:30].rearrange("p (t j) -> p t j", j=4), AX.X, ALU.add))
            rstd(stat[:, 30:35], DI, "stdy", "vary")
            V.reciprocal(stat[:, 30:35], stat[:, 30:35]).then_inc(s("rstdy"), 1)
            for u in range(16):
                v_, h = divmod(u, 2)
                dve.wait_ge(s("row_full"), u + 1)
                CP(rows[:, v_, 512 * h:512 * h + 512], bank[6 + h][:, :]).then_inc(s("row_free"), 1)
            for n in range(20):
                j, t = divmod(n, NT)
                dve.wait_ge(s("tm_free"), Q_SO + n + 1)
                o = slice(256 * j, 256 * j + 256)
                g_ = gt[:, n % 4, 0:256]
                ch(TT(g_, g_, sB[:, t, o], ALU.mult))
                TT(a_out[:, t, o], a_out[:, t, o], g_, ALU.add).then_inc(s("mg_done"), 1)
            for u in range(10):
                t, h = divmod(u, 2)
                dve.wait_ge(s("tr_full"), T_MERGE + u + 1)
                CP(mT[:, 4 * h:4 * h + 4, t * P:(t + 1) * P],
                   bank[5 + (T_MERGE + u) % 2][:, :].rearrange("p (k t) -> p k t", k=4)).then_inc(s("tr_free"), 1)
            def norm_mix(first, end, turn):
                ssq = stat[:, 36:46].rearrange("p (t j) -> p t j", j=2)
                cols = stat[:, 46 + first:46 + end]
                ch(TT(cols, ssq[:, first:end, 0], ssq[:, first:end, 1], ALU.add))
                rstd(cols, D, "stdm", "varm", turn)
                ch(V.reciprocal(cols, cols))
                for t in range(first, end):
                    ch(STT(mix[:, t, :], mix[:, t, :], stat[:, 46 + t:47 + t], rows[:, 1 if t else 0, :],
                           ALU.mult, ALU.mult))
                    TT(x1[:, t, :], x1[:, t, :], mix[:, t, :], ALU.add).then_inc(s("x1_done"), 1)

            def norm_x1(first, end, turn):
                dve.wait_ge(s("ssqn"), end)
                rstd(stat[:, 51 + first:51 + end], D, "stdn", "varn", turn)
                ch(V.reciprocal(stat[:, 51 + first:51 + end], stat[:, 51 + first:51 + end]))

            dve.wait_ge(s("x1_in"), 32)
            dve.wait_ge(s("row_free"), 16)
            dve.wait_ge(s("ssqm"), NT + 1)
            dve.wait_ge(s("tm_free"), Q_WO + NT + 1)
            norm_mix(0, 1, 1)
            norm_x1(0, 1, 1)
            ch(STT(mix[:, 0, :], x1[:, 0, :], stat[:, 51:52], rows[:, 2, :], ALU.mult, ALU.mult))
            TT(h2c, mix[:, 0, :], rows[:, 4, :], ALU.add).then_inc(s("h2_ready"), 1)
            for t in range(1, NT):
                last = TT(x1[:, t, :], x1[:, t, :], pos1[:, t - 1, :], ALU.add)
            ch(last)
            for h in range(2):
                dve.wait_ge(s("tr_full"), T_NORM2 + h + 1)
                CP(h2Tc[:, 4 * h:4 * h + 4, :],
                   bank[5 + (T_NORM2 + h) % 2][:, :].rearrange("p (k t) -> p k t", k=4)).then_inc(s("tr_free"), 1)
            dve.wait_ge(s("ssqm"), 10)
            dve.wait_ge(s("tm_free"), Q_WO + 10)
            norm_mix(1, NT, 2)
            norm_x1(1, NT, 2)
            for t in range(1, NT):
                ch(STT(h2[:, t, :], x1[:, t, :], stat[:, 51 + t:52 + t], rows[:, 3, :], ALU.mult, ALU.mult))
                TT(h2[:, t, :], h2[:, t, :], rows[:, 5, :], ALU.add).then_inc(s("h2_ready"), 1)

            def best16(vals, idx, src, src2):
                ch(V.max(vals[:, 0:8], src), wait_alone)
                V.max_index(idx[:, 0:8], vals[:, 0:8], src)
                ch(V.match_replace(src2, vals[:, 0:8], src, LOWEST), wait_alone)
                ch(V.max(vals[:, 8:16], src2), wait_alone)
                ch(V.max_index(idx[:, 8:16], vals[:, 8:16], src2), wait_alone)

            def top(slot, n, h, done="topk_done"):
                ch(CP(sw, score[:, slot:slot + 1, ds(h * 256, 256)].rearrange("p t (h n) -> p (t h) n", h=2)
                      if isinstance(slot, int) else score[:, ds(slot, 1), ds(h * 256, 256)].rearrange("p t (h n) -> p (t h) n", h=2)), wait_alone)
                for half in range(2):
                    best16(v16[:, 16 * half:16 * half + 16], i16[:, 16 * half:16 * half + 16],
                           sw[:, half, :], sw2[:, half, :])
                CP(i16f, i16)
                ch(TT(cand.rearrange("p (a b) -> p a b", a=TOPK),
                      v16[:, 0:16].unsqueeze(2).broadcast_to([P, 16, 16]),
                      v16[:, 16:32].unsqueeze(1).broadcast_to([P, 16, 16]), ALU.add), wait_alone)
                best16(tv, tp, cand, cand2)
                TS(d_tab[:, ds(n, TOPK)], tv, tv[:, 0:1], None, ALU.subtract)
                TS(tij[:, 0:16], tp, 4, None, ALU.logical_shift_right)
                ch(TS(tij[:, 16:32], tp, 15, None, ALU.bitwise_and))
                ch(CP(tijf, tij))
                ch(TT(eq, iota16.unsqueeze(1).broadcast_to([P, 32, 16]), tijf.unsqueeze(2).broadcast_to([P, 32, 16]),
                      ALU.is_equal))
                e4 = eq.rearrange("p (h k) n -> p h k n", h=2)
                ch(TT(e4, e4, i16f.rearrange("p (h n) -> p h n", h=2).unsqueeze(2).broadcast_to([P, 2, 16, 16]),
                      ALU.mult))
                ch(V.tensor_reduce(pick, eq, AX.X, ALU.add))
                STT(idx_tab[:, ds(n, TOPK)], pick[:, 0:16], float(NKEY), pick[:, 16:32],
                    ALU.mult, ALU.add).then_inc(s(done), 1)

            TOP = 1 + 8 + 1 + 4 + 1 + 1 + 1 + 1 + 1

            def step(t, h, tops):
                n = t * PH + h
                for m in range(TOPK):
                    dve.wait_ge(u_in[m % NSLOT], n * 32 + 16 * (m // NSLOT + 1))
                    V.tensor_tensor_reduce(out=urow[m % NSLOT], in0=urow[m % NSLOT], in1=h2c, scale=1.0,
                                           scalar=0.0, op0=ALU.mult, op1=ALU.add,
                                           accum_out=dots[:, m:m + 1]).then_inc(s("u_used"), 1)
                    if m in tops:
                        tops[m]()
                dve.wait_ge(s("ge_done"), n + 1)
                ch(V.reciprocal(erec, esum))
                STT(w_tab[:, ds(n * TOPK, TOPK)], ge, erec, ex, ALU.mult, ALU.mult).then_inc(s("w_done"), 1)

            def top_context(h):
                top(3, h * TOPK, h, "topk0_done")

            def top_first_latents(h):
                dve.wait_ge(s("fs_out"), h * 2 + 3)
                top(0, (h + PH) * TOPK, h)

            def after_half(t, h):
                return {8: lambda: top(t, ((t + 1) * PH + h) * TOPK, h)}

            def tile_of(t):
                ch(CP(h2c, x1[:, ds(t, 1), :].rearrange("p t c -> p (t c)")))
                ch(STT(h2c, h2c, stat[:, ds(t + 51, 1)], rows[:, 3, :], ALU.mult, ALU.mult))
                ch(TT(h2c, h2c, rows[:, 5, :], ALU.add))

            def result(t, who):
                dve.wait_ge(s("pv_done"), t + 2)
                ch(V.reciprocal(pstat[:, 2:3], pstat[:, 1:2]))
                ch(STT(pv, pv, pstat[:, 2:3], rows[:, 6 + who, :], ALU.mult, ALU.mult))
                TT(pv, pv, x1[:, ds(t, 1), :].rearrange("p t c -> p (t c)"), ALU.add).then_inc(s("out_ready"), 1)

            dve.wait_ge(s("h2_ready"), NT)
            dve.wait_ge(s("ssqn"), NT)
            dve.wait_ge(s("sc_free"), 4)
            top_context(0)
            step(0, 0, {2: lambda: top_context(1), 11: lambda: top_context(2)})
            with ch.loop(PH - 3, 2 * TOP + 1) as h:
                step(0, h + 1, {4: lambda: top_context(h + 3), 11: lambda: top_first_latents(h)})
            with ch.loop(2, TOP + 1) as h:
                step(0, h + (PH - 2), {8: lambda: top_first_latents(h + (PH - 3))})
            top_first_latents(PH - 1)
            tile_of(1)
            step(1, 0, after_half(1, 0))
            result(0, 0)
            with ch.loop(PH - 1, TOP + 1) as h:
                step(1, h + 1, after_half(1, h + 1))
            with ch.loop(2, 3 + (TOP + 1) + 2 + (PH - 1) * (TOP + 1)) as i:
                tile_of(i + 2)
                step(i + 2, 0, after_half(i + 2, 0))
                result(i + 1, 1)
                with ch.loop(PH - 1, TOP + 1) as h:
                    step(i + 2, h + 1, after_half(i + 2, h + 1))
            tile_of(NT - 1)
            step(NT - 1, 0, {})
            result(NT - 2, 1)
            with ch.loop(PH - 1, 1) as h:
                step(NT - 1, h + 1, {})
            result(NT - 1, 1)


def shape_constants():
    f = np.float32
    i = np.arange(P)
    shp = np.zeros((P, 7, P), f)
    shp[:, 0] = np.eye(P)
    shp[:, 1] = i[:, None] <= i[None, :]
    shp[:, 2] = i[:, None] >= i[None, :]
    shp[:, 3] = 1
    shp[:, 6] = i[None, :]
    shp[:, 4] = np.where(i[:, None] <= i[None, :], 0, NEG)
    shp[:, 5] = np.where(i[:, None] >= i[None, :], 0, NEG)
    ang = 2 * np.pi * ((i[:, None] * i[None, :]) % P) / P
    chm = np.stack([np.cos(ang), np.sin(ang), -np.sin(ang)], 1) / np.sqrt(P)
    l = np.arange(LAT)
    angl = 2 * np.pi * ((l[:, None] * l[None, :]) % LAT) / LAT
    quarter = D // 4
    omega = (1.0 / (f(10000.0) ** (np.arange(quarter, dtype=f) / f(quarter)))).astype(f)
    ar = (l // 64).astype(f)[:, None] * omega
    ac = (l % 64).astype(f)[:, None] * omega
    pos = np.concatenate([np.sin(ar), np.cos(ar), np.sin(ac), np.cos(ac)], -1)
    return {"shp": shp, "chm": chm.astype(f), "posc": (np.cos(angl) / np.sqrt(LAT)).astype(f),
            "poss": (np.sin(angl) / np.sqrt(LAT)).astype(f), "pos": pos.astype(f)}


def layout(i):
    cols = lambda v, n: np.ascontiguousarray(np.asarray(v).reshape(n, P).T)
    i = {k: np.asarray(v) for k, v in i.items()}
    out = dict(shape_constants())
    out["x"] = np.concatenate([i["x_prompt"][0], i["x_sample"][0]], 0)
    out["cond"] = np.stack([cols(i["c_ctx"], KT), cols(i["c"][0], KT)], -1)
    out["ada_b"] = cols(i["b_ada"][0], 48)
    out["norms"] = np.stack([cols(i[n][0], KT) for n in
                             ("norm_mix_pre", "norm_mix_post", "norm_ffn_pre", "norm_ffn_post")], 1)
    out["ssd_norm"] = cols(i["ssd_norm"][0], 16)
    out["conv_w"] = i["w_conv"][0].reshape(TAPS, 24, P).transpose(2, 1, 0)
    out["conv_b"] = cols(i["b_conv"][0], 24)
    for n in ("a_log", "dt_bias", "d_skip"):
        out[n] = i[n].reshape(2 * HEADS)
    out["state"] = i["state_ssd"][0, 0].reshape(2, DI, P).transpose(0, 2, 1)
    for n in ("w_ada", "w_in", "w_fourier", "w_ssd_out", "w_out"):
        out[n] = i[n][0]
    out["w_query"] = i["peer_query"][0]
    out["keys"] = i["peer_sub_keys"][0].reshape(16, P, P).transpose(2, 0, 1)
    out["peer_u"], out["peer_v"] = i["peer_u"][0], i["peer_v"][0]
    return {k: np.ascontiguousarray(v) for k, v in out.items()}


def kernel(**inputs):
    import concourse.bacc as bacc
    from concourse.bass_utils import run_bass_kernel_spmd

    arrays = layout(inputs)
    nc = bacc.Bacc("TRN2", target_bir_lowering=False, num_devices=1)
    args = {k: nc.dram_tensor(f"in_{k}", v.shape, mybir.dt.from_np(v.dtype), kind="ExternalInput").ap()
            for k, v in arrays.items()}
    outs = (nc.dram_tensor("y_out", (TOK, D), F32, kind="ExternalOutput").ap(),
            nc.dram_tensor("state_out", (2, P, DI), F32, kind="ExternalOutput").ap())
    layer_kernel(nc, args, outs)
    r = run_bass_kernel_spmd(nc, [{f"in_{k}": v for k, v in arrays.items()}], core_ids=[0]).results[0]
    y, st = np.asarray(r["y_out"]), np.asarray(r["state_out"])
    return (y[0:P].reshape(1, P, D), y[P:].reshape(1, LAT, D),
            np.ascontiguousarray(st.transpose(0, 2, 1)).reshape(1, 1, 2, HEADS, HD, P))
```
